# Optimizing a Trainium2 kernel written in Bass

```python
import math
import jax, jax.numpy as jnp
from jax import lax
import numpy as np

D_MODEL = 1024
BATCH = 1
SEQ = 256
DEPTH = 2

GRID_W = 64
CTX_LEN = 256
N_MIXERS = 4
Q_BLOCK = 128
CHUNK = 64
ROPE_THETA = 10000.0
NORM_EPS = 1e-6
N_MOD = 9
D_FF = 2816

DIFF_HEADS = 8
DIFF_HEAD_DIM = D_MODEL // DIFF_HEADS // 2

RET_HEADS = 4
RET_KEY_DIM = D_MODEL // RET_HEADS
RET_VAL_DIM = 2 * D_MODEL // RET_HEADS

HGRN_EXPAND = 128
HGRN_HEADS = D_MODEL // HGRN_EXPAND
HGRN_KEY_DIM = HGRN_EXPAND
HGRN_VAL_DIM = D_MODEL // HGRN_HEADS

GQA_HEAD_DIM = 128
GQA_Q_HEADS = D_MODEL // GQA_HEAD_DIM
GQA_KV_HEADS = 2
GQA_GROUP = GQA_Q_HEADS // GQA_KV_HEADS

kernel_name = "hybrid_interleaved_diffusion_trunk"

def _rms(x, eps=NORM_EPS):
    xf = x.astype(jnp.float32)
    return (xf * lax.rsqrt(jnp.mean(xf * xf, axis=-1, keepdims=True) + eps)).astype(x.dtype)

def _modulate(h, shift, scale):
    return _rms(h) * (1.0 + scale) + shift

def _split_mod(v):
    v = v.reshape(*v.shape[:-1], N_MOD, 1, D_MODEL)
    return [v[..., k, :, :] for k in range(N_MOD)]

def _swiglu(h, w13, w2):
    a, b = jnp.split(h @ w13, 2, axis=-1)
    return (jax.nn.silu(a) * b) @ w2

def _axial_rope_tables(n_tokens, head_dim):
    rows = n_tokens // GRID_W
    row = jnp.repeat(jnp.arange(rows, dtype=jnp.float32), GRID_W)
    col = jnp.tile(jnp.arange(GRID_W, dtype=jnp.float32), rows)
    nq = head_dim // 4
    inv = ROPE_THETA ** (-jnp.arange(nq, dtype=jnp.float32) * 2.0 / (head_dim // 2))
    ang = jnp.stack([row[:, None] * inv, col[:, None] * inv], axis=1)
    return jnp.cos(ang), jnp.sin(ang)

def _apply_rope(x, cos, sin):
    shp = x.shape
    xr = x.reshape(*shp[:-1], 2, 2, shp[-1] // 4)
    x1, x2 = xr[..., 0, :], xr[..., 1, :]
    extra = len(shp) - 3
    c = cos.reshape(cos.shape[0], *([1] * extra), 2, -1)
    s = sin.reshape(sin.shape[0], *([1] * extra), 2, -1)
    out = jnp.stack([x1 * c - x2 * s, x2 * c + x1 * s], axis=-2)
    return out.reshape(shp).astype(x.dtype)

def _to_blocks(t):
    B, T = t.shape[:2]
    return jnp.moveaxis(t.reshape(B, T // Q_BLOCK, Q_BLOCK, *t.shape[2:]), 1, 0)

def _from_blocks(t):
    nb, B, qb = t.shape[:3]
    return jnp.moveaxis(t, 0, 1).reshape(B, nb * qb, *t.shape[3:])

def _chunk_gla(q, k, v, log_a, s0):
    B, T, H, _ = q.shape
    n = T // CHUNK

    def chunks(t):
        return jnp.moveaxis(t.astype(jnp.float32).reshape(B, n, CHUNK, *t.shape[2:]), 1, 0)

    causal = jnp.tril(jnp.ones((CHUNK, CHUNK), dtype=bool))

    def step(state, inp):
        qc, kc, vc, lc = inp
        b = jnp.cumsum(lc, axis=1)
        b_last = b[:, -1]
        q_dec = qc * jnp.exp(b)
        k_dec = kc * jnp.exp(-b)
        att = jnp.where(causal, jnp.einsum('bchk,bshk->bhcs', q_dec, k_dec), 0.0)
        o = (jnp.einsum('bchk,bhkv->bchv', q_dec, state)
             + jnp.einsum('bhcs,bshv->bchv', att, vc))
        state = (jnp.exp(b_last)[..., None] * state
                 + jnp.einsum('bshk,bshv->bhkv', kc * jnp.exp(b_last[:, None] - b), vc))
        return state, o

    state, o = lax.scan(step, s0, (chunks(q), chunks(k), chunks(v), chunks(log_a)))
    o = jnp.moveaxis(o, 0, 1).reshape(B, T, H, v.shape[-1]).astype(v.dtype)
    return o, state

def _bidir_scan(q_c, v_c, dirs_c, q_l, v_l, dirs_l):
    B, _, H, dk = q_c.shape
    s0 = jnp.zeros((B, H, dk, v_c.shape[-1]), jnp.float32)
    rev = lambda t: t[:, ::-1]
    (kcf, lcf), (kcb, lcb) = dirs_c
    (klf, llf), (klb, llb) = dirs_l
    oc_f, s_f = _chunk_gla(q_c, kcf, v_c, lcf, s0)
    oc_b, s_b = _chunk_gla(rev(q_c), rev(kcb), rev(v_c), rev(lcb), s0)
    ol_f, _ = _chunk_gla(q_l, klf, v_l, llf, s_f)
    ol_b, _ = _chunk_gla(rev(q_l), rev(klb), rev(v_l), rev(llb), s_b)
    return oc_f + rev(oc_b), ol_f + rev(ol_b)

def _diff_attention(h_lat, h_ctx, w_in, w_out, lam, subln_g, layer_idx, need_ctx):
    H, d = DIFF_HEADS, DIFF_HEAD_DIM
    lam_init = 0.8 - 0.6 * math.exp(-0.3 * layer_idx)
    l32 = lam.astype(jnp.float32)
    lam_full = jnp.exp(jnp.sum(l32[0] * l32[1])) - jnp.exp(jnp.sum(l32[2] * l32[3])) + lam_init
    cos, sin = _axial_rope_tables(h_lat.shape[1], d)

    def project(h, rotate):
        B, T, _ = h.shape
        q, k, v = jnp.split(h @ w_in, 3, axis=-1)
        q = q.reshape(B, T, H, 2, d) * (d ** -0.5)
        k = k.reshape(B, T, H, 2, d)
        if rotate:
            q, k = _apply_rope(q, cos, sin), _apply_rope(k, cos, sin)
        return q, k, v.reshape(B, T, H, 2 * d)

    def attend(q, k, v):
        s = jnp.einsum('bqhjd,bshjd->bhjqs', q, k).astype(jnp.float32)
        p = jax.nn.softmax(s, axis=-1)
        a = (p[:, :, 0] - lam_full * p[:, :, 1]).astype(v.dtype)
        o = jnp.einsum('bhqs,bshe->bqhe', a, v)
        return _rms(o) * subln_g * (1.0 - lam_init)

    def out_proj(o):
        B, T = o.shape[:2]
        return o.reshape(B, T, D_MODEL) @ w_out

    ql, kl, vl = project(h_lat, True)
    qc, kc, vc = project(h_ctx, False)
    k_all = jnp.concatenate([kc, kl], axis=1)
    v_all = jnp.concatenate([vc, vl], axis=1)
    o_lat = _from_blocks(lax.map(lambda qb: attend(qb, k_all, v_all), _to_blocks(ql)))
    o_ctx = out_proj(attend(qc, kc, vc)) if need_ctx else None
    return out_proj(o_lat), o_ctx

def _retention(h_lat, h_ctx, w_in, w_out, decay_exp, need_ctx):
    H, dk, dv = RET_HEADS, RET_KEY_DIM, RET_VAL_DIM
    D = D_MODEL
    log_gamma = jnp.log1p(-jnp.exp2(-decay_exp.astype(jnp.float32)))
    cos, sin = _axial_rope_tables(h_lat.shape[1], dk)

    def project(h, rotate):
        B, T, _ = h.shape
        q, k, v, g = jnp.split(h @ w_in, [D, 2 * D, 4 * D], axis=-1)
        q = q.reshape(B, T, H, dk)
        k = k.reshape(B, T, H, dk) * (dk ** -0.5)
        if rotate:
            q, k = _apply_rope(q, cos, sin), _apply_rope(k, cos, sin)
        dirs = tuple((k, jnp.broadcast_to(log_gamma[r][None, None, :, None], (B, T, H, 1)))
                     for r in range(2))
        return q, v.reshape(B, T, H, dv), dirs, g

    ql, vl, dl, gl = project(h_lat, True)
    qc, vc, dc, gc = project(h_ctx, False)
    o_ctx, o_lat = _bidir_scan(qc, vc, dc, ql, vl, dl)

    def readout(o, g):
        B, T = o.shape[:2]
        return (jax.nn.silu(g) * _rms(o).reshape(B, T, 2 * D)) @ w_out

    return readout(o_lat, gl), (readout(o_ctx, gc) if need_ctx else None)

def _hgrn2(h_lat, h_ctx, w_in, w_out, lb_logits, norm_g, layer_idx, need_ctx):
    H, dk, dv = HGRN_HEADS, HGRN_KEY_DIM, HGRN_VAL_DIM
    p = jax.nn.softmax(lb_logits.astype(jnp.float32), axis=0)
    lb = (jnp.cumsum(p, axis=0) - p[0])[layer_idx].reshape(H, dk)

    def project(h):
        B, T, _ = h.shape
        q, i, g, zf, zb = jnp.split(h @ w_in, 5, axis=-1)
        q = jax.nn.silu(q).reshape(B, T, H, dk)

        def gate(z):
            f = lb + (1.0 - lb) * jax.nn.sigmoid(z.astype(jnp.float32).reshape(B, T, H, dk))
            return (1.0 - f, jnp.log(f))

        return q, i.reshape(B, T, H, dv), (gate(zf), gate(zb)), g

    ql, il, dl, gl = project(h_lat)
    qc, ic, dc, gc = project(h_ctx)
    o_ctx, o_lat = _bidir_scan(qc, ic, dc, ql, il, dl)

    def readout(o, g):
        B, T = o.shape[:2]
        return ((_rms(o) * norm_g).reshape(B, T, D_MODEL) * jax.nn.silu(g)) @ w_out

    return readout(o_lat, gl), (readout(o_ctx, gc) if need_ctx else None)

def _gqa(h_lat, h_ctx, w_in, w_out, q_g, k_g, need_ctx):
    Hk, G, d = GQA_KV_HEADS, GQA_GROUP, GQA_HEAD_DIM
    cos, sin = _axial_rope_tables(h_lat.shape[1], d)

    def project(h, rotate):
        B, T, _ = h.shape
        q, k, v = jnp.split(h @ w_in, [D_MODEL, D_MODEL + Hk * d], axis=-1)
        q = _rms(q.reshape(B, T, Hk, G, d)) * q_g * (d ** -0.5)
        k = _rms(k.reshape(B, T, Hk, d)) * k_g
        if rotate:
            q, k = _apply_rope(q, cos, sin), _apply_rope(k, cos, sin)
        return q, k, v.reshape(B, T, Hk, d)

    def attend(q, k, v):
        s = jnp.einsum('bqhgd,bshd->bhgqs', q, k).astype(jnp.float32)
        pr = jax.nn.softmax(s, axis=-1).astype(v.dtype)
        return jnp.einsum('bhgqs,bshd->bqhgd', pr, v)

    def out_proj(o):
        B, T = o.shape[:2]
        return o.reshape(B, T, D_MODEL) @ w_out

    ql, kl, vl = project(h_lat, True)
    qc, kc, vc = project(h_ctx, False)
    k_all = jnp.concatenate([kc, kl], axis=1)
    v_all = jnp.concatenate([vc, vl], axis=1)
    o_lat = _from_blocks(lax.map(lambda qb: attend(qb, k_all, v_all), _to_blocks(ql)))
    o_ctx = out_proj(attend(qc, kc, vc)) if need_ctx else None
    return out_proj(o_lat), o_ctx

def setup_inputs(seed: int = 0) -> dict:
    key = jax.random.key(seed)
    ks = jax.random.split(key, 32)
    D, F = D_MODEL, D_FF
    cnt = [len(range(m, DEPTH, N_MIXERS)) for m in range(N_MIXERS)]
    nA, nB, nC, nD = cnt

    def nrm(i, shape, scale):
        return jax.random.normal(ks[i], shape, jnp.float32) * scale

    gqa_in = D + 2 * GQA_KV_HEADS * GQA_HEAD_DIM
    return {
        "x": nrm(0, (BATCH, SEQ, D), 1.0),
        "c": nrm(1, (BATCH, D), 1.0),
        "ctx": nrm(2, (BATCH, CTX_LEN, D), 1.0),
        "c_ctx": nrm(3, (D,), 1.0),
        "mod_w": nrm(4, (DEPTH, D, N_MOD * D), 0.5 * D ** -0.5),
        "mod_b": nrm(5, (DEPTH, N_MOD * D), 0.02),
        "ffn1_w13": nrm(6, (DEPTH, D, 2 * F), D ** -0.5),
        "ffn1_w2": nrm(7, (DEPTH, F, D), F ** -0.5),
        "ffn2_w13": nrm(8, (DEPTH, D, 2 * F), D ** -0.5),
        "ffn2_w2": nrm(9, (DEPTH, F, D), F ** -0.5),
        "diff_w_in": nrm(10, (nA, D, 3 * D), D ** -0.5),
        "diff_w_out": nrm(11, (nA, D, D), D ** -0.5),
        "diff_lambda": nrm(12, (nA, 4, DIFF_HEAD_DIM), 0.1),
        "diff_subln_g": 1.0 + nrm(13, (nA, 2 * DIFF_HEAD_DIM), 0.02),
        "ret_w_in": nrm(14, (nB, D, 6 * D), D ** -0.5),
        "ret_w_out": nrm(15, (nB, 2 * D, D), (2 * D) ** -0.5),
        "ret_decay_exp": 5.0 + jnp.arange(RET_HEADS, dtype=jnp.float32) + nrm(16, (nB, 2, RET_HEADS), 0.1),
        "hgrn_w_in": nrm(17, (nC, D, 5 * D), D ** -0.5),
        "hgrn_w_out": nrm(18, (nC, D, D), D ** -0.5),
        "hgrn_lb_logits": nrm(19, (DEPTH, D), 0.1),
        "hgrn_norm_g": 1.0 + nrm(20, (nC, HGRN_VAL_DIM), 0.02),
        "gqa_w_in": nrm(21, (nD, D, gqa_in), D ** -0.5),
        "gqa_w_out": nrm(22, (nD, D, D), D ** -0.5),
        "gqa_q_norm_g": 1.0 + nrm(23, (nD, GQA_HEAD_DIM), 0.02),
        "gqa_k_norm_g": 1.0 + nrm(24, (nD, GQA_HEAD_DIM), 0.02),
        "final_norm_g": 1.0 + nrm(25, (D,), 0.02),
    }

def reference(x, c, ctx, c_ctx, mod_w, mod_b, ffn1_w13, ffn1_w2, ffn2_w13, ffn2_w2,
              diff_w_in, diff_w_out, diff_lambda, diff_subln_g,
              ret_w_in, ret_w_out, ret_decay_exp,
              hgrn_w_in, hgrn_w_out, hgrn_lb_logits, hgrn_norm_g,
              gqa_w_in, gqa_w_out, gqa_q_norm_g, gqa_k_norm_g,
              final_norm_g):
    cond_lat = jax.nn.silu(c)
    cond_ctx = jax.nn.silu(c_ctx)
    h, hc = x, ctx
    for i in range(DEPTH):
        kind, j = i % N_MIXERS, i // N_MIXERS
        need_ctx = i < DEPTH - 1
        ml = _split_mod(cond_lat @ mod_w[i] + mod_b[i])
        mc = _split_mod(cond_ctx @ mod_w[i] + mod_b[i])

        h = h + 0.5 * ml[2] * _swiglu(_modulate(h, ml[0], ml[1]), ffn1_w13[i], ffn1_w2[i])
        hc = hc + 0.5 * mc[2] * _swiglu(_modulate(hc, mc[0], mc[1]), ffn1_w13[i], ffn1_w2[i])

        a_l = _modulate(h, ml[3], ml[4])
        a_c = _modulate(hc, mc[3], mc[4])
        if kind == 0:
            o_l, o_c = _diff_attention(a_l, a_c, diff_w_in[j], diff_w_out[j], diff_lambda[j],
                                       diff_subln_g[j], i, need_ctx)
        elif kind == 1:
            o_l, o_c = _retention(a_l, a_c, ret_w_in[j], ret_w_out[j], ret_decay_exp[j], need_ctx)
        elif kind == 2:
            o_l, o_c = _hgrn2(a_l, a_c, hgrn_w_in[j], hgrn_w_out[j], hgrn_lb_logits,
                              hgrn_norm_g[j], i, need_ctx)
        else:
            o_l, o_c = _gqa(a_l, a_c, gqa_w_in[j], gqa_w_out[j], gqa_q_norm_g[j],
                            gqa_k_norm_g[j], need_ctx)
        h = h + ml[5] * o_l

        h = h + 0.5 * ml[8] * _swiglu(_modulate(h, ml[6], ml[7]), ffn2_w13[i], ffn2_w2[i])
        if need_ctx:
            hc = hc + mc[5] * o_c
            hc = hc + 0.5 * mc[8] * _swiglu(_modulate(hc, mc[6], mc[7]), ffn2_w13[i], ffn2_w2[i])
    return _rms(h) * final_norm_g


_drawn_inputs = setup_inputs


def setup_inputs(seed=0):
    import zlib

    import numpy as np

    out = dict(_drawn_inputs(seed))
    spreads = {}
    factors = {'diff_lambda': 3.766, 'diff_subln_g': 8.0, 'final_norm_g': 2.808}
    for name, (base, spread) in spreads.items():
        noise = np.random.default_rng([zlib.crc32(name.encode()), seed]).standard_normal(out[name].shape)
        drawn = base * np.exp(spread * noise) if base else spread * noise
        out[name] = __import__('jax').numpy.asarray(drawn.astype(out[name].dtype))
    for name, factor in factors.items():
        out[name] = (out[name] * factor).astype(out[name].dtype)
    return out
```

```python
from contextlib import ExitStack

import concourse.bass as bass
from concourse import mybir
import numpy as np

ALU = mybir.AluOpType
ACT = mybir.ActivationFunctionType
AX = mybir.AxisListType
F32 = mybir.dt.float32
F32R = mybir.dt.float32r

P = 128
D = 1024
DT = D // P
LAT = 256
CTX = 256
TOK = LAT + CTX
TT = TOK // P
F = 2816
FT = F // P
DEPTH = 2
N_MOD = 9
MODT = N_MOD * DT
EPS = 1e-6
GRID_W = 64
THETA = 10000.0
CW = 256
W2_ROWS = (6, 5, 6, 5)
UP_PAIRS = F // CW

DH = 8
DD = 64
LAM_INIT = 0.8 - 0.6 * float(np.exp(np.float64(0.0)))
RH = 4
RK = 256
RV = 512

EARLY_MODS = 28
EARLY_NEED = 16
STAGE = 8
MODS_PER_PAIR = 4
G_STEPS = 18


def rope_rows(n_tokens, head_dim):
    nq = head_dim // 4
    t = np.arange(n_tokens, dtype=np.float32)
    row, col = np.floor(t / GRID_W).astype(np.float32), np.mod(t, GRID_W).astype(np.float32)
    inv = np.float32(THETA) ** (-np.arange(nq, dtype=np.float32) * np.float32(2.0) / np.float32(head_dim // 2))
    cos, sin = [], []
    for pos in (row, col):
        ang = (inv[:, None] * pos[None, :]).astype(np.float32)
        cos += [np.cos(ang), np.cos(ang)]
        sin += [-np.sin(ang), np.sin(ang)]
    return np.concatenate(cos).astype(np.float32), np.concatenate(sin).astype(np.float32)


def swap_rows(half):
    m = np.zeros((P, P), np.float32)
    m[np.arange(P), np.arange(P) ^ half] = 1.0
    return m


def shape_constants():
    dcos, dsin = rope_rows(LAT, DD)
    rcos, rsin = rope_rows(LAT, RK)
    gap = np.arange(LAT, dtype=np.float32)[None, :] - np.arange(P, dtype=np.float32)[:, None]
    parts = [np.eye(P, dtype=np.float32), swap_rows(DD // 4), swap_rows(RK // 4), gap,
             np.tile(dcos, (2, 1)), np.tile(dsin, (2, 1)), rcos[:P], rcos[P:], rsin[:P], rsin[P:]]
    return np.ascontiguousarray(np.concatenate(parts, axis=1))


C_KEEP = 3 * P + LAT
C_DROPE = C_KEEP
C_RROPE = C_DROPE + 2 * LAT
C_ALL = C_RROPE + 4 * LAT


def plan():
    phases = []
    at = dict(q=0, s=0, n=0, x=0, u=0, xh=0, dg=0)

    def add(kind, q=0, s=0, n=0, x=0, u=0, **kw):
        phases.append(dict(kind=kind, **at, **kw))
        halves = kw["T"] // LAT if kind == "norm" else 0
        for key, v in dict(q=q, s=s, n=n, x=x, u=u, xh=DT * halves, dg=2 * halves).items():
            at[key] += v

    for L in range(DEPTH):
        last = L == DEPTH - 1
        add("norm", n=1, x=DT, L=L, sub=0, T=TOK)
        add("up", q=UP_PAIRS, s=UP_PAIRS, u=FT, L=L, f=1, T=TOK, mod0=L * MODT + EARLY_MODS, mods=UP_PAIRS)
        add("down", q=8, s=2, L=L, f=1, T=TOK, gate=2, half=0.5, rows=W2_ROWS)
        add("norm", n=1, x=DT, L=L, sub=1, T=TOK)
        if L == 0:
            add("diff_qk", q=4, s=4)
            add("diff_v", q=2, s=2)
            add("diff_attn", x=DH)
            add("down", q=2, s=2, L=L, f=0, T=TOK, gate=5, half=1.0, rows=(8,))
        else:
            add("ret_q", q=2, s=2)
            add("ret_k", q=2, s=2)
            add("ret_v", q=4, s=4)
            add("ret_attn")
            add("ret_gate", q=4, s=4, x=16)
            add("down", q=4, s=2, L=L, f=0, T=LAT, gate=5, half=1.0, rows=(8, 8))
        add("norm", n=1, x=DT, L=L, sub=2, T=LAT if last else TOK)
        add("up", q=UP_PAIRS, s=UP_PAIRS, u=FT, L=L, f=2, T=LAT if last else TOK,
            mod0=MODT if L == 0 else None, mods=EARLY_MODS // MODS_PER_PAIR if L == 0 else 0)
        add("down", q=8, s=2, L=L, f=2, T=LAT if last else TOK, gate=8, half=0.5, rows=W2_ROWS)
    add("final", n=1)
    return phases


def row(t, i):
    if isinstance(i, int):
        return t[:, i, :]
    return t[:, bass.ds(i, 1), :].rearrange("p a b -> p (a b)")


def trunk(nc, x, c, ctx_in, c_ctx, mod_w, mod_b, f1_w13, f1_w2, f2_w13, f2_w2, diff_w_in, diff_w_out,
          diff_lambda, diff_subln_g, ret_w_in, ret_w_out, ret_decay_exp, final_norm_g, consts, out):
    phases = plan()
    pairs_total = phases[-1]["q"]

    with ExitStack() as stack:
        def sb(name, shape, dt=F32, where=stack):
            return where.enter_context(nc.sbuf_tensor(name, shape, dt))

        def sem(name):
            return stack.enter_context(nc.semaphore(name))

        hT = sb("hT", [P, DT, TOK])
        xh = sb("xh", [P, DT, TOK], F32R)
        xl = sb("xl", [P, DT, TOK], F32R)
        raw = sb("raw", [P, 2, 8, CW])
        wh = sb("wh", [P, 2, 8, CW], F32R)
        wl = sb("wl", [P, 2, 8, CW], F32R)
        tmp = sb("tmp", [P, 5, TOK])
        keep = sb("keep", [P, C_KEEP])
        ones = sb("ones", [P, P])
        modT = sb("modT", [P, DEPTH * MODT, 2])
        modb = sb("modb", [P, DEPTH * MODT])
        cond = sb("cond", [P, DT, 2])
        gcols = sb("gcols", [P, DT + 1])
        sc1 = sb("sc1", [P, DT, 2])
        gate = sb("gate", [P, DT, 2])
        small = sb("small", [P, 168])
        ident, swap_d, swap_r, gap = keep[:, 0:P], keep[:, P:2 * P], keep[:, 2 * P:3 * P], keep[:, 3 * P:]
        ssq = tmp[:, 4, :]
        diag = tmp[:, 4, :]
        modw = sb("modw", [P, 2 * DT * P])
        modw_slot = modw[:].rearrange("p (s k c) -> p s k c", s=2, k=DT)
        later, earlier, twice = (modw[:, n * 2 * LAT:(n + 1) * 2 * LAT].rearrange("p (k t) -> p k t", k=2)
                                 for n in range(3))

        with ExitStack() as g:
            uh = sb("uh", [P, FT, TOK], F32R, where=g)
            ul = sb("ul", [P, FT, TOK], F32R, where=g)
        with ExitStack() as g:
            oh = sb("oh", [P, 2 * D // P, LAT], F32R, where=g)
            ol = sb("ol", [P, 2 * D // P, LAT], F32R, where=g)
        region = sb("region", [P, 2 * FT * TOK])
        taken = [0]

        def part(*shape, at=None):
            a = taken[0] if at is None else at
            n = int(np.prod(shape))
            taken[0] = a + n
            assert taken[0] <= 2 * FT * TOK
            names = "abcd"[:len(shape)]
            flat = region[:, a:a + n]
            if len(shape) == 1:
                return flat
            return flat.rearrange(f"p ({' '.join(names)}) -> p {' '.join(names)}",
                                  **{k: v for k, v in zip(names[1:], shape[1:])})

        crows = part(P, at=0)
        brows = part(DEPTH, P)
        lamr = part(4, DD)
        lamp = part(2, DD)
        decr = part(2 * RH)
        assert taken[0] <= 2 * TOK
        in_uh = (FT * TOK - 2 * TOK) // (DT * CW)
        stage = [part(DT, CW, at=2 * TOK + n * DT * CW if n < in_uh else FT * TOK + 2 * TOK + (n - in_uh) * DT * CW)
                 for n in range(STAGE)]
        xrows = part(TT, D)
        qk = part(2 * DH, TOK, at=0)
        vd = part(TT, D)
        ex = part(2, 2, TOK)
        aTd = part(2, TT, LAT)
        orawd = part(DH, TOK)
        droped = part(2, LAT)
        qr = part(DT, LAT, at=0)
        kr = part(DT, TOK)
        vr = part(TT, 2 * D)
        dec = part(2, TT, LAT)
        aTr = part(2, TT, LAT)
        orawr = part(2 * D // P, LAT)
        rroped = part(2, 2, LAT, at=taken[0] - 4 * LAT)
        ylast = part(DT, LAT, at=0)
        yrows = part(2, D)

        used = [0]

        def cols(n):
            a = used[0]
            used[0] = a + n
            return small[:, a:a + n]

        var, rstd, nhalf = cols(TT), cols(TT), cols(1)
        lam2, lam_e, neglam, subg = cols(2), cols(2), cols(1), cols(1)
        top, shift, mass, share = cols(4), cols(4), cols(4), cols(4)
        hvar, hrstd = cols(DH * TT), cols(DH * TT)
        one_less, left, lgam, nlgam, corr = (cols(2 * RH) for _ in range(5))
        bias_f, bias_b = cols(2 * RH), cols(2 * RH)

        pt = stack.enter_context(nc.psum_tensor("pt", [P, 8, TOK], F32))
        SUM, BC = 7, 6

        raw_landed = [sem("raw_landed0"), sem("raw_landed1")]
        hi_ready = sem("hi_ready")
        lo_ready = sem("lo_ready")
        chunk_done = sem("chunk_done")
        first_tile_done = sem("first_tile_done")
        evac = [sem("evac0"), sem("evac1")]
        u_hi_done, u_ready = sem("u_hi_done"), sem("u_ready")
        x_ready = sem("x_ready")
        x_hi_done = sem("x_hi_done")
        normed, affine = sem("normed"), sem("affine")
        sq_ready, sq_added = sem("sq_ready"), sem("sq_added")
        sum_ready, var_ready, rstd_ready = sem("sum_ready"), sem("var_ready"), sem("rstd_ready")
        diag_ready, bcast_ready = sem("diag_ready"), sem("bcast_ready")
        cols_ready = sem("cols_ready")
        mod_landed = [sem("mod_landed0"), sem("mod_landed1")]
        mod_used, mod_ready = sem("mod_used"), sem("mod_ready")
        stage_landed = [sem(f"stage_landed{n}") for n in range(STAGE)]
        keep_landed, xrows_landed, rows_landed = sem("keep_landed"), sem("xrows_landed"), sem("rows_landed")
        ones_ready, turned, unturned = sem("ones_ready"), sem("turned"), sem("unturned")
        cond_ready, h_loaded = sem("cond_ready"), sem("h_loaded")
        lam_step, lam_exp = sem("lam_step"), sem("lam_exp")
        rope_landed, swapped, rope_terms, roped = (sem("rope_landed"), sem("swapped"), sem("rope_terms"),
                                                   sem("roped"))
        scored, topped, shifted, exped = sem("scored"), sem("topped"), sem("shifted"), sem("exped")
        share_step, mixed, probs_turned, probs_ready = (sem("share_step"), sem("mixed"), sem("probs_turned"),
                                                        sem("probs_ready"))
        pv_done, o_copied, o_squared, o_summed = sem("pv_done"), sem("o_copied"), sem("o_squared"), sem("o_summed")
        hvar_ready, hrstd_ready, hdiag_ready, hbcast_ready = (sem("hvar_ready"), sem("hrstd_ready"),
                                                              sem("hdiag_ready"), sem("hbcast_ready"))
        o_scaled, o_hi = sem("o_scaled"), sem("o_hi")
        g_step, g_act, expo_ready = sem("g_step"), sem("g_act"), sem("expo_ready")
        dec_sum, dec_exp, dec_done = sem("dec_sum"), sem("dec_exp"), sem("dec_done")
        rscored, rprobs, rpv, rcopied, rsquared, rsummed = (sem("rscored"), sem("rprobs"), sem("rpv"),
                                                            sem("rcopied"), sem("rsquared"), sem("rsummed"))
        rvar, rrstd, rdiag, rbcast, rscaled = sem("rvar"), sem("rrstd"), sem("rdiag"), sem("rbcast"), sem("rscaled")
        gated, gate_hi = sem("gated"), sem("gate_hi")
        y_done, y_turned, y_copied, stored = sem("y_done"), sem("y_turned"), sem("y_copied"), sem("stored")

        w13 = {1: f1_w13, 2: f2_w13}
        w2 = {1: f1_w2, 2: f2_w2}
        mod_v = [mod_w[L].rearrange("(k p) (m c) -> p k m c", p=P, c=P) for L in range(DEPTH)]
        early_v = mod_w[0].rearrange("(k p) (m c) -> p k m c", p=P, c=CW)
        early_groups = EARLY_MODS // 2

        def mod_counts(L, group):
            return L * MODT + (group + 1) * DT

        block = stack.enter_context(nc.Block())

        @block.sync
        def _(sp):
            def load(n, slot, pair, src, rows=8, first=False):
                if not first:
                    sp.wait_ge(lo_ready, n - 1)
                sp.dma_start(raw[:, slot, 0:rows, :], src).then_inc(raw_landed[slot], 16)

            def column(v, j):
                return v[:, :, j, :] if isinstance(j, int) else v[:, :, bass.ds(j, 1), :].rearrange("p k j c -> p k (j c)")

            def early(g):
                if g >= STAGE:
                    sp.wait_ge(mod_used, 2 * (g - STAGE + 1))
                sp.dma_start(stage[g % STAGE], early_v[:, :, g, :]).then_inc(stage_landed[g % STAGE], 16)

            sp.dma_start(keep[:], consts[:, 0:C_KEEP]).then_inc(keep_landed, 16)
            for k, src in enumerate((c, c_ctx.rearrange("(a n) -> a n", a=1), final_norm_g.rearrange("(a n) -> a n", a=1))):
                sp.dma_start(crows[k * DT:(k + 1) * DT, :], src.rearrange("a (k p) -> (a k) p", p=P)).then_inc(rows_landed, 16)
            sp.dma_start(crows[3 * DT:3 * DT + 1, :], diff_subln_g).then_inc(rows_landed, 16)
            for L in range(DEPTH):
                sp.dma_start(brows[0:MODT, L, :], mod_b[L].rearrange("(m p) -> m p", p=P)).then_inc(rows_landed, 16)
            for n in range(2):
                sp.dma_start(xrows[:, n, :], x[0, n * P:(n + 1) * P, :]).then_inc(xrows_landed, 16)
                sp.dma_start(xrows[:, 2 + n, :], ctx_in[0, n * P:(n + 1) * P, :]).then_inc(xrows_landed, 16)
            sp.dma_start(lamr, diff_lambda[0].partition_broadcast(P)).then_inc(rows_landed, 16)
            sp.dma_start(decr, ret_decay_exp[0].rearrange("r h -> (r h)").partition_broadcast(P)).then_inc(rows_landed, 16)
            for g in range(STAGE):
                early(g)

            for ph in phases:
                kind, q0 = ph["kind"], ph["q"]
                if kind == "up":
                    v = w13[ph["f"]][ph["L"]].rearrange("(k p) (a j c) -> a p k j c", p=P, a=2, c=CW)

                    def pair(i, first=False):
                        for s in range(2):
                            load(2 * (q0 + i) + s, s, q0 + i, column(v[s], i), first=first)

                    if q0 == 0:
                        pair(0, first=True)
                        for g in range(STAGE, early_groups):
                            if g == (STAGE + early_groups) // 2:
                                pair(1)
                            early(g)
                        rest = 2
                    else:
                        rest = 0
                    with sp.Fori(rest, UP_PAIRS) as i:
                        pair(i)
                elif kind == "down":
                    v = (w2[ph["f"]][ph["L"]] if ph["f"] else (diff_w_out if ph["L"] == 0 else ret_w_out)[0]).rearrange(
                        "(k p) (j c) -> p k j c", p=P, c=CW)
                    nc_ = len(ph["rows"])
                    with sp.Fori(0, 2) as i:
                        for g in range(2):
                            k0 = 0
                            for e, rows in enumerate(ph["rows"]):
                                n = g * nc_ + e
                                load(2 * q0 + 2 * nc_ * i + n, n % 2, None, column(v[:, k0:k0 + rows], 2 * i + g), rows)
                                k0 += rows
                elif kind in ("diff_qk", "diff_v", "ret_q", "ret_k", "ret_v", "ret_gate"):
                    w, col0, count = {"diff_qk": (diff_w_in, 0, 4), "diff_v": (diff_w_in, 2 * D, 2),
                                      "ret_q": (ret_w_in, 0, 2), "ret_k": (ret_w_in, D, 2),
                                      "ret_v": (ret_w_in, 2 * D, 4), "ret_gate": (ret_w_in, 4 * D, 4)}[kind]
                    v = w[0][:, col0:col0 + 2 * count * CW].rearrange("(k p) (j c) -> p k j c", p=P, c=CW)
                    if kind == "diff_v":
                        sp.wait_ge(x_ready, ph["x"])
                        sp.dma_start(droped, consts[:, C_DROPE:C_RROPE].rearrange("p (a t) -> p a t", a=2)).then_inc(rope_landed, 16)
                    if kind == "ret_v":
                        sp.wait_ge(x_ready, ph["x"])
                        sp.dma_start(rroped, consts[:, C_RROPE:C_ALL].rearrange("p (a b t) -> p a b t", a=2, b=2)).then_inc(rope_landed, 16)
                    with sp.Fori(0, count) as i:
                        for s in range(2):
                            load(2 * (q0 + i) + s, s, None, column(v, 2 * i + s))
                elif kind == "final":
                    for n in range(2):
                        sp.wait_ge(y_copied, DT * (n + 1))
                        sp.dma_start(out[0, n * P:(n + 1) * P, :], yrows[:, n, :]).then_inc(stored, 16)
                    sp.wait_ge(stored, 32)

        @block.gpsimd
        def _(pool):
            nc.gpsimd.memset(ones[:], 1.0).then_inc(ones_ready, 1)
            nc.gpsimd.memset(nhalf, -0.5).then_inc(ones_ready, 1)

            def clear(n):
                if n:
                    pool.wait_ge(bcast_ready, n)
                nc.gpsimd.memset(ssq, 0.0).then_inc(sq_added, 1)

            def add(count, slot, T):
                nc.gpsimd.tensor_tensor(ssq[:, 0:T], ssq[:, 0:T], tmp[:, slot, 0:T], ALU.add).then_inc(sq_added, 1)

            def power(n, T):
                pool.wait_ge(var_ready, n + 1)
                if n == 0:
                    pool.wait_ge(ones_ready, 2)
                nc.gpsimd.tensor_tensor(rstd[:, 0:T // P], var[:, 0:T // P], nhalf.to_broadcast([P, T // P]),
                                        ALU.pow).then_inc(rstd_ready, 1)

            clear(0)
            for d in range(DT):
                pool.wait_ge(sq_ready, d + 1)
                pool.wait_ge(sq_added, d + 1)
                add(d, d % 2, TOK)
            for ph in phases:
                kind = ph["kind"]
                if kind in ("norm", "final"):
                    power(ph["n"], ph.get("T", LAT))
                elif kind == "up" and ph["mods"]:
                    L, m0 = ph["mod0"] // MODT, ph["mod0"]
                    early_left = ph["q"] == 0

                    def fetch(m, slot):
                        src = mod_v[L]
                        j = m - L * MODT
                        src = src[:, :, j, :] if isinstance(j, int) else src[:, :, bass.ds(j, 1), :].rearrange("p k m c -> p k (m c)")
                        pool.dma_start(modw_slot[:, slot], src).then_inc(mod_landed[slot], 16)

                    if early_left:
                        fetch(m0, 0)
                        fetch(m0 + 1, 1)
                    else:
                        for n in range(2):
                            pool.wait_ge(mod_used, m0 + n - 1)
                            fetch(m0 + n, n)
                    for n in range(2, MODS_PER_PAIR):
                        pool.wait_ge(mod_used, m0 + n - 1)
                        fetch(m0 + n, n % 2)
                    with pool.Fori(1, ph["mods"]) as i:
                        for n in range(MODS_PER_PAIR):
                            pool.wait_ge(mod_used, m0 + MODS_PER_PAIR * i + n - 1)
                            fetch(m0 + MODS_PER_PAIR * i + n, n % 2)
                elif kind == "down":
                    n, T = ph["n"], ph["T"]
                    clear(n)
                    with pool.Fori(0, 2) as i:
                        for b in range(4):
                            pool.wait_ge(sq_ready, DT * n + 4 * i + b + 1)
                            pool.wait_ge(sq_added, 9 * n + 4 * i + b + 1)
                            add(None, b % 2, T)
                elif kind == "diff_attn":
                    pool.wait_ge(hvar_ready, 1)
                    nc.gpsimd.tensor_tensor(hrstd, hvar, nhalf.to_broadcast([P, DH * TT]), ALU.pow).then_inc(hrstd_ready, 1)
                elif kind == "ret_attn":
                    pool.wait_ge(rvar, 1)
                    nc.gpsimd.tensor_tensor(hrstd[:, 0:2 * RH], hvar[:, 0:2 * RH], nhalf.to_broadcast([P, 2 * RH]),
                                            ALU.pow).then_inc(rrstd, 1)

        @block.scalar
        def _(act):
            def split(pair, s, first=False):
                act.wait_ge(raw_landed[s], 16 * (pair + 1))
                if not first:
                    act.wait_ge(chunk_done, 2 * pair + s - 1)
                nc.scalar.copy(wh[:, s], raw[:, s]).then_inc(hi_ready, 1)

            def tile_done(set_use, s, t, n):
                if t == 0:
                    act.wait_ge(first_tile_done, 2 * set_use + s + 1)
                else:
                    act.wait_ge(chunk_done, n + 1)

            def square(n, e, slot, d, T):
                nc.scalar.activation(tmp[:, slot, 0:T], row(hT, d)[:, 0:T], ACT.Square).then_inc(sq_ready, 1)

            act.wait_ge(turned, 1)
            nc.scalar.activation(cond[:, :, 0], pt[:, 4, 0:DT], ACT.Silu).then_inc(cond_ready, 1)
            nc.scalar.activation(cond[:, :, 1], pt[:, 4, DT:2 * DT], ACT.Silu).then_inc(cond_ready, 1)
            nc.scalar.copy(gcols[:], pt[:, 4, 2 * DT:3 * DT + 1]).then_inc(cond_ready, 1)
            for d in range(DT):
                act.wait_ge(h_loaded, d + 1)
                if d >= 2:
                    act.wait_ge(sq_added, d)
                square(0, d, d % 2, d, TOK)
            for s in range(2):
                split(0, s, first=True)

            for ph in phases:
                kind, q0, s0, T = ph["kind"], ph["q"], ph["s"], ph.get("T")
                if kind == "norm":
                    n, x0, m0 = ph["n"], ph["x"], ph["L"] * MODT + 3 * ph["sub"] * DT
                    act.wait_ge(cols_ready, 2 * n + 1)
                    act.wait_ge(mod_ready, mod_counts(ph["L"], 3 * ph["sub"] + 1))
                    for k in range(DT):
                        act.wait_ge(normed, DT * n + k + 1)
                        for b in range(T // LAT):
                            nc.scalar.activation(xh[:, k, b * LAT:(b + 1) * LAT], tmp[:, k % 2, b * LAT:(b + 1) * LAT],
                                                 ACT.Identity, bias=modT[:, m0 + k, b:b + 1],
                                                 scale=sc1[:, k, b:b + 1]).then_inc(x_hi_done, 1)
                elif kind == "up":
                    def pair(i):
                        for t in range(2):
                            tile_done(s0 + i, 0, t, 2 * (q0 + i))
                            nc.scalar.activation(tmp[:, t, 0:T], pt[:, t, 0:T], ACT.Silu).then_inc(evac[0], 1)
                        split(q0 + i + 1, 0)
                        for t in range(2):
                            act.wait_ge(evac[1], 2 * (s0 + i) + t + 1)
                            nc.scalar.copy(row(uh, 2 * i + t)[:, 0:T], tmp[:, 2 + t, 0:T]).then_inc(u_hi_done, 1)
                        split(q0 + i + 1, 1)

                    pair(0)
                    with act.Fori(1, UP_PAIRS) as i:
                        pair(i)
                elif kind == "down":
                    nc_, n = len(ph["rows"]), ph["n"]

                    def two_tiles(i):
                        for g in range(2):
                            for e in range(nc_):
                                c_ = g * nc_ + e
                                chunk = 2 * q0 + 2 * nc_ * i + c_
                                if e == nc_ - 1:
                                    for t in range(2):
                                        act.wait_ge(evac[g], 2 * (s0 + i) + t + 1)
                                        act.wait_ge(sq_added, 9 * n + 4 * i + 2 * g + t)
                                        square(n, None, t, 4 * i + 2 * g + t, T)
                                pair = q0 + nc_ * i + c_ // 2 + 1
                                if isinstance(pair, int) and pair >= pairs_total:
                                    continue
                                split(pair, c_ % 2)

                    if q0 + 2 * nc_ == pairs_total:
                        for i in range(2):
                            two_tiles(i)
                    else:
                        with act.Fori(0, 2) as i:
                            two_tiles(i)
                elif kind in ("diff_qk", "ret_q", "ret_k"):
                    dst, T = {"diff_qk": (qk, TOK), "ret_q": (qr, LAT), "ret_k": (kr, TOK)}[kind]
                    with act.Fori(0, (2 if kind != "diff_qk" else 4)) as i:
                        for s in range(2):
                            for t in range(2):
                                tile_done(s0 + i, s, t, 2 * (q0 + i) + s)
                                nc.scalar.copy(row(dst, 4 * i + 2 * s + t)[:, 0:T], pt[:, 2 * s + t, 0:T]).then_inc(evac[s], 1)
                            split(q0 + i + 1, s)
                elif kind in ("diff_v", "ret_v"):
                    dst, count = (vd, 2) if kind == "diff_v" else (vr, 4)
                    with act.Fori(0, count) as i:
                        for s in range(2):
                            for b in range(2):
                                tile_done(s0 + i, s, b, 2 * (q0 + i) + s)
                                nc.scalar.copy(dst[:, 2 * b:2 * b + 2, bass.ds((2 * i + s) * CW, CW)],
                                               pt[:, 2 * s + b, :].rearrange("p (a c) -> p a c", a=2)).then_inc(evac[s], 1)
                            split(q0 + i + 1, s)
                elif kind == "diff_attn":
                    act.wait_ge(lam_step, 2)
                    nc.scalar.activation(lam_e, lam2, ACT.Exp).then_inc(lam_exp, 1)

                    def exps(u, b):
                        nk = TOK if u % 2 == 0 else CTX
                        act.wait_ge(shifted, 2 * u + b + 1)
                        if u:
                            act.wait_ge(probs_turned, 2 * (u - 1) + b + 1)
                        for j in range(2):
                            nc.scalar.activation(ex[:, b, j, 0:nk], pt[:, 2 * b + j, 0:nk], ACT.Exp, scale=DD ** -0.5,
                                                 bias=shift[:, 2 * b + j:2 * b + j + 1],
                                                 accum_out=mass[:, 2 * b + j:2 * b + j + 1]).then_inc(exped, 1)

                    def turn_out(u, b):
                        k0, nt = (0, TT) if u % 2 == 0 else (TT // 2, TT // 2)
                        act.wait_ge(probs_turned, 2 * u + b + 1)
                        if u >= 2:
                            act.wait_ge(pv_done, u - 1)
                        nc.scalar.copy(aTd[:, u % 2, k0:k0 + nt, b * P:(b + 1) * P],
                                       pt[:, 4 + b, k0 * P:(k0 + nt) * P].rearrange("p (k c) -> p k c", k=nt)).then_inc(probs_ready, 1)

                    def square_o(h):
                        act.wait_ge(o_copied, h + 1)
                        if h >= 2:
                            act.wait_ge(o_summed, h - 1)
                        nc.scalar.activation(tmp[:, h % 2, :], orawd[:, h, :], ACT.Square).then_inc(o_squared, 1)

                    for u in range(2 * DH + 1):
                        for b in range(2):
                            if u < 2 * DH:
                                exps(u, b)
                            if u:
                                turn_out(u - 1, b)
                        if u and u % 2 == 0:
                            square_o(u // 2 - 1)
                    for h in range(DH):
                        act.wait_ge(o_scaled, h + 1)
                        nc.scalar.copy(xh[:, h, :], tmp[:, 2 + h % 2, :]).then_inc(o_hi, 1)
                elif kind == "ret_attn":
                    def square_r(h):
                        act.wait_ge(rcopied, h + 1)
                        if h:
                            act.wait_ge(rsummed, h)
                        nc.scalar.activation(tmp[:, 0:2, :].rearrange("p a c -> p (a c)"),
                                             orawr[:, 4 * h:4 * h + 4, :].rearrange("p a c -> p (a c)"),
                                             ACT.Square).then_inc(rsquared, 1)

                    act.wait_ge(g_step, 1)
                    y = hvar[:, 0:2 * RH]
                    nc.scalar.activation(y, lgam, ACT.Exp, scale=-float(np.log(2.0))).then_inc(g_act, 1)
                    act.wait_ge(g_step, 3)
                    nc.scalar.activation(lgam, one_less, ACT.Ln).then_inc(g_act, 1)
                    act.wait_ge(g_step, G_STEPS)
                    for h in range(RH):
                        if h >= 2:
                            act.wait_ge(rprobs, h - 1)
                        act.wait_ge(dec_sum, h + 1)
                        nc.scalar.activation(dec[:, h % 2, 0:2], dec[:, h % 2, 0:2], ACT.Exp).then_inc(dec_exp, 1)
                        for k in range(2):
                            nc.scalar.activation(dec[:, h % 2, 2 + k], gap, ACT.Exp, scale=lgam[:, h:h + 1],
                                                 bias=bias_f[:, 2 * h + k:2 * h + k + 1]).then_inc(dec_exp, 1)
                            nc.scalar.activation(tmp[:, 2 + h % 2, k * LAT:(k + 1) * LAT], gap, ACT.Exp,
                                                 scale=nlgam[:, RH + h:RH + h + 1],
                                                 bias=bias_b[:, 2 * h + k:2 * h + k + 1]).then_inc(dec_exp, 1)
                        if h:
                            square_r(h - 1)
                    square_r(RH - 1)
                elif kind == "ret_gate":
                    def gate_pair(i):
                        for s in range(2):
                            for t in range(2):
                                tile_done(s0 + i, s, t, 2 * (q0 + i) + s)
                                nc.scalar.activation(tmp[:, t, 0:LAT], pt[:, 2 * s + t, 0:LAT], ACT.Silu).then_inc(evac[s], 1)
                            for t in range(2):
                                act.wait_ge(gated, 4 * i + 2 * s + t + 1)
                                nc.scalar.copy(row(oh, 4 * i + 2 * s + t), tmp[:, 2 + t, 0:LAT]).then_inc(gate_hi, 1)
                            split(q0 + i + 1, s)

                    gate_pair(0)
                    with act.Fori(1, 4) as i:
                        gate_pair(i)

        @block.vector
        def _(dve):
            def rest(chunk, s):
                dve.wait_ge(hi_ready, chunk + 1)
                nc.vector.tensor_tensor(wl[:, s], raw[:, s], wh[:, s].bitcast(F32), ALU.subtract).then_inc(lo_ready, 1)

            def tile_done(set_use, s, t, n):
                if t == 0:
                    dve.wait_ge(first_tile_done, 2 * set_use + s + 1)
                else:
                    dve.wait_ge(chunk_done, n + 1)

            def mod_out(m, b):
                dve.wait_ge(mod_used, m + 1)
                bias = modb[:, m:m + 1] if isinstance(m, int) else modb[:, bass.ds(m, 1)]
                nc.vector.tensor_scalar(row(modT, m), pt[:, 4 + b, 0:2], bias, None, ALU.add).then_inc(mod_ready, 1)

            def mean(dst, src, width):
                return nc.vector.tensor_scalar(dst, src, 1.0 / width, EPS, ALU.mult, ALU.add)

            def gate_columns(ph):
                L, sub = ph["L"], ph["sub"]
                m0 = L * MODT + (3 * sub + 2) * DT
                dve.wait_ge(mod_ready, mod_counts(L, 3 * sub + 2))
                if ph["n"]:
                    dve.wait_ge(normed, DT * ph["n"])
                nc.vector.tensor_scalar(gate[:], modT[:, m0:m0 + DT, :], 1.0 if sub == 1 else 0.5, None,
                                        ALU.mult).then_inc(cols_ready, 1)

            dve.wait_ge(turned, 2)
            nc.vector.tensor_copy(modb[:, 0:MODT], pt[:, 5, 0:MODT]).then_inc(unturned, 1)
            dve.wait_ge(turned, 3)
            nc.vector.tensor_copy(modb[:, MODT:2 * MODT], pt[:, 6, 0:MODT]).then_inc(unturned, 1)
            for d in range(DT):
                dve.wait_ge(turned, 4 + d)
                nc.vector.tensor_copy(hT[:, d, :], pt[:, d % 4, :]).then_inc(h_loaded, 1)
            dve.wait_ge(rows_landed, 16 * 8)
            nc.vector.tensor_tensor(lamp, lamr[:, 0:4:2, :], lamr[:, 1:4:2, :], ALU.mult).then_inc(lam_step, 1)
            dve.wait_ge(lam_step, 1)
            nc.vector.tensor_reduce(lam2, lamp, AX.X, ALU.add).then_inc(lam_step, 1)
            nc.vector.tensor_copy(lgam, decr).then_inc(g_step, 1)
            dve.wait_ge(unturned, 2)
            for m in range(EARLY_NEED):
                mod_out(m, m % 2)
            for s in range(2):
                rest(s, s)

            for ph in phases:
                kind, q0, s0, T = ph["kind"], ph["q"], ph["s"], ph.get("T")
                if kind in ("norm", "final"):
                    n, T = ph["n"], T or LAT
                    if kind == "norm":
                        L, first = ph["L"], 3 * ph["sub"]
                        m0 = L * MODT + (first + 1) * DT
                        dve.wait_ge(mod_ready, mod_counts(L, first + 1))
                        nc.vector.tensor_scalar(sc1[:], modT[:, m0:m0 + DT, :], 1.0, None, ALU.add).then_inc(cols_ready, 1)
                    dve.wait_ge(sum_ready, n + 1)
                    mean(var[:, 0:T // P], pt[:, SUM, 0:T // P], D).then_inc(var_ready, 1)
                    dve.wait_ge(rstd_ready, n + 1)
                    for b in range(T // P):
                        nc.vector.tensor_scalar(diag[:, b * P:(b + 1) * P], ident, rstd[:, b:b + 1], None,
                                                ALU.mult).then_inc(diag_ready, 1)
                    dve.wait_ge(bcast_ready, n + 1)
                    if kind == "final":
                        for d in range(DT):
                            nc.vector.scalar_tensor_tensor(ylast[:, d], hT[:, d, 0:LAT], gcols[:, d:d + 1],
                                                           pt[:, BC, 0:LAT], ALU.mult, ALU.mult).then_inc(y_done, 1)
                        for b in range(2):
                            for d in range(DT):
                                e = DT * b + d
                                dve.wait_ge(y_turned, e + 1)
                                nc.vector.tensor_copy(yrows[:, b, d * P:(d + 1) * P], pt[:, e % 4, 0:P]).then_inc(y_copied, 1)
                        continue
                    halves = T // LAT
                    m0 = L * MODT + first * DT
                    dve.wait_ge(cols_ready, 2 * n + 1)

                    def normalise(k):
                        if k >= 2:
                            dve.wait_ge(x_hi_done, ph["xh"] + halves * (k - 1))
                        nc.vector.tensor_tensor(tmp[:, k % 2, 0:T], hT[:, k, 0:T], pt[:, BC, 0:T], ALU.mult).then_inc(normed, 1)

                    normalise(0)
                    for k in range(DT):
                        if k + 1 < DT:
                            normalise(k + 1)
                        dve.wait_ge(normed, DT * n + k + 1)
                        for b in range(halves):
                            cut = slice(b * LAT, (b + 1) * LAT)
                            nc.vector.tensor_scalar(tmp[:, 2 + k % 2, cut], tmp[:, k % 2, cut], sc1[:, k, b:b + 1],
                                                    modT[:, m0 + k, b:b + 1], ALU.mult, ALU.add).then_inc(affine, 1)
                        dve.wait_ge(affine, ph["xh"] + halves * (k + 1))
                        dve.wait_ge(x_hi_done, ph["xh"] + halves * (k + 1))
                        nc.vector.tensor_tensor(xl[:, k, 0:T], tmp[:, 2 + k % 2, 0:T], xh[:, k, 0:T].bitcast(F32),
                                                ALU.subtract).then_inc(x_ready, 1)
                    if not (n == 0):
                        gate_columns(ph)
                elif kind == "up":
                    def pair(i, mods, first=False):
                        m = None if not mods else ph["mod0"] + MODS_PER_PAIR * i
                        behind = first or not mods
                        if not behind:
                            mod_out(m, 0)
                        rest(2 * (q0 + i + 1), 0)
                        if not behind:
                            mod_out(m + 1, 1)
                        for t in range(2):
                            tile_done(s0 + i, 1, t, 2 * (q0 + i) + 1)
                            dve.wait_ge(evac[0], 2 * (s0 + i) + t + 1)
                            nc.vector.tensor_tensor(tmp[:, 2 + t, 0:T], tmp[:, t, 0:T], pt[:, 2 + t, 0:T],
                                                    ALU.mult).then_inc(evac[1], 1)
                            if not behind and t == 0:
                                mod_out(m + 2, 0)
                        for t in range(2):
                            dve.wait_ge(u_hi_done, ph["u"] + 2 * i + t + 1)
                            nc.vector.tensor_tensor(row(ul, 2 * i + t)[:, 0:T], tmp[:, 2 + t, 0:T],
                                                    row(uh, 2 * i + t)[:, 0:T].bitcast(F32), ALU.subtract).then_inc(u_ready, 1)
                        rest(2 * (q0 + i + 1) + 1, 1)
                        if not behind:
                            mod_out(m + 3, 1)
                        if first and q0 == 0:
                            for e in range(EARLY_NEED, EARLY_MODS):
                                mod_out(e, e % 2)
                        if first and mods:
                            for e in range(MODS_PER_PAIR):
                                mod_out(m + e, e % 2)

                    pair(0, ph["mods"] > 0, first=True)
                    if ph["mods"]:
                        with dve.Fori(1, ph["mods"]) as i:
                            pair(i, True)
                    if ph["mods"] < UP_PAIRS:
                        with dve.Fori(max(1, ph["mods"]), UP_PAIRS) as i:
                            pair(i, False)
                    if ph["n"] == 1:
                        gate_columns(dict(L=0, sub=0, n=0))
                elif kind == "down":
                    nc_ = len(ph["rows"])
                    dve.wait_ge(cols_ready, 2 * ph["n"])

                    def two_tiles(i):
                        for g in range(2):
                            for e in range(nc_):
                                c_ = g * nc_ + e
                                chunk = 2 * q0 + 2 * nc_ * i + c_
                                if e == nc_ - 1:
                                    for t in range(2):
                                        tile_done(s0 + i, g, t, chunk)
                                        d = 4 * i + 2 * g + t
                                        for b in range(T // LAT):
                                            cut = slice(b * LAT, (b + 1) * LAT)
                                            ins = nc.vector.scalar_tensor_tensor(
                                                row(hT, d)[:, cut], pt[:, 2 * g + t, cut], row(gate, d)[:, b:b + 1],
                                                row(hT, d)[:, cut], ALU.mult, ALU.add)
                                        ins.then_inc(evac[g], 1)
                                if isinstance(chunk, int) and chunk + 2 >= 2 * pairs_total:
                                    continue
                                rest(chunk + 2, c_ % 2)

                    if q0 + 2 * nc_ == pairs_total:
                        for i in range(2):
                            two_tiles(i)
                    else:
                        with dve.Fori(0, 2) as i:
                            two_tiles(i)
                elif kind in ("diff_qk", "ret_q", "ret_k"):
                    with dve.Fori(0, (2 if kind != "diff_qk" else 4)) as i:
                        for s in range(2):
                            rest(2 * (q0 + i + 1) + s, s)
                elif kind in ("diff_v", "ret_v"):
                    diff = kind == "diff_v"
                    per, count, base = (4, 2, 0) if diff else (2, 4, 16)
                    cos_sin = (lambda t: (droped[:, 0], droped[:, 1])) if diff else (lambda t: (rroped[:, 0, t % 2], rroped[:, 1, t % 2]))

                    def rope(r, bank, tile, table):
                        cos, sin = table
                        dve.wait_ge(swapped, r + 1)
                        nc.vector.tensor_tensor(tmp[:, bank % 2, 0:LAT], pt[:, bank, 0:LAT], sin, ALU.mult).then_inc(rope_terms, 1)
                        nc.vector.tensor_tensor(tile, tile, cos, ALU.mult).then_inc(rope_terms, 1)
                        dve.wait_ge(rope_terms, 2 * r + 2)
                        nc.vector.tensor_tensor(tile, tile, tmp[:, bank % 2, 0:LAT], ALU.add).then_inc(roped, 1)

                    dve.wait_ge(rope_landed, 16 if diff else 32)
                    for s in range(2):
                        dve.wait_ge(evac[s], 2 * s0)
                    with dve.Fori(0, count) as i:
                        for s in range(2):
                            rest(2 * (q0 + i + 1) + s, s)
                            for e in range(per):
                                r = base + 2 * per * i + per * s + e
                                tile = row(qk, 8 * i + 4 * s + e) if diff else row((qr, kr)[s], 2 * i + e)
                                rope(r, 4 + (per * s + e) % 4, tile[:, 0:LAT], cos_sin(e))
                elif kind == "diff_attn":
                    dve.wait_ge(lam_exp, 1)
                    nc.vector.tensor_tensor(neglam, lam_e[:, 1:2], lam_e[:, 0:1], ALU.subtract).then_inc(lam_step, 1)
                    dve.wait_ge(lam_step, 3)
                    nc.vector.tensor_scalar(neglam, neglam, -LAM_INIT, None, ALU.add).then_inc(lam_step, 1)
                    nc.vector.tensor_scalar(subg, gcols[:, DT:DT + 1], 1.0 - LAM_INIT, None, ALU.mult).then_inc(lam_step, 1)
                    dve.wait_ge(lam_step, 5)

                    def row_max(u, b):
                        nk = TOK if u % 2 == 0 else CTX
                        dve.wait_ge(scored, 2 * u + b + 1)
                        nc.vector.tensor_reduce(top[:, 2 * b:2 * b + 2], pt[:, 2 * b:2 * b + 2, 0:nk], AX.X, ALU.max).then_inc(topped, 1)
                        dve.wait_ge(topped, 2 * u + b + 1)
                        nc.vector.tensor_scalar(shift[:, 2 * b:2 * b + 2], top[:, 2 * b:2 * b + 2], -(DD ** -0.5), None,
                                                ALU.mult).then_inc(shifted, 1)

                    def mix(u, b):
                        nk = TOK if u % 2 == 0 else CTX
                        v = 2 * u + b
                        dve.wait_ge(exped, 2 * v + 2)
                        nc.vector.reciprocal(share[:, 2 * b:2 * b + 2], mass[:, 2 * b:2 * b + 2]).then_inc(share_step, 1)
                        dve.wait_ge(share_step, 3 * v + 1)
                        nc.vector.tensor_tensor(share[:, 2 * b + 1:2 * b + 2], share[:, 2 * b + 1:2 * b + 2], neglam,
                                                ALU.mult).then_inc(share_step, 1)
                        nc.vector.tensor_scalar(ex[:, b, 0, 0:nk], ex[:, b, 0, 0:nk], share[:, 2 * b:2 * b + 1], None,
                                                ALU.mult).then_inc(share_step, 1)
                        dve.wait_ge(share_step, 3 * v + 3)
                        nc.vector.scalar_tensor_tensor(ex[:, b, 0, 0:nk], ex[:, b, 1, 0:nk], share[:, 2 * b + 1:2 * b + 2],
                                                       ex[:, b, 0, 0:nk], ALU.mult, ALU.add).then_inc(mixed, 1)

                    def copy_o(h):
                        dve.wait_ge(pv_done, 2 * h + 2)
                        nc.vector.tensor_copy(orawd[:, h, :], pt[:, 6, :]).then_inc(o_copied, 1)

                    row_max(0, 0)
                    row_max(0, 1)
                    for u in range(2 * DH):
                        for b in range(2):
                            mix(u, b)
                            if u + 1 < 2 * DH:
                                row_max(u + 1, b)
                        if u and u % 2 == 0:
                            copy_o(u // 2 - 1)
                    copy_o(DH - 1)
                    dve.wait_ge(o_summed, DH)
                    mean(hvar, pt[:, SUM, 0:DH * TT], P).then_inc(hvar_ready, 1)
                    dve.wait_ge(hrstd_ready, 1)

                    def head_diag(h):
                        if h >= 2:
                            dve.wait_ge(hbcast_ready, h - 1)
                        for b in range(TT):
                            nc.vector.tensor_scalar(tmp[:, h % 2, b * P:(b + 1) * P], ident,
                                                    hrstd[:, TT * h + b:TT * h + b + 1], None, ALU.mult).then_inc(hdiag_ready, 1)

                    head_diag(0)
                    for h in range(DH):
                        if h + 1 < DH:
                            head_diag(h + 1)
                        dve.wait_ge(hbcast_ready, h + 1)
                        nc.vector.scalar_tensor_tensor(tmp[:, 2 + h % 2, :], orawd[:, h, :], subg, pt[:, 6 + h % 2, :],
                                                       ALU.mult, ALU.mult).then_inc(o_scaled, 1)
                        dve.wait_ge(o_hi, h + 1)
                        nc.vector.tensor_tensor(xl[:, h, :], tmp[:, 2 + h % 2, :], xh[:, h, :].bitcast(F32),
                                                ALU.subtract).then_inc(x_ready, 1)
                elif kind == "ret_attn":
                    y = hvar[:, 0:2 * RH]
                    step = [1]

                    def link(ins, wait=True):
                        step[0] += 1
                        ins.then_inc(g_step, 1)
                        if wait:
                            dve.wait_ge(g_step, step[0])

                    dve.wait_ge(g_act, 1)
                    link(nc.vector.tensor_scalar(one_less, y, -1.0, 1.0, ALU.mult, ALU.add))
                    link(nc.vector.tensor_scalar(left, one_less, -1.0, 1.0, ALU.mult, ALU.add))
                    link(nc.vector.tensor_tensor(left, left, y, ALU.subtract), wait=False)
                    link(nc.vector.reciprocal(corr, one_less))
                    link(nc.vector.tensor_tensor(corr, corr, left, ALU.mult))
                    dve.wait_ge(g_act, 2)
                    link(nc.vector.tensor_tensor(lgam, lgam, corr, ALU.add))
                    link(nc.vector.tensor_scalar(nlgam, lgam, -1.0, None, ALU.mult), wait=False)
                    for k in range(2):
                        link(nc.vector.tensor_scalar(bias_f[:, k:2 * RH:2], lgam[:, 0:RH], float(CTX - k * P), None, ALU.mult), wait=False)
                        link(nc.vector.tensor_scalar(bias_b[:, k:2 * RH:2], lgam[:, RH:2 * RH], float(LAT + k * P), None, ALU.mult), wait=False)
                    for k in range(2):
                        link(nc.vector.tensor_scalar(later[:, k], gap, -float(k * P), 0.0, ALU.add, ALU.max), wait=False)
                        link(nc.vector.tensor_scalar(earlier[:, k], gap, -float(k * P), 0.0, ALU.add, ALU.min), wait=False)
                        link(nc.vector.tensor_scalar(twice[:, k], gap, float(k * P), 1.0, ALU.is_equal, ALU.add), wait=False)
                    assert step[0] == G_STEPS
                    dve.wait_ge(g_step, G_STEPS)

                    def decays(h):
                        if h >= 2:
                            dve.wait_ge(rprobs, h - 1)
                        nc.vector.tensor_scalar(dec[:, h % 2, 0:2], earlier, nlgam[:, RH + h:RH + h + 1], None,
                                                ALU.mult).then_inc(expo_ready, 1)
                        dve.wait_ge(expo_ready, h + 1)
                        nc.vector.scalar_tensor_tensor(dec[:, h % 2, 0:2], later, lgam[:, h:h + 1], dec[:, h % 2, 0:2],
                                                       ALU.mult, ALU.add).then_inc(dec_sum, 1)

                    def copy_r(h):
                        dve.wait_ge(rpv, h + 1)
                        nc.vector.tensor_copy(orawr[:, 4 * h:4 * h + 4, :].rearrange("p k t -> p (k t)"),
                                              pt[:, 4:6, :].rearrange("p k t -> p (k t)")).then_inc(rcopied, 1)

                    decays(0)
                    for h in range(RH):
                        if h + 1 < RH:
                            decays(h + 1)
                        dve.wait_ge(dec_exp, 5 * h + 1)
                        nc.vector.tensor_tensor(dec[:, h % 2, 0:2], dec[:, h % 2, 0:2], twice, ALU.mult).then_inc(dec_done, 1)
                        dve.wait_ge(dec_exp, 5 * h + 5)
                        nc.vector.tensor_tensor(dec[:, h % 2, 2:4], dec[:, h % 2, 2:4],
                                                tmp[:, 2 + h % 2, :].rearrange("p (k t) -> p k t", k=2), ALU.add).then_inc(dec_done, 1)
                        dve.wait_ge(dec_done, 2 * h + 2)
                        dve.wait_ge(rscored, h + 1)
                        if h >= 2:
                            dve.wait_ge(rpv, h - 1)
                        nc.vector.scalar_tensor_tensor(aTr[:, h % 2].rearrange("p k t -> p (k t)"),
                                                       pt[:, 2 * (h % 2):2 * (h % 2) + 2, :].rearrange("p k t -> p (k t)"),
                                                       RK ** -0.5, dec[:, h % 2].rearrange("p k t -> p (k t)"),
                                                       ALU.mult, ALU.mult).then_inc(rprobs, 1)
                        if h:
                            copy_r(h - 1)
                    copy_r(RH - 1)
                    dve.wait_ge(rsummed, RH)
                    mean(hvar[:, 0:2 * RH], pt[:, SUM, 0:2 * RH], RV).then_inc(rvar, 1)
                    dve.wait_ge(rrstd, 1)

                    def head_diag(h):
                        if h >= 2:
                            dve.wait_ge(rbcast, h - 1)
                        for b in range(2):
                            nc.vector.tensor_scalar(tmp[:, h % 2, b * P:(b + 1) * P], ident,
                                                    hrstd[:, 2 * h + b:2 * h + b + 1], None, ALU.mult).then_inc(rdiag, 1)

                    head_diag(0)
                    for h in range(RH):
                        if h + 1 < RH:
                            head_diag(h + 1)
                        dve.wait_ge(rbcast, h + 1)
                        nc.vector.tensor_tensor(orawr[:, 4 * h:4 * h + 4, :], orawr[:, 4 * h:4 * h + 4, :],
                                                pt[:, 6 + h % 2:7 + h % 2, 0:LAT].broadcast_to([P, 4, LAT]),
                                                ALU.mult).then_inc(rscaled, 1)
                elif kind == "ret_gate":
                    dve.wait_ge(rscaled, RH)

                    def gate_pair(i):
                        for s in range(2):
                            for t in range(2):
                                dve.wait_ge(evac[s], 2 * (s0 + i) + t + 1)
                                dve.wait_ge(x_ready, ph["x"] + 4 * i + 2 * s + t - 1)
                                nc.vector.tensor_tensor(tmp[:, 2 + t, 0:LAT], tmp[:, t, 0:LAT],
                                                        row(orawr, 4 * i + 2 * s + t), ALU.mult).then_inc(gated, 1)
                            for t in range(2):
                                tile = 4 * i + 2 * s + t
                                dve.wait_ge(gate_hi, tile + 1)
                                nc.vector.tensor_tensor(row(ol, tile), tmp[:, 2 + t, 0:LAT], row(oh, tile).bitcast(F32),
                                                        ALU.subtract).then_inc(x_ready, 1)
                            rest(2 * (q0 + i + 1) + s, s)

                    with dve.Fori(0, 4) as i:
                        gate_pair(i)

        @block.tensor
        def _(pe):
            state = dict()

            def products(s, nk, hi, lo, T, start, stop, order, marks):
                def one(t, k):
                    a, b = start and k == 0, stop and k == nk - 1
                    cut = slice(t * P, (t + 1) * P)
                    bank = pt[:, s_bank + t, 0:T]
                    nc.tensor.matmul(bank, wh[:, s, k, cut], hi(k), start=a, stop=False)
                    nc.tensor.matmul(bank, wh[:, s, k, cut], lo(k), start=False, stop=False)
                    return nc.tensor.matmul(bank, wl[:, s, k, cut], hi(k), start=False, stop=b)

                s_bank = state["bank"]
                if order == "row":
                    for k in range(nk):
                        marks(k)
                        a = one(0, k)
                        b = one(1, k)
                else:
                    for k in range(nk):
                        a = one(0, k)
                    if stop:
                        a.then_inc(first_tile_done, 1)
                        marks(0)
                    for k in range(nk):
                        b = one(1, k)
                if stop and order == "row":
                    a.then_inc(first_tile_done, 1)
                b.then_inc(chunk_done, 1)

            def claim(s, set_use):
                if not (isinstance(set_use, int) and set_use == 0):
                    pe.wait_ge(evac[s], 2 * set_use)
                state["bank"] = 2 * s

            def mod_tile(m, w, b):
                if not (isinstance(m, int) and m < 2):
                    pe.wait_ge(mod_ready, m - 1)
                for k in range(DT):
                    ins = nc.tensor.matmul(pt[:, 4 + b, 0:2], w(k), cond[:, k, :], start=(k == 0), stop=(k == DT - 1))
                ins.then_inc(mod_used, 1)

            def early_mod(m):
                g = m // 2
                pe.wait_ge(stage_landed[g % STAGE], 16 * (g // STAGE + 1))
                mod_tile(m, lambda k: stage[g % STAGE][:, k, (m % 2) * P:(m % 2 + 1) * P], m % 2)

            def x_tiles(T):
                return (lambda k: xh[:, k, 0:T]), (lambda k: xl[:, k, 0:T])

            def linear_pair(ph, i, T, first, x0, mods):
                hi, lo = x_tiles(T)
                m0 = None if not mods else ph["mod0"] + MODS_PER_PAIR * i
                for s in range(2):
                    pe.wait_ge(lo_ready, 2 * (ph["q"] + i) + s + 1)
                    claim(s, ph["s"] + i)
                    if first:
                        products(s, DT, hi, lo, T, True, True, "row", lambda k: pe.wait_ge(x_ready, x0 + k + 1) if s == 0 else None)
                    else:
                        def between(_, s=s):
                            if mods:
                                late_mod_at(ph, i, 2 * s)
                        products(s, DT, hi, lo, T, True, True, "tile", between)
                        if mods:
                            late_mod_at(ph, i, 2 * s + 1)
                if first and ph["q"] == 0:
                    for m in range(EARLY_NEED, EARLY_MODS):
                        early_mod(m)
                if first and mods:
                    for e in range(MODS_PER_PAIR):
                        late_mod_at(ph, i, e)

            def late_mod_at(ph, i, e):
                m = ph["mod0"] + MODS_PER_PAIR * i + e
                slot = e % 2
                pe.wait_ge(mod_landed[slot], 16 * ((ph["mod0"] - EARLY_MODS) // 2 + 2 * i + e // 2 + 1))
                mod_tile(m, lambda k: modw_slot[:, slot, k, :], slot)

            def turn(dst, src):
                n = src.shape[0]
                return nc.tensor.transpose(dst, src, ident[0:n, 0:n])

            pe.wait_ge(keep_landed, 16)
            pe.wait_ge(rows_landed, 16 * 8)
            turn(pt[:, 4, 0:3 * DT + 1], crows[0:3 * DT + 1, :]).then_inc(turned, 1)
            for L in range(DEPTH):
                turn(pt[:, 5 + L, 0:MODT], brows[0:MODT, L, :]).then_inc(turned, 1)
            pe.wait_ge(xrows_landed, 16 * TT)
            for d in range(DT):
                if d >= 4:
                    pe.wait_ge(h_loaded, d - 3)
                for n in range(TT):
                    ins = turn(pt[:, d % 4, n * P:(n + 1) * P], xrows[:, n, d * P:(d + 1) * P])
                ins.then_inc(turned, 1)
            pe.wait_ge(cond_ready, 3)
            pe.wait_ge(unturned, 2)
            for m in range(EARLY_NEED):
                early_mod(m)
            pe.wait_ge(ones_ready, 1)
            pe.wait_ge(h_loaded, DT)

            for ph in phases:
                kind, q0, s0, T = ph["kind"], ph["q"], ph["s"], ph.get("T")
                if kind in ("norm", "final"):
                    n, T = ph["n"], T or LAT
                    pe.wait_ge(sq_added, 9 * (n + 1))
                    for b in range(T // P):
                        ins = nc.tensor.matmul(pt[:, SUM, b:b + 1], ssq[:, b * P:(b + 1) * P], ones[:, 0:1], start=True, stop=True)
                    ins.then_inc(sum_ready, 1)
                    pe.wait_ge(diag_ready, ph["dg"] + T // P)
                    nc.tensor.matmul(pt[:, BC, 0:T], ones[:], diag[:, 0:T], start=True, stop=True).then_inc(bcast_ready, 1)
                    if kind == "final":
                        for b in range(2):
                            for d in range(DT):
                                e = DT * b + d
                                pe.wait_ge(y_done, d + 1)
                                if e >= 4:
                                    pe.wait_ge(y_copied, e - 3)
                                turn(pt[:, e % 4, 0:P], ylast[:, d, b * P:(b + 1) * P]).then_inc(y_turned, 1)
                elif kind == "up":
                    x0 = ph["x"] - DT
                    linear_pair(ph, 0, T, True, x0, ph["mods"] > 0)
                    if ph["mods"]:
                        with pe.Fori(1, ph["mods"]) as i:
                            linear_pair(ph, i, T, False, x0, True)
                    if ph["mods"] < UP_PAIRS:
                        with pe.Fori(max(1, ph["mods"]), UP_PAIRS) as i:
                            linear_pair(ph, i, T, False, x0, False)
                elif kind in ("diff_qk", "ret_q", "ret_k", "ret_gate"):
                    count, T = {"diff_qk": (4, TOK), "ret_q": (2, LAT), "ret_k": (2, TOK), "ret_gate": (4, LAT)}[kind]
                    fresh = kind in ("diff_qk", "ret_q")
                    if fresh:
                        linear_pair(ph, 0, T, True, ph["x"] - DT, False)
                    with pe.Fori(1 if fresh else 0, count) as i:
                        linear_pair(ph, i, T, False, None, False)
                elif kind in ("diff_v", "ret_v"):
                    diff = kind == "diff_v"
                    per, count, base = (4, 2, 0) if diff else (2, 4, 16)

                    def natural_pair(i, first):
                        for s in range(2):
                            pe.wait_ge(lo_ready, 2 * (q0 + i) + s + 1)
                            claim(s, s0 + i)
                            for n in range(TT):
                                at = pt[:, 2 * s + n // 2, (n % 2) * CW:(n % 2 + 1) * CW]
                                cut = slice(n * P, (n + 1) * P)
                                for k in range(DT):
                                    nc.tensor.matmul(at, xh[:, k, cut], wh[:, s, k, :], start=(k == 0), stop=False)
                                    nc.tensor.matmul(at, xh[:, k, cut], wl[:, s, k, :], start=False, stop=False)
                                    ins = nc.tensor.matmul(at, xl[:, k, cut], wh[:, s, k, :], start=False, stop=(k == DT - 1))
                                if n == 1:
                                    ins.then_inc(first_tile_done, 1)
                            ins.then_inc(chunk_done, 1)
                            if first and s == 0:
                                pe.wait_ge(evac[1], 2 * s0)
                            for e in range(per):
                                r = base + 2 * per * i + per * s + e
                                tile = row(qk, 8 * i + 4 * s + e) if diff else row((qr, kr)[s], 2 * i + e)
                                if not (first and per * s + e < 4):
                                    pe.wait_ge(roped, r - 3)
                                nc.tensor.matmul(pt[:, 4 + (per * s + e) % 4, 0:LAT], swap_d if diff else swap_r,
                                                 tile[:, 0:LAT], start=True, stop=True).then_inc(swapped, 1)

                    natural_pair(0, True)
                    with pe.Fori(1, count) as i:
                        natural_pair(i, False)
                elif kind == "diff_attn":
                    def score(u, b):
                        h, g = u // 2, u % 2
                        nk, k0 = (TOK, 0) if g == 0 else (CTX, LAT)
                        if u:
                            pe.wait_ge(exped, 4 * (u - 1) + 2 * b + 2)
                        for j in range(2):
                            half = slice(j * DD, (j + 1) * DD)
                            ins = nc.tensor.matmul(pt[:, 2 * b + j, 0:nk],
                                                   qk[half, h, g * LAT + b * P:g * LAT + (b + 1) * P],
                                                   qk[half, DH + h, k0:k0 + nk], start=True, stop=True)
                        ins.then_inc(scored, 1)

                    def turn_probs(u, b):
                        k0 = 0 if u % 2 == 0 else TT // 2
                        pe.wait_ge(mixed, 2 * u + b + 1)
                        if u:
                            pe.wait_ge(probs_ready, 2 * (u - 1) + b + 1)
                        for k in range(k0, TT):
                            ins = turn(pt[:, 4 + b, k * P:(k + 1) * P], ex[:, b, 0, (k - k0) * P:(k - k0 + 1) * P])
                        ins.then_inc(probs_turned, 1)

                    def values(u):
                        h, g = u // 2, u % 2
                        k0 = 0 if g == 0 else TT // 2
                        pe.wait_ge(probs_ready, 2 * u + 2)
                        if g == 0 and h:
                            pe.wait_ge(o_copied, h)
                        for k in range(k0, TT):
                            ins = nc.tensor.matmul(pt[:, 6, g * LAT:(g + 1) * LAT], vd[:, k, h * P:(h + 1) * P],
                                                   aTd[:, u % 2, k, :], start=(k == k0), stop=(k == TT - 1))
                        ins.then_inc(pv_done, 1)

                    def sum_head(h):
                        pe.wait_ge(o_squared, h + 1)
                        for b in range(TT):
                            ins = nc.tensor.matmul(pt[:, SUM, TT * h + b:TT * h + b + 1], tmp[:, h % 2, b * P:(b + 1) * P],
                                                   ones[:, 0:1], start=True, stop=True)
                        ins.then_inc(o_summed, 1)

                    for s in range(2):
                        pe.wait_ge(evac[s], 2 * s0)
                    pe.wait_ge(roped, 16)
                    for b in range(2):
                        score(0, b)
                    for u in range(1, 2 * DH + 1):
                        for b in range(2):
                            if u < 2 * DH:
                                score(u, b)
                            turn_probs(u - 1, b)
                        values(u - 1)
                        if u % 2 == 0 and u >= 4:
                            sum_head(u // 2 - 2)
                    sum_head(DH - 1)
                    for h in range(DH):
                        pe.wait_ge(hdiag_ready, TT * (h + 1))
                        if h >= 2:
                            pe.wait_ge(o_scaled, h - 1)
                        nc.tensor.matmul(pt[:, 6 + h % 2, :], ones[:], tmp[:, h % 2, :], start=True, stop=True).then_inc(hbcast_ready, 1)
                elif kind == "ret_attn":
                    def score_r(h):
                        b0 = 2 * (h % 2)
                        if h >= 2:
                            pe.wait_ge(rprobs, h - 1)
                        for k in range(TT):
                            for e in range(2):
                                ins = nc.tensor.matmul(pt[:, b0 + k // 2, (k % 2) * LAT:(k % 2 + 1) * LAT],
                                                       kr[:, 2 * h + e, k * P:(k + 1) * P], qr[:, 2 * h + e, :],
                                                       start=(e == 0), stop=(e == 1))
                        ins.then_inc(rscored, 1)

                    def values_r(h):
                        pe.wait_ge(rprobs, h + 1)
                        if h:
                            pe.wait_ge(rcopied, h)
                        for e in range(4):
                            for k in range(TT):
                                ins = nc.tensor.matmul(pt[:, 4 + e // 2, (e % 2) * LAT:(e % 2 + 1) * LAT],
                                                       vr[:, k, h * RV + e * P:h * RV + (e + 1) * P], aTr[:, h % 2, k, :],
                                                       start=(k == 0), stop=(k == TT - 1))
                        ins.then_inc(rpv, 1)

                    def sum_r(h):
                        pe.wait_ge(rsquared, h + 1)
                        for b in range(2):
                            for e in range(4):
                                at = e * LAT + b * P
                                ins = nc.tensor.matmul(pt[:, SUM, 2 * h + b:2 * h + b + 1],
                                                       tmp[:, at // TOK, at % TOK:at % TOK + P], ones[:, 0:1],
                                                       start=(e == 0), stop=(e == 3))
                        ins.then_inc(rsummed, 1)

                    for s in range(2):
                        pe.wait_ge(evac[s], 2 * s0)
                    pe.wait_ge(roped, 32)
                    score_r(0)
                    for h in range(RH):
                        if h + 1 < RH:
                            score_r(h + 1)
                        values_r(h)
                        if h:
                            sum_r(h - 1)
                    sum_r(RH - 1)
                    for h in range(RH):
                        pe.wait_ge(rdiag, 2 * (h + 1))
                        if h >= 2:
                            pe.wait_ge(rscaled, h - 1)
                        nc.tensor.matmul(pt[:, 6 + h % 2, 0:LAT], ones[:], tmp[:, h % 2, 0:LAT], start=True, stop=True).then_inc(rbcast, 1)
                elif kind == "down":
                    nc_, x0, u0 = len(ph["rows"]), ph["x"], ph["u"]
                    if ph["f"]:
                        hi, lo = (lambda k: uh[:, k, 0:T]), (lambda k: ul[:, k, 0:T])
                    elif ph["L"] == 0:
                        hi, lo = x_tiles(T)
                    else:
                        hi, lo = (lambda k: oh[:, k, :]), (lambda k: ol[:, k, :])
                    ready, upto = (u_ready, u0 - FT) if ph["f"] else (x_ready, x0 - sum(ph["rows"]))
                    with pe.Fori(0, 2) as i:
                        for g in range(2):
                            claim(g, s0 + i)
                            k0 = 0
                            for e, rows_ in enumerate(ph["rows"]):
                                c_ = g * nc_ + e
                                pe.wait_ge(lo_ready, 2 * q0 + 2 * nc_ * i + c_ + 1)
                                last = e == nc_ - 1
                                early = g == 0 and (e == 0 if not ph["f"] else True)
                                h_, l_ = (lambda k, k0=k0: hi(k0 + k)), (lambda k, k0=k0: lo(k0 + k))
                                if c_ == 0 and not ph["f"]:
                                    products(c_ % 2, rows_, h_, l_, T, e == 0, last, "row",
                                             lambda k: pe.wait_ge(ready, upto + k + 1))
                                else:
                                    if g == 0:
                                        pe.wait_ge(ready, upto + k0 + rows_)
                                    products(c_ % 2, rows_, h_, l_, T, e == 0, last, "tile", lambda _: None)
                                k0 += rows_


_INPUTS = ["x", "c", "ctx", "c_ctx", "mod_w", "mod_b", "ffn1_w13", "ffn1_w2", "ffn2_w13", "ffn2_w2",
           "diff_w_in", "diff_w_out", "diff_lambda", "diff_subln_g", "ret_w_in", "ret_w_out", "ret_decay_exp",
           "final_norm_g"]


def kernel(**inputs):
    import concourse.bacc as bacc
    from concourse.bass_utils import run_bass_kernel_spmd

    nc = bacc.Bacc("TRN2", target_bir_lowering=False, num_devices=1)
    arrays, args = {}, []
    for name in _INPUTS:
        a = np.ascontiguousarray(inputs[name])
        arrays[f"in_{name}"] = a
        args.append(nc.dram_tensor(f"in_{name}", a.shape, mybir.dt.from_np(a.dtype), kind="ExternalInput").ap())
    a = shape_constants()
    arrays["shape_constants"] = a
    args.append(nc.dram_tensor("shape_constants", a.shape, F32, kind="ExternalInput").ap())
    out = nc.dram_tensor("latent_out", (1, LAT, D), F32, kind="ExternalOutput").ap()
    trunk(nc, *args, out)
    r = run_bass_kernel_spmd(nc, [arrays], core_ids=[0])
    return r.results[0]["latent_out"]
```

```python
from contextlib import ExitStack

import concourse.bass as bass
from concourse import mybir
import numpy as np

ALU = mybir.AluOpType
ACT = mybir.ActivationFunctionType
AX = mybir.AxisListType
F32 = mybir.dt.float32
F32R = mybir.dt.float32r

P = 128
D = 1024
DT = D // P
LAT = 256
CTX = 256
TOK = LAT + CTX
TT = TOK // P
F = 2816
FT = F // P
DEPTH = 2
N_MOD = 9
MODT = N_MOD * DT
EPS = 1e-6
GRID_W = 64
THETA = 10000.0
CW = 256
W2_ROWS = (6, 5, 6, 5)
UP_PAIRS = F // CW

DH = 8
DD = 64
LAM_INIT = 0.8 - 0.6 * float(np.exp(np.float64(0.0)))
RH = 4
RK = 256
RV = 512

UNITS = DEPTH * MODT // 2
START_UNITS = 2 * DT // 2
START_ORDER = (1, 0, 3, 2, 5, 4, 7, 6)
UNIT_STEPS = 2 * DT
UP_UNITS = 2 * UP_PAIRS - 1
G_STEPS = 18


def rope_rows(n_tokens, head_dim):
    nq = head_dim // 4
    t = np.arange(n_tokens, dtype=np.float32)
    row, col = np.floor(t / GRID_W).astype(np.float32), np.mod(t, GRID_W).astype(np.float32)
    inv = np.float32(THETA) ** (-np.arange(nq, dtype=np.float32) * np.float32(2.0) / np.float32(head_dim // 2))
    cos, sin = [], []
    for pos in (row, col):
        ang = (inv[:, None] * pos[None, :]).astype(np.float32)
        cos += [np.cos(ang), np.cos(ang)]
        sin += [-np.sin(ang), np.sin(ang)]
    return np.concatenate(cos).astype(np.float32), np.concatenate(sin).astype(np.float32)


def swap_rows(half):
    m = np.zeros((P, P), np.float32)
    m[np.arange(P), np.arange(P) ^ half] = 1.0
    return m


def shape_constants():
    dcos, dsin = rope_rows(LAT, DD)
    rcos, rsin = rope_rows(LAT, RK)
    gap = np.arange(LAT, dtype=np.float32)[None, :] - np.arange(P, dtype=np.float32)[:, None]
    parts = [np.eye(P, dtype=np.float32), swap_rows(DD // 4), swap_rows(RK // 4), gap,
             np.tile(dcos, (2, 1)), np.tile(dsin, (2, 1)), rcos[:P], rcos[P:], rsin[:P], rsin[P:]]
    return np.ascontiguousarray(np.concatenate(parts, axis=1))


C_KEEP = 3 * P + LAT
C_DROPE = C_KEEP
C_RROPE = C_DROPE + 2 * LAT
C_ALL = C_RROPE + 4 * LAT


def plan():
    phases = []
    at = dict(q=0, s=0, n=0, x=0, u=0, xh=0, dg=0, unit=START_UNITS)

    def add(kind, q=0, s=0, n=0, x=0, u=0, **kw):
        phases.append(dict(kind=kind, **at, **kw))
        at["unit"] += kw.get("units", 0)
        halves = kw["T"] // LAT if kind == "norm" else 0
        for key, v in dict(q=q, s=s, n=n, x=x, u=u, xh=DT * halves, dg=2 * halves).items():
            at[key] += v

    for L in range(DEPTH):
        last = L == DEPTH - 1
        add("norm", n=1, x=DT, L=L, sub=0, T=TOK)
        add("up", q=UP_PAIRS, s=UP_PAIRS, u=FT, L=L, f=1, T=TOK, units=min(UP_UNITS, UNITS - at["unit"]))
        add("down", q=8, s=2, L=L, f=1, T=TOK, gate=2, half=0.5, rows=W2_ROWS)
        add("norm", n=1, x=DT, L=L, sub=1, T=TOK)
        if L == 0:
            add("diff_qk", q=4, s=4, units=3)
            add("diff_v", q=2, s=2)
            add("diff_attn", x=DH)
            add("down", q=2, s=2, L=L, f=0, T=TOK, gate=5, half=1.0, rows=(8,))
        else:
            add("ret_q", q=2, s=2)
            add("ret_k", q=2, s=2)
            add("ret_v", q=4, s=4)
            add("ret_attn")
            add("ret_gate", q=4, s=4, x=16)
            add("down", q=4, s=2, L=L, f=0, T=LAT, gate=5, half=1.0, rows=(8, 8))
        add("norm", n=1, x=DT, L=L, sub=2, T=LAT if last else TOK)
        add("up", q=UP_PAIRS, s=UP_PAIRS, u=FT, L=L, f=2, T=LAT if last else TOK,
            units=0 if last else UP_UNITS)
        add("down", q=8, s=2, L=L, f=2, T=LAT if last else TOK, gate=8, half=0.5, rows=W2_ROWS)
    add("final", n=1)
    assert at["unit"] == UNITS
    return phases


def row(t, i):
    if isinstance(i, int):
        return t[:, i, :]
    return t[:, bass.ds(i, 1), :].rearrange("p a b -> p (a b)")


def trunk(nc, x, c, ctx_in, c_ctx, mod_w, mod_b, f1_w13, f1_w2, f2_w13, f2_w2, diff_w_in, diff_w_out,
          diff_lambda, diff_subln_g, ret_w_in, ret_w_out, ret_decay_exp, final_norm_g, consts, out):
    phases = plan()
    pairs_total = phases[-1]["q"]

    with ExitStack() as stack:
        def sb(name, shape, dt=F32, where=stack):
            return where.enter_context(nc.sbuf_tensor(name, shape, dt))

        def sem(name):
            return stack.enter_context(nc.semaphore(name))

        hT = sb("hT", [P, DT, TOK])
        xh = sb("xh", [P, DT, TOK], F32R)
        xl = sb("xl", [P, DT, TOK], F32R)
        raw = sb("raw", [P, 2, 8, CW])
        wh = sb("wh", [P, 2, 8, CW], F32R)
        wl = sb("wl", [P, 2, 8, CW], F32R)
        tmp = sb("tmp", [P, 5, TOK])
        keep = sb("keep", [P, C_KEEP])
        ones = sb("ones", [P, P])
        modT = sb("modT", [P, DEPTH * MODT, 2])
        modb = sb("modb", [P, DEPTH * MODT])
        cond = sb("cond", [P, DT, 2])
        gcols = sb("gcols", [P, DT + 1])
        sc1 = sb("sc1", [P, DT, 2])
        gate = sb("gate", [P, DT, 2])
        small = sb("small", [P, 168])
        ident, swap_d, swap_r, gap = keep[:, 0:P], keep[:, P:2 * P], keep[:, 2 * P:3 * P], keep[:, 3 * P:]
        ssq = tmp[:, 4, :]
        diag = tmp[:, 4, :]
        acc = tmp[:, 4, :].rearrange("p (j c) -> p j c", j=2)
        modw = sb("modw", [P, 2 * DT * P])
        modw_slot = modw[:].rearrange("p (s k c) -> p s k c", s=2, k=DT // 2)
        later, earlier, twice = (modw[:, n * 2 * LAT:(n + 1) * 2 * LAT].rearrange("p (k t) -> p k t", k=2)
                                 for n in range(3))

        with ExitStack() as g:
            uh = sb("uh", [P, FT, TOK], F32R, where=g)
            ul = sb("ul", [P, FT, TOK], F32R, where=g)
        with ExitStack() as g:
            oh = sb("oh", [P, 2 * D // P, LAT], F32R, where=g)
            ol = sb("ol", [P, 2 * D // P, LAT], F32R, where=g)
        region = sb("region", [P, 2 * FT * TOK])
        taken = [0]

        def part(*shape, at=None):
            a = taken[0] if at is None else at
            n = int(np.prod(shape))
            taken[0] = a + n
            assert taken[0] <= 2 * FT * TOK
            names = "abcd"[:len(shape)]
            flat = region[:, a:a + n]
            if len(shape) == 1:
                return flat
            return flat.rearrange(f"p ({' '.join(names)}) -> p {' '.join(names)}",
                                  **{k: v for k, v in zip(names[1:], shape[1:])})

        crows = part(P, at=0)
        brows = part(DEPTH, P)
        lamr = part(4, DD)
        lamp = part(2, DD)
        decr = part(2 * RH)
        stage = [part(DT, CW) for _ in range(START_UNITS)]
        start_acc = [part(2, CW) for _ in range(2)]
        xrows = part(TT, D)
        qk = part(2 * DH, TOK, at=0)
        vd = part(TT, D)
        ex = part(2, 2, TOK)
        aTd = part(2, TT, LAT)
        orawd = part(DH, TOK)
        droped = part(2, LAT)
        qr = part(DT, LAT, at=0)
        kr = part(DT, TOK)
        vr = part(TT, 2 * D)
        dec = part(2, TT, LAT)
        aTr = part(2, TT, LAT)
        orawr = part(2 * D // P, LAT)
        rroped = part(2, 2, LAT, at=taken[0] - 4 * LAT)
        ylast = part(DT, LAT, at=0)
        yrows = part(2, D)

        used = [0]

        def cols(n):
            a = used[0]
            used[0] = a + n
            return small[:, a:a + n]

        var, rstd, nhalf = cols(TT), cols(TT), cols(1)
        lam2, lam_e, neglam, subg = cols(2), cols(2), cols(1), cols(1)
        top, shift, mass, share = cols(4), cols(4), cols(4), cols(4)
        hvar, hrstd = cols(DH * TT), cols(DH * TT)
        one_less, left, lgam, nlgam, corr = (cols(2 * RH) for _ in range(5))
        bias_f, bias_b = cols(2 * RH), cols(2 * RH)

        pt = stack.enter_context(nc.psum_tensor("pt", [P, 8, TOK], F32))
        SUM, BC = 7, 6

        raw_landed = [sem("raw_landed0"), sem("raw_landed1")]
        hi_ready = sem("hi_ready")
        lo_ready = sem("lo_ready")
        chunk_done = sem("chunk_done")
        first_tile_done = sem("first_tile_done")
        evac = [sem("evac0"), sem("evac1")]
        u_hi_done, u_ready = sem("u_hi_done"), sem("u_ready")
        x_ready = sem("x_ready")
        x_hi_done = sem("x_hi_done")
        normed, affine = sem("normed"), sem("affine")
        sq_ready, sq_added = sem("sq_ready"), sem("sq_added")
        sum_ready, var_ready, rstd_ready = sem("sum_ready"), sem("var_ready"), sem("rstd_ready")
        diag_ready, bcast_ready = sem("diag_ready"), sem("bcast_ready")
        cols_ready = sem("cols_ready")
        mod_landed = [sem("mod_landed0"), sem("mod_landed1")]
        unit_step = sem("unit_step")
        unit_summed, unit_ready = sem("unit_summed"), sem("unit_ready")
        stage_landed = [sem(f"stage_landed{n}") for n in range(START_UNITS)]
        keep_landed, xrows_landed, rows_landed = sem("keep_landed"), sem("xrows_landed"), sem("rows_landed")
        ones_ready, turned, unturned = sem("ones_ready"), sem("turned"), sem("unturned")
        cond_ready, h_loaded = sem("cond_ready"), sem("h_loaded")
        lam_step, lam_exp = sem("lam_step"), sem("lam_exp")
        rope_landed, swapped, rope_terms, roped = (sem("rope_landed"), sem("swapped"), sem("rope_terms"),
                                                   sem("roped"))
        scored, topped, shifted, exped = sem("scored"), sem("topped"), sem("shifted"), sem("exped")
        share_step, mixed, probs_turned, probs_ready = (sem("share_step"), sem("mixed"), sem("probs_turned"),
                                                        sem("probs_ready"))
        pv_done, o_copied, o_squared, o_summed = sem("pv_done"), sem("o_copied"), sem("o_squared"), sem("o_summed")
        hvar_ready, hrstd_ready, hdiag_ready, hbcast_ready = (sem("hvar_ready"), sem("hrstd_ready"),
                                                              sem("hdiag_ready"), sem("hbcast_ready"))
        o_scaled, o_hi = sem("o_scaled"), sem("o_hi")
        g_step, g_act, expo_ready = sem("g_step"), sem("g_act"), sem("expo_ready")
        dec_sum, dec_exp, dec_done = sem("dec_sum"), sem("dec_exp"), sem("dec_done")
        rscored, rprobs, rpv, rcopied, rsquared, rsummed = (sem("rscored"), sem("rprobs"), sem("rpv"),
                                                            sem("rcopied"), sem("rsquared"), sem("rsummed"))
        rvar, rrstd, rdiag, rbcast, rscaled = sem("rvar"), sem("rrstd"), sem("rdiag"), sem("rbcast"), sem("rscaled")
        gated, gate_hi = sem("gated"), sem("gate_hi")
        y_done, y_turned, y_copied, stored = sem("y_done"), sem("y_turned"), sem("y_copied"), sem("stored")

        w13 = {1: f1_w13, 2: f2_w13}
        w2 = {1: f1_w2, 2: f2_w2}
        unit_v = [mod_w[L].rearrange("(k p) (m c) -> p k m c", p=P, c=CW) for L in range(DEPTH)]
        start_mine = START_UNITS // 2

        def units_of(L, group):
            return (L * MODT + (group + 1) * DT) // 2

        def start_sum(position):
            return pt[:, (4, 5, 0, 1, 2, 3)[position % 6], 0:4]

        block = stack.enter_context(nc.Block())

        @block.sync
        def _(sp):
            def load(n, slot, pair, src, rows=8, first=False):
                if not first:
                    sp.wait_ge(lo_ready, n - 1)
                sp.dma_start(raw[:, slot, 0:rows, :], src).then_inc(raw_landed[slot], 16)

            def column(v, j):
                return v[:, :, j, :] if isinstance(j, int) else v[:, :, bass.ds(j, 1), :].rearrange("p k j c -> p k (j c)")

            sp.dma_start(keep[:], consts[:, 0:C_KEEP]).then_inc(keep_landed, 16)
            for k, src in enumerate((c, c_ctx.rearrange("(a n) -> a n", a=1), final_norm_g.rearrange("(a n) -> a n", a=1))):
                sp.dma_start(crows[k * DT:(k + 1) * DT, :], src.rearrange("a (k p) -> (a k) p", p=P)).then_inc(rows_landed, 16)
            sp.dma_start(crows[3 * DT:3 * DT + 1, :], diff_subln_g).then_inc(rows_landed, 16)
            for L in range(DEPTH):
                sp.dma_start(brows[0:MODT, L, :], mod_b[L].rearrange("(m p) -> m p", p=P)).then_inc(rows_landed, 16)
            for n in range(2):
                sp.dma_start(xrows[:, n, :], x[0, n * P:(n + 1) * P, :]).then_inc(xrows_landed, 16)
                sp.dma_start(xrows[:, 2 + n, :], ctx_in[0, n * P:(n + 1) * P, :]).then_inc(xrows_landed, 16)
            sp.dma_start(lamr, diff_lambda[0].partition_broadcast(P)).then_inc(rows_landed, 16)
            sp.dma_start(decr, ret_decay_exp[0].rearrange("r h -> (r h)").partition_broadcast(P)).then_inc(rows_landed, 16)
            for g in range(START_UNITS):
                sp.dma_start(stage[g], unit_v[0][:, :, g, :]).then_inc(stage_landed[g], 16)

            for ph in phases:
                kind, q0 = ph["kind"], ph["q"]
                if kind == "up":
                    v = w13[ph["f"]][ph["L"]].rearrange("(k p) (a j c) -> a p k j c", p=P, a=2, c=CW)

                    def pair(i, first=False):
                        for s in range(2):
                            load(2 * (q0 + i) + s, s, q0 + i, column(v[s], i), first=first)

                    if q0 == 0:
                        pair(0, first=True)
                    with sp.Fori(0 if q0 else 1, UP_PAIRS) as i:
                        pair(i)
                elif kind == "down":
                    v = (w2[ph["f"]][ph["L"]] if ph["f"] else (diff_w_out if ph["L"] == 0 else ret_w_out)[0]).rearrange(
                        "(k p) (j c) -> p k j c", p=P, c=CW)
                    nc_ = len(ph["rows"])
                    with sp.Fori(0, 2) as i:
                        for g in range(2):
                            k0 = 0
                            for e, rows in enumerate(ph["rows"]):
                                n = g * nc_ + e
                                load(2 * q0 + 2 * nc_ * i + n, n % 2, None, column(v[:, k0:k0 + rows], 2 * i + g), rows)
                                k0 += rows
                elif kind in ("diff_qk", "diff_v", "ret_q", "ret_k", "ret_v", "ret_gate"):
                    w, col0, count = {"diff_qk": (diff_w_in, 0, 4), "diff_v": (diff_w_in, 2 * D, 2),
                                      "ret_q": (ret_w_in, 0, 2), "ret_k": (ret_w_in, D, 2),
                                      "ret_v": (ret_w_in, 2 * D, 4), "ret_gate": (ret_w_in, 4 * D, 4)}[kind]
                    v = w[0][:, col0:col0 + 2 * count * CW].rearrange("(k p) (j c) -> p k j c", p=P, c=CW)
                    if kind == "diff_v":
                        sp.wait_ge(x_ready, ph["x"])
                        sp.dma_start(droped, consts[:, C_DROPE:C_RROPE].rearrange("p (a t) -> p a t", a=2)).then_inc(rope_landed, 16)
                    if kind == "ret_v":
                        sp.wait_ge(x_ready, ph["x"])
                        sp.dma_start(rroped, consts[:, C_RROPE:C_ALL].rearrange("p (a b t) -> p a b t", a=2, b=2)).then_inc(rope_landed, 16)
                    with sp.Fori(0, count) as i:
                        for s in range(2):
                            load(2 * (q0 + i) + s, s, None, column(v, 2 * i + s))
                elif kind == "final":
                    for n in range(2):
                        sp.wait_ge(y_copied, DT * (n + 1))
                        sp.dma_start(out[0, n * P:(n + 1) * P, :], yrows[:, n, :]).then_inc(stored, 16)
                    sp.wait_ge(stored, 32)

        @block.gpsimd
        def _(pool):
            nc.gpsimd.memset(ones[:], 1.0).then_inc(ones_ready, 1)
            nc.gpsimd.memset(nhalf, -0.5).then_inc(ones_ready, 1)

            def clear(n, units=0):
                if n:
                    pool.wait_ge(bcast_ready, n)
                    pool.wait_ge(unit_summed, units)
                nc.gpsimd.memset(ssq, 0.0).then_inc(sq_added, 1)

            def add(count, slot, T):
                nc.gpsimd.tensor_tensor(ssq[:, 0:T], ssq[:, 0:T], tmp[:, slot, 0:T], ALU.add).then_inc(sq_added, 1)

            def power(n, T):
                pool.wait_ge(var_ready, n + 1)
                if n == 0:
                    pool.wait_ge(ones_ready, 2)
                nc.gpsimd.tensor_tensor(rstd[:, 0:T // P], var[:, 0:T // P], nhalf.to_broadcast([P, T // P]),
                                        ALU.pow).then_inc(rstd_ready, 1)

            clear(0)
            for d in range(DT):
                pool.wait_ge(sq_ready, d + 1)
                pool.wait_ge(sq_added, d + 1)
                add(d, d % 2, TOK)
            for ph in phases:
                kind = ph["kind"]
                if kind in ("norm", "final"):
                    power(ph["n"], ph.get("T", LAT))
                if ph.get("units"):
                    u0 = ph["unit"]

                    def fetch(u, e, L):
                        if not (isinstance(u, int) and u == START_UNITS):
                            pool.wait_ge(unit_step, UNIT_STEPS * (u - 1 - start_mine) + UNIT_STEPS // 2 * (e + 1))
                        j = u - L * MODT // 2
                        src = unit_v[L][:, e * DT // 2:(e + 1) * DT // 2]
                        src = src[:, :, j, :] if isinstance(j, int) else src[:, :, bass.ds(j, 1), :].rearrange("p k m c -> p k (m c)")
                        pool.dma_start(modw_slot[:, e], src).then_inc(mod_landed[e], 16)

                    for e in range(2):
                        fetch(u0, e, u0 // (MODT // 2))
                    for L in range(DEPTH):
                        a = max(u0 + 1, L * MODT // 2)
                        b = min(u0 + ph["units"], (L + 1) * MODT // 2)
                        if a < b:
                            with pool.Fori(a, b) as u:
                                for e in range(2):
                                    fetch(u, e, L)
                if kind == "down":
                    n, T = ph["n"], ph["T"]
                    clear(n, ph["unit"])
                    with pool.Fori(0, 2) as i:
                        for b in range(4):
                            pool.wait_ge(sq_ready, DT * n + 4 * i + b + 1)
                            pool.wait_ge(sq_added, 9 * n + 4 * i + b + 1)
                            add(None, b % 2, T)
                elif kind == "diff_attn":
                    pool.wait_ge(hvar_ready, 1)
                    nc.gpsimd.tensor_tensor(hrstd, hvar, nhalf.to_broadcast([P, DH * TT]), ALU.pow).then_inc(hrstd_ready, 1)
                elif kind == "ret_attn":
                    pool.wait_ge(rvar, 1)
                    nc.gpsimd.tensor_tensor(hrstd[:, 0:2 * RH], hvar[:, 0:2 * RH], nhalf.to_broadcast([P, 2 * RH]),
                                            ALU.pow).then_inc(rrstd, 1)

        @block.scalar
        def _(act):
            def split(pair, s, first=False):
                act.wait_ge(raw_landed[s], 16 * (pair + 1))
                if not first:
                    act.wait_ge(chunk_done, 2 * pair + s - 1)
                nc.scalar.copy(wh[:, s], raw[:, s]).then_inc(hi_ready, 1)

            def tile_done(set_use, s, t, n):
                if t == 0:
                    act.wait_ge(first_tile_done, 2 * set_use + s + 1)
                else:
                    act.wait_ge(chunk_done, n + 1)

            def square(n, e, slot, d, T):
                nc.scalar.activation(tmp[:, slot, 0:T], row(hT, d)[:, 0:T], ACT.Square).then_inc(sq_ready, 1)

            act.wait_ge(turned, 1)
            nc.scalar.activation(cond[:, :, 0], pt[:, 4, 0:DT], ACT.Silu).then_inc(cond_ready, 1)
            nc.scalar.activation(cond[:, :, 1], pt[:, 4, DT:2 * DT], ACT.Silu).then_inc(cond_ready, 1)
            nc.scalar.copy(gcols[:], pt[:, 4, 2 * DT:3 * DT + 1]).then_inc(cond_ready, 1)
            for d in range(DT):
                act.wait_ge(h_loaded, d + 1)
                if d >= 2:
                    act.wait_ge(sq_added, d)
                square(0, d, d % 2, d, TOK)
            for s in range(2):
                split(0, s, first=True)

            for ph in phases:
                kind, q0, s0, T = ph["kind"], ph["q"], ph["s"], ph.get("T")
                if kind == "norm":
                    n, x0, m0 = ph["n"], ph["x"], ph["L"] * MODT + 3 * ph["sub"] * DT
                    act.wait_ge(cols_ready, 2 * n + 1)
                    act.wait_ge(unit_ready, units_of(ph["L"], 3 * ph["sub"] + 1))
                    for k in range(DT):
                        act.wait_ge(normed, DT * n + k + 1)
                        for b in range(T // LAT):
                            nc.scalar.activation(xh[:, k, b * LAT:(b + 1) * LAT], tmp[:, k % 2, b * LAT:(b + 1) * LAT],
                                                 ACT.Identity, bias=modT[:, m0 + k, b:b + 1],
                                                 scale=sc1[:, k, b:b + 1]).then_inc(x_hi_done, 1)
                elif kind == "up":
                    def pair(i):
                        for t in range(2):
                            tile_done(s0 + i, 0, t, 2 * (q0 + i))
                            nc.scalar.activation(tmp[:, t, 0:T], pt[:, t, 0:T], ACT.Silu).then_inc(evac[0], 1)
                        split(q0 + i + 1, 0)
                        for t in range(2):
                            act.wait_ge(evac[1], 2 * (s0 + i) + t + 1)
                            nc.scalar.copy(row(uh, 2 * i + t)[:, 0:T], tmp[:, 2 + t, 0:T]).then_inc(u_hi_done, 1)
                        split(q0 + i + 1, 1)

                    pair(0)
                    with act.Fori(1, UP_PAIRS) as i:
                        pair(i)
                elif kind == "down":
                    nc_, n = len(ph["rows"]), ph["n"]

                    def two_tiles(i):
                        for g in range(2):
                            for e in range(nc_):
                                c_ = g * nc_ + e
                                chunk = 2 * q0 + 2 * nc_ * i + c_
                                if e == nc_ - 1:
                                    for t in range(2):
                                        act.wait_ge(evac[g], 2 * (s0 + i) + t + 1)
                                        act.wait_ge(sq_added, 9 * n + 4 * i + 2 * g + t)
                                        square(n, None, t, 4 * i + 2 * g + t, T)
                                pair = q0 + nc_ * i + c_ // 2 + 1
                                if isinstance(pair, int) and pair >= pairs_total:
                                    continue
                                split(pair, c_ % 2)

                    if q0 + 2 * nc_ == pairs_total:
                        for i in range(2):
                            two_tiles(i)
                    else:
                        with act.Fori(0, 2) as i:
                            two_tiles(i)
                elif kind in ("diff_qk", "ret_q", "ret_k"):
                    dst, T = {"diff_qk": (qk, TOK), "ret_q": (qr, LAT), "ret_k": (kr, TOK)}[kind]
                    with act.Fori(0, (2 if kind != "diff_qk" else 4)) as i:
                        for s in range(2):
                            for t in range(2):
                                tile_done(s0 + i, s, t, 2 * (q0 + i) + s)
                                nc.scalar.copy(row(dst, 4 * i + 2 * s + t)[:, 0:T], pt[:, 2 * s + t, 0:T]).then_inc(evac[s], 1)
                            split(q0 + i + 1, s)
                elif kind in ("diff_v", "ret_v"):
                    dst, count = (vd, 2) if kind == "diff_v" else (vr, 4)
                    with act.Fori(0, count) as i:
                        for s in range(2):
                            for b in range(2):
                                tile_done(s0 + i, s, b, 2 * (q0 + i) + s)
                                nc.scalar.copy(dst[:, 2 * b:2 * b + 2, bass.ds((2 * i + s) * CW, CW)],
                                               pt[:, 2 * s + b, :].rearrange("p (a c) -> p a c", a=2)).then_inc(evac[s], 1)
                            split(q0 + i + 1, s)
                elif kind == "diff_attn":
                    act.wait_ge(lam_step, 2)
                    nc.scalar.activation(lam_e, lam2, ACT.Exp).then_inc(lam_exp, 1)

                    def exps(u, b):
                        nk = TOK if u % 2 == 0 else CTX
                        act.wait_ge(shifted, 2 * u + b + 1)
                        if u:
                            act.wait_ge(probs_turned, 2 * (u - 1) + b + 1)
                        for j in range(2):
                            nc.scalar.activation(ex[:, b, j, 0:nk], pt[:, 2 * b + j, 0:nk], ACT.Exp, scale=DD ** -0.5,
                                                 bias=shift[:, 2 * b + j:2 * b + j + 1],
                                                 accum_out=mass[:, 2 * b + j:2 * b + j + 1]).then_inc(exped, 1)

                    def turn_out(u, b):
                        k0, nt = (0, TT) if u % 2 == 0 else (TT // 2, TT // 2)
                        act.wait_ge(probs_turned, 2 * u + b + 1)
                        if u >= 2:
                            act.wait_ge(pv_done, u - 1)
                        nc.scalar.copy(aTd[:, u % 2, k0:k0 + nt, b * P:(b + 1) * P],
                                       pt[:, 4 + b, k0 * P:(k0 + nt) * P].rearrange("p (k c) -> p k c", k=nt)).then_inc(probs_ready, 1)

                    def square_o(h):
                        act.wait_ge(o_copied, h + 1)
                        if h >= 2:
                            act.wait_ge(o_summed, h - 1)
                        nc.scalar.activation(tmp[:, h % 2, :], orawd[:, h, :], ACT.Square).then_inc(o_squared, 1)

                    for u in range(2 * DH + 1):
                        for b in range(2):
                            if u < 2 * DH:
                                exps(u, b)
                            if u:
                                turn_out(u - 1, b)
                        if u and u % 2 == 0:
                            square_o(u // 2 - 1)
                    for h in range(DH):
                        act.wait_ge(o_scaled, h + 1)
                        nc.scalar.copy(xh[:, h, :], tmp[:, 2 + h % 2, :]).then_inc(o_hi, 1)
                elif kind == "ret_attn":
                    def square_r(h):
                        act.wait_ge(rcopied, h + 1)
                        if h:
                            act.wait_ge(rsummed, h)
                        nc.scalar.activation(tmp[:, 0:2, :].rearrange("p a c -> p (a c)"),
                                             orawr[:, 4 * h:4 * h + 4, :].rearrange("p a c -> p (a c)"),
                                             ACT.Square).then_inc(rsquared, 1)

                    act.wait_ge(g_step, 1)
                    y = hvar[:, 0:2 * RH]
                    nc.scalar.activation(y, lgam, ACT.Exp, scale=-float(np.log(2.0))).then_inc(g_act, 1)
                    act.wait_ge(g_step, 3)
                    nc.scalar.activation(lgam, one_less, ACT.Ln).then_inc(g_act, 1)
                    act.wait_ge(g_step, G_STEPS)
                    for h in range(RH):
                        if h >= 2:
                            act.wait_ge(rprobs, h - 1)
                        act.wait_ge(dec_sum, h + 1)
                        nc.scalar.activation(dec[:, h % 2, 0:2], dec[:, h % 2, 0:2], ACT.Exp).then_inc(dec_exp, 1)
                        for k in range(2):
                            nc.scalar.activation(dec[:, h % 2, 2 + k], gap, ACT.Exp, scale=lgam[:, h:h + 1],
                                                 bias=bias_f[:, 2 * h + k:2 * h + k + 1]).then_inc(dec_exp, 1)
                            nc.scalar.activation(tmp[:, 2 + h % 2, k * LAT:(k + 1) * LAT], gap, ACT.Exp,
                                                 scale=nlgam[:, RH + h:RH + h + 1],
                                                 bias=bias_b[:, 2 * h + k:2 * h + k + 1]).then_inc(dec_exp, 1)
                        if h:
                            square_r(h - 1)
                    square_r(RH - 1)
                elif kind == "ret_gate":
                    def gate_pair(i):
                        for s in range(2):
                            for t in range(2):
                                tile_done(s0 + i, s, t, 2 * (q0 + i) + s)
                                nc.scalar.activation(tmp[:, t, 0:LAT], pt[:, 2 * s + t, 0:LAT], ACT.Silu).then_inc(evac[s], 1)
                            for t in range(2):
                                act.wait_ge(gated, 4 * i + 2 * s + t + 1)
                                nc.scalar.copy(row(oh, 4 * i + 2 * s + t), tmp[:, 2 + t, 0:LAT]).then_inc(gate_hi, 1)
                            split(q0 + i + 1, s)

                    gate_pair(0)
                    with act.Fori(1, 4) as i:
                        gate_pair(i)

        @block.vector
        def _(dve):
            def rest(chunk, s):
                dve.wait_ge(hi_ready, chunk + 1)
                nc.vector.tensor_tensor(wl[:, s], raw[:, s], wh[:, s].bitcast(F32), ALU.subtract).then_inc(lo_ready, 1)

            def tile_done(set_use, s, t, n):
                if t == 0:
                    dve.wait_ge(first_tile_done, 2 * set_use + s + 1)
                else:
                    dve.wait_ge(chunk_done, n + 1)

            def unit(u, at, w, landed):
                for k in range(DT):
                    if k % (DT // 2) == 0:
                        dve.wait_ge(*landed(k // (DT // 2)))
                    for j in range(2):
                        if k:
                            dve.wait_ge(unit_step, UNIT_STEPS * u + 2 * k + j - 1)
                            nc.vector.scalar_tensor_tensor(at[:, j], w(k), cond[:, k, j:j + 1], at[:, j],
                                                           ALU.mult, ALU.add).then_inc(unit_step, 1)
                        else:
                            nc.vector.tensor_scalar(at[:, j], w(k), cond[:, k, j:j + 1], None, ALU.mult).then_inc(unit_step, 1)

            def unit_bias(u, position, at):
                dve.wait_ge(unit_summed, position + 1)
                two = slice(2 * u, 2 * u + 2) if isinstance(u, int) else bass.ds(2 * u, 2)
                nc.vector.tensor_tensor(modT[:, two, :], at.rearrange("p (t j) -> p t j", t=2),
                                        modb[:, two].rearrange("p (t j) -> p t j", j=1).broadcast_to([P, 2, 2]),
                                        ALU.add).then_inc(unit_ready, 1)

            def late_unit(u):
                unit(u - start_mine, acc, lambda k: modw_slot[:, k // (DT // 2), k % (DT // 2), :],
                     lambda e: (mod_landed[e], 16 * (u - START_UNITS + 1)))

            def late_bias(u, odd):
                unit_bias(u, u, pt[:, 4 + odd, 0:4])

            def mean(dst, src, width):
                return nc.vector.tensor_scalar(dst, src, 1.0 / width, EPS, ALU.mult, ALU.add)

            def gate_columns(ph):
                L, sub = ph["L"], ph["sub"]
                m0 = L * MODT + (3 * sub + 2) * DT
                dve.wait_ge(unit_ready, units_of(L, 3 * sub + 2))
                if ph["n"]:
                    dve.wait_ge(normed, DT * ph["n"])
                nc.vector.tensor_scalar(gate[:], modT[:, m0:m0 + DT, :], 1.0 if sub == 1 else 0.5, None,
                                        ALU.mult).then_inc(cols_ready, 1)

            dve.wait_ge(turned, 2)
            nc.vector.tensor_copy(modb[:, 0:MODT], pt[:, 5, 0:MODT]).then_inc(unturned, 1)
            dve.wait_ge(turned, 3)
            nc.vector.tensor_copy(modb[:, MODT:2 * MODT], pt[:, 6, 0:MODT]).then_inc(unturned, 1)
            for d in range(DT):
                dve.wait_ge(turned, 4 + d)
                nc.vector.tensor_copy(hT[:, d, :], pt[:, d % 4, :]).then_inc(h_loaded, 1)
            dve.wait_ge(rows_landed, 16 * 8)
            nc.vector.tensor_tensor(lamp, lamr[:, 0:4:2, :], lamr[:, 1:4:2, :], ALU.mult).then_inc(lam_step, 1)
            dve.wait_ge(lam_step, 1)
            nc.vector.tensor_reduce(lam2, lamp, AX.X, ALU.add).then_inc(lam_step, 1)
            nc.vector.tensor_copy(lgam, decr).then_inc(g_step, 1)
            dve.wait_ge(unturned, 2)
            dve.wait_ge(cond_ready, 3)
            for w in range(start_mine):
                if w >= 2:
                    dve.wait_ge(unit_summed, 2 * (w - 2) + 2)
                if w == start_mine - 1:
                    for position in range(2):
                        unit_bias(START_ORDER[position], position, start_sum(position))
                unit(w, start_acc[w % 2], lambda k: stage[2 * w][:, k, :], lambda e: (stage_landed[2 * w], 16))
            for position in range(2, START_UNITS):
                unit_bias(START_ORDER[position], position, start_sum(position))
            for s in range(2):
                rest(s, s)

            for ph in phases:
                kind, q0, s0, T = ph["kind"], ph["q"], ph["s"], ph.get("T")
                if kind in ("norm", "final"):
                    n, T = ph["n"], T or LAT
                    if kind == "norm":
                        L, first = ph["L"], 3 * ph["sub"]
                        m0 = L * MODT + (first + 1) * DT
                        dve.wait_ge(unit_ready, units_of(L, first + 1))
                        nc.vector.tensor_scalar(sc1[:], modT[:, m0:m0 + DT, :], 1.0, None, ALU.add).then_inc(cols_ready, 1)
                    dve.wait_ge(sum_ready, n + 1)
                    mean(var[:, 0:T // P], pt[:, SUM, 0:T // P], D).then_inc(var_ready, 1)
                    dve.wait_ge(rstd_ready, n + 1)
                    for b in range(T // P):
                        nc.vector.tensor_scalar(diag[:, b * P:(b + 1) * P], ident, rstd[:, b:b + 1], None,
                                                ALU.mult).then_inc(diag_ready, 1)
                    dve.wait_ge(bcast_ready, n + 1)
                    if kind == "final":
                        for d in range(DT):
                            nc.vector.scalar_tensor_tensor(ylast[:, d], hT[:, d, 0:LAT], gcols[:, d:d + 1],
                                                           pt[:, BC, 0:LAT], ALU.mult, ALU.mult).then_inc(y_done, 1)
                        for b in range(2):
                            for d in range(DT):
                                e = DT * b + d
                                dve.wait_ge(y_turned, e + 1)
                                nc.vector.tensor_copy(yrows[:, b, d * P:(d + 1) * P], pt[:, e % 4, 0:P]).then_inc(y_copied, 1)
                        continue
                    halves = T // LAT
                    m0 = L * MODT + first * DT
                    dve.wait_ge(cols_ready, 2 * n + 1)

                    def normalise(k):
                        if k >= 2:
                            dve.wait_ge(x_hi_done, ph["xh"] + halves * (k - 1))
                        nc.vector.tensor_tensor(tmp[:, k % 2, 0:T], hT[:, k, 0:T], pt[:, BC, 0:T], ALU.mult).then_inc(normed, 1)

                    normalise(0)
                    for k in range(DT):
                        if k + 1 < DT:
                            normalise(k + 1)
                        dve.wait_ge(normed, DT * n + k + 1)
                        for b in range(halves):
                            cut = slice(b * LAT, (b + 1) * LAT)
                            nc.vector.tensor_scalar(tmp[:, 2 + k % 2, cut], tmp[:, k % 2, cut], sc1[:, k, b:b + 1],
                                                    modT[:, m0 + k, b:b + 1], ALU.mult, ALU.add).then_inc(affine, 1)
                        dve.wait_ge(affine, ph["xh"] + halves * (k + 1))
                        dve.wait_ge(x_hi_done, ph["xh"] + halves * (k + 1))
                        nc.vector.tensor_tensor(xl[:, k, 0:T], tmp[:, 2 + k % 2, 0:T], xh[:, k, 0:T].bitcast(F32),
                                                ALU.subtract).then_inc(x_ready, 1)
                    if units_of(L, first + 2) <= ph["unit"]:
                        gate_columns(ph)
                elif kind == "up":
                    u0 = ph["unit"]

                    def pair(i, units):
                        if units:
                            late_bias(u0 + 2 * i - 2, u0 % 2)
                            late_unit(u0 + 2 * i - 1)
                        rest(2 * (q0 + i + 1), 0)
                        if units:
                            late_bias(u0 + 2 * i - 1, (u0 + 1) % 2)
                            late_unit(u0 + 2 * i)
                        for t in range(2):
                            tile_done(s0 + i, 1, t, 2 * (q0 + i) + 1)
                            dve.wait_ge(evac[0], 2 * (s0 + i) + t + 1)
                            nc.vector.tensor_tensor(tmp[:, 2 + t, 0:T], tmp[:, t, 0:T], pt[:, 2 + t, 0:T],
                                                    ALU.mult).then_inc(evac[1], 1)
                        for t in range(2):
                            dve.wait_ge(u_hi_done, ph["u"] + 2 * i + t + 1)
                            nc.vector.tensor_tensor(row(ul, 2 * i + t)[:, 0:T], tmp[:, 2 + t, 0:T],
                                                    row(uh, 2 * i + t)[:, 0:T].bitcast(F32), ALU.subtract).then_inc(u_ready, 1)
                        rest(2 * (q0 + i + 1) + 1, 1)

                    pair(0, False)
                    if ph["units"]:
                        late_unit(u0)
                    beside = 1 + ph["units"] // 2
                    if beside > 1:
                        with dve.Fori(1, beside) as i:
                            pair(i, True)
                        late_bias(u0 + ph["units"] - 1, u0 % 2)
                    if beside < UP_PAIRS:
                        with dve.Fori(beside, UP_PAIRS) as i:
                            pair(i, False)
                    sub = 0 if ph["f"] == 1 else 2
                    if units_of(ph["L"], 3 * sub + 2) > u0:
                        gate_columns(dict(L=ph["L"], sub=sub, n=ph["n"] - 1))
                elif kind == "down":
                    nc_ = len(ph["rows"])
                    dve.wait_ge(cols_ready, 2 * ph["n"])

                    def two_tiles(i):
                        for g in range(2):
                            for e in range(nc_):
                                c_ = g * nc_ + e
                                chunk = 2 * q0 + 2 * nc_ * i + c_
                                if e == nc_ - 1:
                                    for t in range(2):
                                        tile_done(s0 + i, g, t, chunk)
                                        d = 4 * i + 2 * g + t
                                        for b in range(T // LAT):
                                            cut = slice(b * LAT, (b + 1) * LAT)
                                            ins = nc.vector.scalar_tensor_tensor(
                                                row(hT, d)[:, cut], pt[:, 2 * g + t, cut], row(gate, d)[:, b:b + 1],
                                                row(hT, d)[:, cut], ALU.mult, ALU.add)
                                        ins.then_inc(evac[g], 1)
                                if isinstance(chunk, int) and chunk + 2 >= 2 * pairs_total:
                                    continue
                                rest(chunk + 2, c_ % 2)

                    if q0 + 2 * nc_ == pairs_total:
                        for i in range(2):
                            two_tiles(i)
                    else:
                        with dve.Fori(0, 2) as i:
                            two_tiles(i)
                elif kind == "diff_qk":
                    for i in range(4):
                        rest(2 * (q0 + i + 1), 0)
                        if i < ph["units"]:
                            late_unit(ph["unit"] + i)
                        rest(2 * (q0 + i + 1) + 1, 1)
                        if i < ph["units"]:
                            late_bias(ph["unit"] + i, (ph["unit"] + i) % 2)
                elif kind in ("ret_q", "ret_k"):
                    with dve.Fori(0, 2) as i:
                        for s in range(2):
                            rest(2 * (q0 + i + 1) + s, s)
                elif kind in ("diff_v", "ret_v"):
                    diff = kind == "diff_v"
                    per, count, base = (4, 2, 0) if diff else (2, 4, 16)
                    cos_sin = (lambda t: (droped[:, 0], droped[:, 1])) if diff else (lambda t: (rroped[:, 0, t % 2], rroped[:, 1, t % 2]))

                    def rope(r, bank, tile, table):
                        cos, sin = table
                        dve.wait_ge(swapped, r + 1)
                        nc.vector.tensor_tensor(tmp[:, bank % 2, 0:LAT], pt[:, bank, 0:LAT], sin, ALU.mult).then_inc(rope_terms, 1)
                        nc.vector.tensor_tensor(tile, tile, cos, ALU.mult).then_inc(rope_terms, 1)
                        dve.wait_ge(rope_terms, 2 * r + 2)
                        nc.vector.tensor_tensor(tile, tile, tmp[:, bank % 2, 0:LAT], ALU.add).then_inc(roped, 1)

                    dve.wait_ge(rope_landed, 16 if diff else 32)
                    for s in range(2):
                        dve.wait_ge(evac[s], 2 * s0)
                    with dve.Fori(0, count) as i:
                        for s in range(2):
                            rest(2 * (q0 + i + 1) + s, s)
                            for e in range(per):
                                r = base + 2 * per * i + per * s + e
                                tile = row(qk, 8 * i + 4 * s + e) if diff else row((qr, kr)[s], 2 * i + e)
                                rope(r, 4 + (per * s + e) % 4, tile[:, 0:LAT], cos_sin(e))
                elif kind == "diff_attn":
                    dve.wait_ge(lam_exp, 1)
                    nc.vector.tensor_tensor(neglam, lam_e[:, 1:2], lam_e[:, 0:1], ALU.subtract).then_inc(lam_step, 1)
                    dve.wait_ge(lam_step, 3)
                    nc.vector.tensor_scalar(neglam, neglam, -LAM_INIT, None, ALU.add).then_inc(lam_step, 1)
                    nc.vector.tensor_scalar(subg, gcols[:, DT:DT + 1], 1.0 - LAM_INIT, None, ALU.mult).then_inc(lam_step, 1)
                    dve.wait_ge(lam_step, 5)

                    def row_max(u, b):
                        nk = TOK if u % 2 == 0 else CTX
                        dve.wait_ge(scored, 2 * u + b + 1)
                        nc.vector.tensor_reduce(top[:, 2 * b:2 * b + 2], pt[:, 2 * b:2 * b + 2, 0:nk], AX.X, ALU.max).then_inc(topped, 1)
                        dve.wait_ge(topped, 2 * u + b + 1)
                        nc.vector.tensor_scalar(shift[:, 2 * b:2 * b + 2], top[:, 2 * b:2 * b + 2], -(DD ** -0.5), None,
                                                ALU.mult).then_inc(shifted, 1)

                    def mix(u, b):
                        nk = TOK if u % 2 == 0 else CTX
                        v = 2 * u + b
                        dve.wait_ge(exped, 2 * v + 2)
                        nc.vector.reciprocal(share[:, 2 * b:2 * b + 2], mass[:, 2 * b:2 * b + 2]).then_inc(share_step, 1)
                        dve.wait_ge(share_step, 3 * v + 1)
                        nc.vector.tensor_tensor(share[:, 2 * b + 1:2 * b + 2], share[:, 2 * b + 1:2 * b + 2], neglam,
                                                ALU.mult).then_inc(share_step, 1)
                        nc.vector.tensor_scalar(ex[:, b, 0, 0:nk], ex[:, b, 0, 0:nk], share[:, 2 * b:2 * b + 1], None,
                                                ALU.mult).then_inc(share_step, 1)
                        dve.wait_ge(share_step, 3 * v + 3)
                        nc.vector.scalar_tensor_tensor(ex[:, b, 0, 0:nk], ex[:, b, 1, 0:nk], share[:, 2 * b + 1:2 * b + 2],
                                                       ex[:, b, 0, 0:nk], ALU.mult, ALU.add).then_inc(mixed, 1)

                    def copy_o(h):
                        dve.wait_ge(pv_done, 2 * h + 2)
                        nc.vector.tensor_copy(orawd[:, h, :], pt[:, 6, :]).then_inc(o_copied, 1)

                    row_max(0, 0)
                    row_max(0, 1)
                    for u in range(2 * DH):
                        for b in range(2):
                            mix(u, b)
                            if u + 1 < 2 * DH:
                                row_max(u + 1, b)
                        if u and u % 2 == 0:
                            copy_o(u // 2 - 1)
                    copy_o(DH - 1)
                    dve.wait_ge(o_summed, DH)
                    mean(hvar, pt[:, SUM, 0:DH * TT], P).then_inc(hvar_ready, 1)
                    dve.wait_ge(hrstd_ready, 1)

                    def head_diag(h):
                        if h >= 2:
                            dve.wait_ge(hbcast_ready, h - 1)
                        for b in range(TT):
                            nc.vector.tensor_scalar(tmp[:, h % 2, b * P:(b + 1) * P], ident,
                                                    hrstd[:, TT * h + b:TT * h + b + 1], None, ALU.mult).then_inc(hdiag_ready, 1)

                    head_diag(0)
                    for h in range(DH):
                        if h + 1 < DH:
                            head_diag(h + 1)
                        dve.wait_ge(hbcast_ready, h + 1)
                        nc.vector.scalar_tensor_tensor(tmp[:, 2 + h % 2, :], orawd[:, h, :], subg, pt[:, 6 + h % 2, :],
                                                       ALU.mult, ALU.mult).then_inc(o_scaled, 1)
                        dve.wait_ge(o_hi, h + 1)
                        nc.vector.tensor_tensor(xl[:, h, :], tmp[:, 2 + h % 2, :], xh[:, h, :].bitcast(F32),
                                                ALU.subtract).then_inc(x_ready, 1)
                elif kind == "ret_attn":
                    y = hvar[:, 0:2 * RH]
                    step = [1]

                    def link(ins, wait=True):
                        step[0] += 1
                        ins.then_inc(g_step, 1)
                        if wait:
                            dve.wait_ge(g_step, step[0])

                    dve.wait_ge(g_act, 1)
                    link(nc.vector.tensor_scalar(one_less, y, -1.0, 1.0, ALU.mult, ALU.add))
                    link(nc.vector.tensor_scalar(left, one_less, -1.0, 1.0, ALU.mult, ALU.add))
                    link(nc.vector.tensor_tensor(left, left, y, ALU.subtract), wait=False)
                    link(nc.vector.reciprocal(corr, one_less))
                    link(nc.vector.tensor_tensor(corr, corr, left, ALU.mult))
                    dve.wait_ge(g_act, 2)
                    link(nc.vector.tensor_tensor(lgam, lgam, corr, ALU.add))
                    link(nc.vector.tensor_scalar(nlgam, lgam, -1.0, None, ALU.mult), wait=False)
                    for k in range(2):
                        link(nc.vector.tensor_scalar(bias_f[:, k:2 * RH:2], lgam[:, 0:RH], float(CTX - k * P), None, ALU.mult), wait=False)
                        link(nc.vector.tensor_scalar(bias_b[:, k:2 * RH:2], lgam[:, RH:2 * RH], float(LAT + k * P), None, ALU.mult), wait=False)
                    for k in range(2):
                        link(nc.vector.tensor_scalar(later[:, k], gap, -float(k * P), 0.0, ALU.add, ALU.max), wait=False)
                        link(nc.vector.tensor_scalar(earlier[:, k], gap, -float(k * P), 0.0, ALU.add, ALU.min), wait=False)
                        link(nc.vector.tensor_scalar(twice[:, k], gap, float(k * P), 1.0, ALU.is_equal, ALU.add), wait=False)
                    assert step[0] == G_STEPS
                    dve.wait_ge(g_step, G_STEPS)

                    def decays(h):
                        if h >= 2:
                            dve.wait_ge(rprobs, h - 1)
                        nc.vector.tensor_scalar(dec[:, h % 2, 0:2], earlier, nlgam[:, RH + h:RH + h + 1], None,
                                                ALU.mult).then_inc(expo_ready, 1)
                        dve.wait_ge(expo_ready, h + 1)
                        nc.vector.scalar_tensor_tensor(dec[:, h % 2, 0:2], later, lgam[:, h:h + 1], dec[:, h % 2, 0:2],
                                                       ALU.mult, ALU.add).then_inc(dec_sum, 1)

                    def copy_r(h):
                        dve.wait_ge(rpv, h + 1)
                        nc.vector.tensor_copy(orawr[:, 4 * h:4 * h + 4, :].rearrange("p k t -> p (k t)"),
                                              pt[:, 4:6, :].rearrange("p k t -> p (k t)")).then_inc(rcopied, 1)

                    decays(0)
                    for h in range(RH):
                        if h + 1 < RH:
                            decays(h + 1)
                        dve.wait_ge(dec_exp, 5 * h + 1)
                        nc.vector.tensor_tensor(dec[:, h % 2, 0:2], dec[:, h % 2, 0:2], twice, ALU.mult).then_inc(dec_done, 1)
                        dve.wait_ge(dec_exp, 5 * h + 5)
                        nc.vector.tensor_tensor(dec[:, h % 2, 2:4], dec[:, h % 2, 2:4],
                                                tmp[:, 2 + h % 2, :].rearrange("p (k t) -> p k t", k=2), ALU.add).then_inc(dec_done, 1)
                        dve.wait_ge(dec_done, 2 * h + 2)
                        dve.wait_ge(rscored, h + 1)
                        if h >= 2:
                            dve.wait_ge(rpv, h - 1)
                        nc.vector.scalar_tensor_tensor(aTr[:, h % 2].rearrange("p k t -> p (k t)"),
                                                       pt[:, 2 * (h % 2):2 * (h % 2) + 2, :].rearrange("p k t -> p (k t)"),
                                                       RK ** -0.5, dec[:, h % 2].rearrange("p k t -> p (k t)"),
                                                       ALU.mult, ALU.mult).then_inc(rprobs, 1)
                        if h:
                            copy_r(h - 1)
                    copy_r(RH - 1)
                    dve.wait_ge(rsummed, RH)
                    mean(hvar[:, 0:2 * RH], pt[:, SUM, 0:2 * RH], RV).then_inc(rvar, 1)
                    dve.wait_ge(rrstd, 1)

                    def head_diag(h):
                        if h >= 2:
                            dve.wait_ge(rbcast, h - 1)
                        for b in range(2):
                            nc.vector.tensor_scalar(tmp[:, h % 2, b * P:(b + 1) * P], ident,
                                                    hrstd[:, 2 * h + b:2 * h + b + 1], None, ALU.mult).then_inc(rdiag, 1)

                    head_diag(0)
                    for h in range(RH):
                        if h + 1 < RH:
                            head_diag(h + 1)
                        dve.wait_ge(rbcast, h + 1)
                        nc.vector.tensor_tensor(orawr[:, 4 * h:4 * h + 4, :], orawr[:, 4 * h:4 * h + 4, :],
                                                pt[:, 6 + h % 2:7 + h % 2, 0:LAT].broadcast_to([P, 4, LAT]),
                                                ALU.mult).then_inc(rscaled, 1)
                elif kind == "ret_gate":
                    dve.wait_ge(rscaled, RH)

                    def gate_pair(i):
                        for s in range(2):
                            for t in range(2):
                                dve.wait_ge(evac[s], 2 * (s0 + i) + t + 1)
                                dve.wait_ge(x_ready, ph["x"] + 4 * i + 2 * s + t - 1)
                                nc.vector.tensor_tensor(tmp[:, 2 + t, 0:LAT], tmp[:, t, 0:LAT],
                                                        row(orawr, 4 * i + 2 * s + t), ALU.mult).then_inc(gated, 1)
                            for t in range(2):
                                tile = 4 * i + 2 * s + t
                                dve.wait_ge(gate_hi, tile + 1)
                                nc.vector.tensor_tensor(row(ol, tile), tmp[:, 2 + t, 0:LAT], row(oh, tile).bitcast(F32),
                                                        ALU.subtract).then_inc(x_ready, 1)
                            rest(2 * (q0 + i + 1) + s, s)

                    with dve.Fori(0, 4) as i:
                        gate_pair(i)

        @block.tensor
        def _(pe):
            state = dict()

            def products(s, nk, hi, lo, T, start, stop, order, marks):
                def one(t, k):
                    a, b = start and k == 0, stop and k == nk - 1
                    cut = slice(t * P, (t + 1) * P)
                    bank = pt[:, s_bank + t, 0:T]
                    nc.tensor.matmul(bank, wh[:, s, k, cut], hi(k), start=a, stop=False)
                    nc.tensor.matmul(bank, wh[:, s, k, cut], lo(k), start=False, stop=False)
                    return nc.tensor.matmul(bank, wl[:, s, k, cut], hi(k), start=False, stop=b)

                s_bank = state["bank"]
                if order == "row":
                    for k in range(nk):
                        marks(k)
                        a = one(0, k)
                        b = one(1, k)
                else:
                    for k in range(nk):
                        a = one(0, k)
                    if stop:
                        a.then_inc(first_tile_done, 1)
                        marks(0)
                    for k in range(nk):
                        b = one(1, k)
                if stop and order == "row":
                    a.then_inc(first_tile_done, 1)
                b.then_inc(chunk_done, 1)

            def claim(s, set_use):
                if not (isinstance(set_use, int) and set_use == 0):
                    pe.wait_ge(evac[s], 2 * set_use)
                state["bank"] = 2 * s

            def start_unit(position, u):
                pe.wait_ge(stage_landed[u], 16)
                for t in range(2):
                    for k in range(DT):
                        ins = nc.tensor.matmul(start_sum(position)[:, 2 * t:2 * t + 2], stage[u][:, k, t * P:(t + 1) * P],
                                               cond[:, k, :], start=(k == 0), stop=(k == DT - 1))
                ins.then_inc(unit_summed, 1)

            def sum_unit(w, at, out_):
                pe.wait_ge(unit_step, UNIT_STEPS * (w + 1))
                for t in range(2):
                    for j in range(2):
                        ins = nc.tensor.matmul(out_[:, 2 * t + j:2 * t + j + 1], at[:, j, t * P:(t + 1) * P], ones[:, 0:1],
                                               start=True, stop=True)
                ins.then_inc(unit_summed, 1)

            def sum_late(u, odd):
                pe.wait_ge(unit_ready, u - 1)
                sum_unit(u - start_mine, acc, pt[:, 4 + odd, 0:4])

            def x_tiles(T):
                return (lambda k: xh[:, k, 0:T]), (lambda k: xl[:, k, 0:T])

            def linear_pair(ph, i, T, first, x0, units=()):
                hi, lo = x_tiles(T)
                for s in range(2):
                    pe.wait_ge(lo_ready, 2 * (ph["q"] + i) + s + 1)
                    claim(s, ph["s"] + i)
                    if first:
                        products(s, DT, hi, lo, T, True, True, "row", lambda k: pe.wait_ge(x_ready, x0 + k + 1) if s == 0 else None)
                    else:
                        products(s, DT, hi, lo, T, True, True, "tile",
                                 lambda _: sum_late(*units[s]) if s < len(units) else None)

            def turn(dst, src):
                n = src.shape[0]
                return nc.tensor.transpose(dst, src, ident[0:n, 0:n])

            pe.wait_ge(keep_landed, 16)
            pe.wait_ge(rows_landed, 16 * 8)
            turn(pt[:, 4, 0:3 * DT + 1], crows[0:3 * DT + 1, :]).then_inc(turned, 1)
            for L in range(DEPTH):
                turn(pt[:, 5 + L, 0:MODT], brows[0:MODT, L, :]).then_inc(turned, 1)
            pe.wait_ge(xrows_landed, 16 * TT)
            for d in range(DT):
                if d >= 4:
                    pe.wait_ge(h_loaded, d - 3)
                for n in range(TT):
                    ins = turn(pt[:, d % 4, n * P:(n + 1) * P], xrows[:, n, d * P:(d + 1) * P])
                ins.then_inc(turned, 1)
            pe.wait_ge(cond_ready, 3)
            pe.wait_ge(unturned, 2)
            pe.wait_ge(ones_ready, 1)
            pe.wait_ge(h_loaded, DT)
            for position, u in enumerate(START_ORDER):
                if position >= 6:
                    pe.wait_ge(unit_ready, position - 5)
                if u % 2:
                    start_unit(position, u)
                else:
                    sum_unit(u // 2, start_acc[u // 2 % 2], start_sum(position))
            pe.wait_ge(h_loaded, DT)

            for ph in phases:
                kind, q0, s0, T = ph["kind"], ph["q"], ph["s"], ph.get("T")
                if kind in ("norm", "final"):
                    n, T = ph["n"], T or LAT
                    pe.wait_ge(sq_added, 9 * (n + 1))
                    for b in range(T // P):
                        ins = nc.tensor.matmul(pt[:, SUM, b:b + 1], ssq[:, b * P:(b + 1) * P], ones[:, 0:1], start=True, stop=True)
                    ins.then_inc(sum_ready, 1)
                    pe.wait_ge(diag_ready, ph["dg"] + T // P)
                    nc.tensor.matmul(pt[:, BC, 0:T], ones[:], diag[:, 0:T], start=True, stop=True).then_inc(bcast_ready, 1)
                    if kind == "final":
                        for b in range(2):
                            for d in range(DT):
                                e = DT * b + d
                                pe.wait_ge(y_done, d + 1)
                                if e >= 4:
                                    pe.wait_ge(y_copied, e - 3)
                                turn(pt[:, e % 4, 0:P], ylast[:, d, b * P:(b + 1) * P]).then_inc(y_turned, 1)
                elif kind == "up":
                    x0 = ph["x"] - DT
                    u0 = ph["unit"]
                    linear_pair(ph, 0, T, True, x0)
                    beside = 1 + ph["units"] // 2
                    if beside > 1:
                        with pe.Fori(1, beside) as i:
                            linear_pair(ph, i, T, False, x0, [(u0 + 2 * i - 2, u0 % 2), (u0 + 2 * i - 1, (u0 + 1) % 2)])
                        sum_late(u0 + ph["units"] - 1, u0 % 2)
                    if beside < UP_PAIRS:
                        with pe.Fori(beside, UP_PAIRS) as i:
                            linear_pair(ph, i, T, False, x0)
                elif kind in ("diff_qk", "ret_q", "ret_k", "ret_gate"):
                    count, T = {"diff_qk": (4, TOK), "ret_q": (2, LAT), "ret_k": (2, TOK), "ret_gate": (4, LAT)}[kind]
                    fresh = kind in ("diff_qk", "ret_q")
                    if fresh:
                        linear_pair(ph, 0, T, True, ph["x"] - DT)
                    if kind == "diff_qk":
                        for i in range(1, count):
                            u = ph["unit"] + i - 1
                            linear_pair(ph, i, T, False, None, [(u, u % 2)])
                        pe.wait_ge(unit_ready, ph["unit"] + ph["units"])
                    else:
                        with pe.Fori(1 if fresh else 0, count) as i:
                            linear_pair(ph, i, T, False, None)
                elif kind in ("diff_v", "ret_v"):
                    diff = kind == "diff_v"
                    per, count, base = (4, 2, 0) if diff else (2, 4, 16)

                    def natural_pair(i, first):
                        for s in range(2):
                            pe.wait_ge(lo_ready, 2 * (q0 + i) + s + 1)
                            claim(s, s0 + i)
                            for n in range(TT):
                                at = pt[:, 2 * s + n // 2, (n % 2) * CW:(n % 2 + 1) * CW]
                                cut = slice(n * P, (n + 1) * P)
                                for k in range(DT):
                                    nc.tensor.matmul(at, xh[:, k, cut], wh[:, s, k, :], start=(k == 0), stop=False)
                                    nc.tensor.matmul(at, xh[:, k, cut], wl[:, s, k, :], start=False, stop=False)
                                    ins = nc.tensor.matmul(at, xl[:, k, cut], wh[:, s, k, :], start=False, stop=(k == DT - 1))
                                if n == 1:
                                    ins.then_inc(first_tile_done, 1)
                            ins.then_inc(chunk_done, 1)
                            if first and s == 0:
                                pe.wait_ge(evac[1], 2 * s0)
                            for e in range(per):
                                r = base + 2 * per * i + per * s + e
                                tile = row(qk, 8 * i + 4 * s + e) if diff else row((qr, kr)[s], 2 * i + e)
                                if not (first and per * s + e < 4):
                                    pe.wait_ge(roped, r - 3)
                                nc.tensor.matmul(pt[:, 4 + (per * s + e) % 4, 0:LAT], swap_d if diff else swap_r,
                                                 tile[:, 0:LAT], start=True, stop=True).then_inc(swapped, 1)

                    natural_pair(0, True)
                    with pe.Fori(1, count) as i:
                        natural_pair(i, False)
                elif kind == "diff_attn":
                    def score(u, b):
                        h, g = u // 2, u % 2
                        nk, k0 = (TOK, 0) if g == 0 else (CTX, LAT)
                        if u:
                            pe.wait_ge(exped, 4 * (u - 1) + 2 * b + 2)
                        for j in range(2):
                            half = slice(j * DD, (j + 1) * DD)
                            ins = nc.tensor.matmul(pt[:, 2 * b + j, 0:nk],
                                                   qk[half, h, g * LAT + b * P:g * LAT + (b + 1) * P],
                                                   qk[half, DH + h, k0:k0 + nk], start=True, stop=True)
                        ins.then_inc(scored, 1)

                    def turn_probs(u, b):
                        k0 = 0 if u % 2 == 0 else TT // 2
                        pe.wait_ge(mixed, 2 * u + b + 1)
                        if u:
                            pe.wait_ge(probs_ready, 2 * (u - 1) + b + 1)
                        for k in range(k0, TT):
                            ins = turn(pt[:, 4 + b, k * P:(k + 1) * P], ex[:, b, 0, (k - k0) * P:(k - k0 + 1) * P])
                        ins.then_inc(probs_turned, 1)

                    def values(u):
                        h, g = u // 2, u % 2
                        k0 = 0 if g == 0 else TT // 2
                        pe.wait_ge(probs_ready, 2 * u + 2)
                        if g == 0 and h:
                            pe.wait_ge(o_copied, h)
                        for k in range(k0, TT):
                            ins = nc.tensor.matmul(pt[:, 6, g * LAT:(g + 1) * LAT], vd[:, k, h * P:(h + 1) * P],
                                                   aTd[:, u % 2, k, :], start=(k == k0), stop=(k == TT - 1))
                        ins.then_inc(pv_done, 1)

                    def sum_head(h):
                        pe.wait_ge(o_squared, h + 1)
                        for b in range(TT):
                            ins = nc.tensor.matmul(pt[:, SUM, TT * h + b:TT * h + b + 1], tmp[:, h % 2, b * P:(b + 1) * P],
                                                   ones[:, 0:1], start=True, stop=True)
                        ins.then_inc(o_summed, 1)

                    for s in range(2):
                        pe.wait_ge(evac[s], 2 * s0)
                    pe.wait_ge(roped, 16)
                    for b in range(2):
                        score(0, b)
                    for u in range(1, 2 * DH + 1):
                        for b in range(2):
                            if u < 2 * DH:
                                score(u, b)
                            turn_probs(u - 1, b)
                        values(u - 1)
                        if u % 2 == 0 and u >= 4:
                            sum_head(u // 2 - 2)
                    sum_head(DH - 1)
                    for h in range(DH):
                        pe.wait_ge(hdiag_ready, TT * (h + 1))
                        if h >= 2:
                            pe.wait_ge(o_scaled, h - 1)
                        nc.tensor.matmul(pt[:, 6 + h % 2, :], ones[:], tmp[:, h % 2, :], start=True, stop=True).then_inc(hbcast_ready, 1)
                elif kind == "ret_attn":
                    def score_r(h):
                        b0 = 2 * (h % 2)
                        if h >= 2:
                            pe.wait_ge(rprobs, h - 1)
                        for k in range(TT):
                            for e in range(2):
                                ins = nc.tensor.matmul(pt[:, b0 + k // 2, (k % 2) * LAT:(k % 2 + 1) * LAT],
                                                       kr[:, 2 * h + e, k * P:(k + 1) * P], qr[:, 2 * h + e, :],
                                                       start=(e == 0), stop=(e == 1))
                        ins.then_inc(rscored, 1)

                    def values_r(h):
                        pe.wait_ge(rprobs, h + 1)
                        if h:
                            pe.wait_ge(rcopied, h)
                        for e in range(4):
                            for k in range(TT):
                                ins = nc.tensor.matmul(pt[:, 4 + e // 2, (e % 2) * LAT:(e % 2 + 1) * LAT],
                                                       vr[:, k, h * RV + e * P:h * RV + (e + 1) * P], aTr[:, h % 2, k, :],
                                                       start=(k == 0), stop=(k == TT - 1))
                        ins.then_inc(rpv, 1)

                    def sum_r(h):
                        pe.wait_ge(rsquared, h + 1)
                        for b in range(2):
                            for e in range(4):
                                at = e * LAT + b * P
                                ins = nc.tensor.matmul(pt[:, SUM, 2 * h + b:2 * h + b + 1],
                                                       tmp[:, at // TOK, at % TOK:at % TOK + P], ones[:, 0:1],
                                                       start=(e == 0), stop=(e == 3))
                        ins.then_inc(rsummed, 1)

                    for s in range(2):
                        pe.wait_ge(evac[s], 2 * s0)
                    pe.wait_ge(roped, 32)
                    score_r(0)
                    for h in range(RH):
                        if h + 1 < RH:
                            score_r(h + 1)
                        values_r(h)
                        if h:
                            sum_r(h - 1)
                    sum_r(RH - 1)
                    for h in range(RH):
                        pe.wait_ge(rdiag, 2 * (h + 1))
                        if h >= 2:
                            pe.wait_ge(rscaled, h - 1)
                        nc.tensor.matmul(pt[:, 6 + h % 2, 0:LAT], ones[:], tmp[:, h % 2, 0:LAT], start=True, stop=True).then_inc(rbcast, 1)
                elif kind == "down":
                    nc_, x0, u0 = len(ph["rows"]), ph["x"], ph["u"]
                    if ph["f"]:
                        hi, lo = (lambda k: uh[:, k, 0:T]), (lambda k: ul[:, k, 0:T])
                    elif ph["L"] == 0:
                        hi, lo = x_tiles(T)
                    else:
                        hi, lo = (lambda k: oh[:, k, :]), (lambda k: ol[:, k, :])
                    ready, upto = (u_ready, u0 - FT) if ph["f"] else (x_ready, x0 - sum(ph["rows"]))
                    with pe.Fori(0, 2) as i:
                        for g in range(2):
                            claim(g, s0 + i)
                            k0 = 0
                            for e, rows_ in enumerate(ph["rows"]):
                                c_ = g * nc_ + e
                                pe.wait_ge(lo_ready, 2 * q0 + 2 * nc_ * i + c_ + 1)
                                last = e == nc_ - 1
                                early = g == 0 and (e == 0 if not ph["f"] else True)
                                h_, l_ = (lambda k, k0=k0: hi(k0 + k)), (lambda k, k0=k0: lo(k0 + k))
                                if c_ == 0 and not ph["f"]:
                                    products(c_ % 2, rows_, h_, l_, T, e == 0, last, "row",
                                             lambda k: pe.wait_ge(ready, upto + k + 1))
                                else:
                                    if g == 0:
                                        pe.wait_ge(ready, upto + k0 + rows_)
                                    products(c_ % 2, rows_, h_, l_, T, e == 0, last, "tile", lambda _: None)
                                k0 += rows_


_INPUTS = ["x", "c", "ctx", "c_ctx", "mod_w", "mod_b", "ffn1_w13", "ffn1_w2", "ffn2_w13", "ffn2_w2",
           "diff_w_in", "diff_w_out", "diff_lambda", "diff_subln_g", "ret_w_in", "ret_w_out", "ret_decay_exp",
           "final_norm_g"]


def kernel(**inputs):
    import concourse.bacc as bacc
    from concourse.bass_utils import run_bass_kernel_spmd

    nc = bacc.Bacc("TRN2", target_bir_lowering=False, num_devices=1)
    arrays, args = {}, []
    for name in _INPUTS:
        a = np.ascontiguousarray(inputs[name])
        arrays[f"in_{name}"] = a
        args.append(nc.dram_tensor(f"in_{name}", a.shape, mybir.dt.from_np(a.dtype), kind="ExternalInput").ap())
    a = shape_constants()
    arrays["shape_constants"] = a
    args.append(nc.dram_tensor("shape_constants", a.shape, F32, kind="ExternalInput").ap())
    out = nc.dram_tensor("latent_out", (1, LAT, D), F32, kind="ExternalOutput").ap()
    trunk(nc, *args, out)
    r = run_bass_kernel_spmd(nc, [arrays], core_ids=[0])
    return r.results[0]["latent_out"]
```

```python
from contextlib import ExitStack

import concourse.bass as bass
from concourse import mybir
import numpy as np

ALU = mybir.AluOpType
ACT = mybir.ActivationFunctionType
AX = mybir.AxisListType
F32 = mybir.dt.float32
F32R = mybir.dt.float32r

P = 128
D = 1024
DT = D // P
LAT = 256
CTX = 256
TOK = LAT + CTX
TT = TOK // P
F = 2816
FT = F // P
DEPTH = 2
N_MOD = 9
MODT = N_MOD * DT
EPS = 1e-6
POOLED = 6
GRID_W = 64
THETA = 10000.0
CW = 256
W2_ROWS = (6, 5, 6, 5)
UP_PAIRS = F // CW

DH = 8
DD = 64
LAM_INIT = 0.8 - 0.6 * float(np.exp(np.float64(0.0)))
V = 4 * DH
AT_VALUES, AT_SUM, AT_SPREAD = 6, 9, 11
AT_SQUARE, AT_HI = 7, 12
V_STEPS = 4 * (DH - 1) + AT_HI + 1
RH = 4
RK = 256
RV = 512

UNITS = DEPTH * MODT // 2
START_UNITS = 2 * DT // 2
START_DVE = (0, 3, 6)
START_PE = (("rows", 1), ("norm sums", 0), ("rows", 2), ("columns", 1), ("sum", 0), ("rows", 4), ("columns", 2),
            ("norm spread", 0), ("rows", 5), ("columns", 4), ("sum", 3), ("rows", 7), ("columns", 5), ("sum", 6),
            ("columns", 7))
START_ORDER = [u for step, u in START_PE if step in ("columns", "sum")]
START_EARLY = 2
UNIT_STEPS = 2 * DT
UP_UNITS = 2 * UP_PAIRS - 1
G_STEPS = 18


def rope_rows(n_tokens, head_dim):
    nq = head_dim // 4
    t = np.arange(n_tokens, dtype=np.float32)
    row, col = np.floor(t / GRID_W).astype(np.float32), np.mod(t, GRID_W).astype(np.float32)
    inv = np.float32(THETA) ** (-np.arange(nq, dtype=np.float32) * np.float32(2.0) / np.float32(head_dim // 2))
    cos, sin = [], []
    for pos in (row, col):
        ang = (inv[:, None] * pos[None, :]).astype(np.float32)
        cos += [np.cos(ang), np.cos(ang)]
        sin += [-np.sin(ang), np.sin(ang)]
    return np.concatenate(cos).astype(np.float32), np.concatenate(sin).astype(np.float32)


def swap_rows(half):
    m = np.zeros((P, P), np.float32)
    m[np.arange(P), np.arange(P) ^ half] = 1.0
    return m


def shape_constants():
    dcos, dsin = rope_rows(LAT, DD)
    rcos, rsin = rope_rows(LAT, RK)
    gap = np.arange(LAT, dtype=np.float32)[None, :] - np.arange(P, dtype=np.float32)[:, None]
    parts = [np.eye(P, dtype=np.float32), swap_rows(DD // 4), swap_rows(RK // 4), gap,
             np.tile(dcos, (2, 1)), np.tile(dsin, (2, 1)), rcos[:P], rcos[P:], rsin[:P], rsin[P:]]
    return np.ascontiguousarray(np.concatenate(parts, axis=1))


C_KEEP = 3 * P + LAT
C_DROPE = C_KEEP
C_RROPE = C_DROPE + 2 * LAT
C_ALL = C_RROPE + 4 * LAT


def plan():
    phases = []
    at = dict(q=0, s=0, n=0, x=0, u=0, xh=0, unit=START_UNITS)

    def add(kind, q=0, s=0, n=0, x=0, u=0, **kw):
        phases.append(dict(kind=kind, **at, **kw))
        at["unit"] += kw.get("units", 0)
        halves = kw["T"] // LAT if kind == "norm" else 0
        for key, v in dict(q=q, s=s, n=n, x=x, u=u, xh=DT * halves).items():
            at[key] += v

    for L in range(DEPTH):
        last = L == DEPTH - 1
        add("norm", n=1, x=DT, L=L, sub=0, T=TOK)
        add("up", q=UP_PAIRS, s=UP_PAIRS, u=FT, L=L, f=1, T=TOK, units=min(UP_UNITS, UNITS - at["unit"]))
        add("down", q=8, s=2, L=L, f=1, T=TOK, gate=2, half=0.5, rows=W2_ROWS)
        add("norm", n=1, x=DT, L=L, sub=1, T=TOK)
        if L == 0:
            add("diff_qk", q=4, s=4, units=3)
            add("diff_v", q=2, s=2)
            add("diff_attn", x=DH)
            add("down", q=2, s=2, L=L, f=0, T=TOK, gate=5, half=1.0, rows=(8,))
        else:
            add("ret_q", q=2, s=2)
            add("ret_k", q=2, s=2)
            add("ret_v", q=4, s=4)
            add("ret_attn")
            add("ret_gate", q=4, s=4, x=16)
            add("down", q=4, s=2, L=L, f=0, T=LAT, gate=5, half=1.0, rows=(8, 8))
        add("norm", n=1, x=DT, L=L, sub=2, T=LAT if last else TOK)
        add("up", q=UP_PAIRS, s=UP_PAIRS, u=FT, L=L, f=2, T=LAT if last else TOK,
            units=0 if last else UP_UNITS)
        add("down", q=8, s=2, L=L, f=2, T=LAT if last else TOK, gate=8, half=0.5, rows=W2_ROWS)
    add("final", n=1)
    assert at["unit"] == UNITS
    return phases


def row(t, i):
    if isinstance(i, int):
        return t[:, i, :]
    return t[:, bass.ds(i, 1), :].rearrange("p a b -> p (a b)")


def trunk(nc, x, c, ctx_in, c_ctx, mod_w, mod_b, f1_w13, f1_w2, f2_w13, f2_w2, diff_w_in, diff_w_out,
          diff_lambda, diff_subln_g, ret_w_in, ret_w_out, ret_decay_exp, final_norm_g, consts, out):
    phases = plan()
    pairs_total = phases[-1]["q"]

    with ExitStack() as stack:
        def sb(name, shape, dt=F32, where=stack):
            return where.enter_context(nc.sbuf_tensor(name, shape, dt))

        def sem(name):
            return stack.enter_context(nc.semaphore(name))

        hT = sb("hT", [P, DT, TOK])
        xh = sb("xh", [P, DT, TOK], F32R)
        xl = sb("xl", [P, DT, TOK], F32R)
        raw = sb("raw", [P, 2, 8, CW])
        wh = sb("wh", [P, 2, 8, CW], F32R)
        wl = sb("wl", [P, 2, 8, CW], F32R)
        tmp = sb("tmp", [P, 5, TOK])
        keep = sb("keep", [P, C_KEEP])
        ones = sb("ones", [P, P])
        modT = sb("modT", [P, DEPTH * MODT, 2])
        modb = sb("modb", [P, DEPTH * MODT])
        cond = sb("cond", [P, DT, 2])
        gcols = sb("gcols", [P, DT + 1])
        sc1 = sb("sc1", [P, DT, 2])
        gate = sb("gate", [P, DT, 2])
        small = sb("small", [P, 168])
        ident, swap_d, swap_r, gap = keep[:, 0:P], keep[:, P:2 * P], keep[:, 2 * P:3 * P], keep[:, 3 * P:]
        ssq = tmp[:, 4, :]
        acc = tmp[:, 4, :].rearrange("p (j c) -> p j c", j=2)
        modw = sb("modw", [P, 2 * DT * P])
        modw_slot = modw[:].rearrange("p (s k c) -> p s k c", s=2, k=DT // 2)
        later, earlier, twice = (modw[:, n * 2 * LAT:(n + 1) * 2 * LAT].rearrange("p (k t) -> p k t", k=2)
                                 for n in range(3))

        ex_odd = modw[:].rearrange("p (b j t) -> p b j t", b=2, j=2)

        with ExitStack() as g:
            uh = sb("uh", [P, FT, TOK], F32R, where=g)
            ul = sb("ul", [P, FT, TOK], F32R, where=g)
        with ExitStack() as g:
            oh = sb("oh", [P, 2 * D // P, LAT], F32R, where=g)
            ol = sb("ol", [P, 2 * D // P, LAT], F32R, where=g)
        region = sb("region", [P, 2 * FT * TOK])
        taken = [0]

        def part(*shape, at=None):
            a = taken[0] if at is None else at
            n = int(np.prod(shape))
            taken[0] = a + n
            assert taken[0] <= 2 * FT * TOK
            names = "abcd"[:len(shape)]
            flat = region[:, a:a + n]
            if len(shape) == 1:
                return flat
            return flat.rearrange(f"p ({' '.join(names)}) -> p {' '.join(names)}",
                                  **{k: v for k, v in zip(names[1:], shape[1:])})

        crows = part(P, at=0)
        brows = part(DEPTH, P)
        lamr = part(4, DD)
        lamp = part(2, DD)
        decr = part(2 * RH)
        stage = [part(DT, CW) for _ in range(START_UNITS)]
        start_acc = [part(2, CW) for _ in range(2)]
        xrows = part(TT, D)
        qk = part(2 * DH, TOK, at=0)
        vd = part(TT, D)
        ex_even = part(2, 2, TOK)
        aTd = part(2, TT, LAT)
        orawd = part(DH, TOK)
        droped = part(2, LAT)
        qr = part(DT, LAT, at=0)
        kr = part(DT, TOK)
        vr = part(TT, 2 * D)
        dec = part(2, TT, LAT)
        aTr = part(2, TT, LAT)
        orawr = part(2 * D // P, LAT)
        rroped = part(2, 2, LAT, at=taken[0] - 4 * LAT)
        ylast = part(DT, LAT, at=0)
        yrows = part(2, D)

        used = [0]

        def cols(n):
            a = used[0]
            used[0] = a + n
            return small[:, a:a + n]

        var, rstd, nhalf = cols(TT), cols(TT), cols(1)
        lam2, lam_e, neglam, subg = cols(2), cols(2), cols(1), cols(1)
        top, shift, mass, share = cols(4), cols(4), cols(8), cols(4)
        hvar, hrstd = cols(DH * TT), cols(DH * TT)
        one_less, left, lgam, nlgam, corr = (cols(2 * RH) for _ in range(5))
        bias_f, bias_b = cols(2 * RH), cols(2 * RH)

        pt = stack.enter_context(nc.psum_tensor("pt", [P, 8, TOK], F32))
        SUM, BC = 7, 6

        raw_landed = [sem("raw_landed0"), sem("raw_landed1")]
        hi_ready = sem("hi_ready")
        lo_ready = sem("lo_ready")
        chunk_done = sem("chunk_done")
        first_tile_done = sem("first_tile_done")
        evac = [sem("evac0"), sem("evac1")]
        u_hi_done, u_ready = sem("u_hi_done"), sem("u_ready")
        x_ready = sem("x_ready")
        x_hi_done = sem("x_hi_done")
        normed, affine = sem("normed"), sem("affine")
        sq_ready, sq_added = sem("sq_ready"), sem("sq_added")
        sum_ready, var_ready, rstd_ready = sem("sum_ready"), sem("var_ready"), sem("rstd_ready")
        bcast_ready = sem("bcast_ready")
        cols_ready = sem("cols_ready")
        mod_landed = [sem("mod_landed0"), sem("mod_landed1")]
        unit_step = sem("unit_step")
        rows_made, rows_copied = sem("rows_made"), sem("rows_copied")
        unit_summed, unit_ready = sem("unit_summed"), sem("unit_ready")
        stage_landed = [sem(f"stage_landed{n}") for n in range(START_UNITS)]
        keep_landed, xrows_landed, rows_landed = sem("keep_landed"), sem("xrows_landed"), sem("rows_landed")
        ones_ready, turned, unturned = sem("ones_ready"), sem("turned"), sem("unturned")
        cond_ready, h_loaded = sem("cond_ready"), sem("h_loaded")
        lam_step, lam_exp = sem("lam_step"), sem("lam_exp")
        rope_landed, swapped, rope_terms, roped = (sem("rope_landed"), sem("swapped"), sem("rope_terms"),
                                                   sem("roped"))
        scored, topped, shifted, exped = sem("scored"), sem("topped"), sem("shifted"), sem("exped")
        share_step, mixed, probs_turned, probs_ready = (sem("share_step"), sem("mixed"), sem("probs_turned"),
                                                        sem("probs_ready"))
        pv_done, o_copied, o_squared, o_summed = sem("pv_done"), sem("o_copied"), sem("o_squared"), sem("o_summed")
        hvar_ready, hrstd_ready, hbcast_ready = sem("hvar_ready"), sem("hrstd_ready"), sem("hbcast_ready")
        o_scaled, o_hi = sem("o_scaled"), sem("o_hi")
        g_step, g_act, expo_ready = sem("g_step"), sem("g_act"), sem("expo_ready")
        dec_sum, dec_exp, dec_done = sem("dec_sum"), sem("dec_exp"), sem("dec_done")
        rscored, rprobs, rpv, rcopied, rsquared, rsummed = (sem("rscored"), sem("rprobs"), sem("rpv"),
                                                            sem("rcopied"), sem("rsquared"), sem("rsummed"))
        rvar, rrstd, rdiag, rbcast, rscaled = sem("rvar"), sem("rrstd"), sem("rdiag"), sem("rbcast"), sem("rscaled")
        gated, gate_hi = sem("gated"), sem("gate_hi")
        y_done, y_turned, y_copied, stored = sem("y_done"), sem("y_turned"), sem("y_copied"), sem("stored")

        w13 = {1: f1_w13, 2: f2_w13}
        w2 = {1: f1_w2, 2: f2_w2}
        unit_v = [mod_w[L].rearrange("(k p) (m c) -> p k m c", p=P, c=CW) for L in range(DEPTH)]
        others = START_UNITS - len(START_DVE)

        def units_of(L, group):
            return (L * MODT + (group + 1) * DT) // 2

        def rows_after(ph, i, c_):
            count = len(ph["rows"])
            return ph["rows"][(c_ + 2) % count] if 2 * count * i + c_ + 2 < 4 * count else DT

        def ex(u, b):
            return (ex_even, ex_odd)[u % 2][:, b]

        def masses(u, b):
            at = 4 * (u % 2) + 2 * b
            return mass[:, at:at + 2]

        start_rows = [u for step, u in START_PE if step == "rows"]

        def start_row(u):
            return tmp[0:2, 2 + start_rows.index(u) % 2, 0:CW]

        def start_bank(u):
            return pt[:, u % 6, :]

        def start_sum(u):
            return start_bank(u)[:, 0:4]

        block = stack.enter_context(nc.Block())

        @block.sync
        def _(sp):
            def load(n, slot, pair, src, rows=8, first=False):
                if not first:
                    sp.wait_ge(lo_ready, n - 1)
                sp.dma_start(raw[:, slot, 0:rows, :], src).then_inc(raw_landed[slot], 16)

            def column(v, j):
                return v[:, :, j, :] if isinstance(j, int) else v[:, :, bass.ds(j, 1), :].rearrange("p k j c -> p k (j c)")

            sp.dma_start(keep[:], consts[:, 0:C_KEEP]).then_inc(keep_landed, 16)
            for k, src in enumerate((c, c_ctx.rearrange("(a n) -> a n", a=1), final_norm_g.rearrange("(a n) -> a n", a=1))):
                sp.dma_start(crows[k * DT:(k + 1) * DT, :], src.rearrange("a (k p) -> (a k) p", p=P)).then_inc(rows_landed, 16)
            sp.dma_start(crows[3 * DT:3 * DT + 1, :], diff_subln_g).then_inc(rows_landed, 16)
            for L in range(DEPTH):
                sp.dma_start(brows[0:MODT, L, :], mod_b[L].rearrange("(m p) -> m p", p=P)).then_inc(rows_landed, 16)
            for n in range(2):
                sp.dma_start(xrows[:, n, :], x[0, n * P:(n + 1) * P, :]).then_inc(xrows_landed, 16)
                sp.dma_start(xrows[:, 2 + n, :], ctx_in[0, n * P:(n + 1) * P, :]).then_inc(xrows_landed, 16)
            sp.dma_start(lamr, diff_lambda[0].partition_broadcast(P)).then_inc(rows_landed, 16)
            sp.dma_start(decr, ret_decay_exp[0].rearrange("r h -> (r h)").partition_broadcast(P)).then_inc(rows_landed, 16)
            for g in range(START_UNITS):
                sp.dma_start(stage[g], unit_v[0][:, :, g, :]).then_inc(stage_landed[g], 16)

            for ph in phases:
                kind, q0 = ph["kind"], ph["q"]
                if kind == "up":
                    v = w13[ph["f"]][ph["L"]].rearrange("(k p) (a j c) -> a p k j c", p=P, a=2, c=CW)

                    def pair(i, first=False):
                        for s in range(2):
                            load(2 * (q0 + i) + s, s, q0 + i, column(v[s], i), first=first)

                    if q0 == 0:
                        pair(0, first=True)
                    with sp.Fori(0 if q0 else 1, UP_PAIRS) as i:
                        pair(i)
                elif kind == "down":
                    v = (w2[ph["f"]][ph["L"]] if ph["f"] else (diff_w_out if ph["L"] == 0 else ret_w_out)[0]).rearrange(
                        "(k p) (j c) -> p k j c", p=P, c=CW)
                    nc_ = len(ph["rows"])
                    with sp.Fori(0, 2) as i:
                        for g in range(2):
                            k0 = 0
                            for e, rows in enumerate(ph["rows"]):
                                n = g * nc_ + e
                                load(2 * q0 + 2 * nc_ * i + n, n % 2, None, column(v[:, k0:k0 + rows], 2 * i + g), rows)
                                k0 += rows
                elif kind in ("diff_qk", "diff_v", "ret_q", "ret_k", "ret_v", "ret_gate"):
                    w, col0, count = {"diff_qk": (diff_w_in, 0, 4), "diff_v": (diff_w_in, 2 * D, 2),
                                      "ret_q": (ret_w_in, 0, 2), "ret_k": (ret_w_in, D, 2),
                                      "ret_v": (ret_w_in, 2 * D, 4), "ret_gate": (ret_w_in, 4 * D, 4)}[kind]
                    v = w[0][:, col0:col0 + 2 * count * CW].rearrange("(k p) (j c) -> p k j c", p=P, c=CW)
                    if kind == "diff_v":
                        sp.wait_ge(x_ready, ph["x"])
                        sp.dma_start(droped, consts[:, C_DROPE:C_RROPE].rearrange("p (a t) -> p a t", a=2)).then_inc(rope_landed, 16)
                    if kind == "ret_v":
                        sp.wait_ge(x_ready, ph["x"])
                        sp.dma_start(rroped, consts[:, C_RROPE:C_ALL].rearrange("p (a b t) -> p a b t", a=2, b=2)).then_inc(rope_landed, 16)
                    with sp.Fori(0, count) as i:
                        for s in range(2):
                            load(2 * (q0 + i) + s, s, None, column(v, 2 * i + s))
                elif kind == "final":
                    for n in range(2):
                        sp.wait_ge(y_copied, DT * (n + 1))
                        sp.dma_start(out[0, n * P:(n + 1) * P, :], yrows[:, n, :]).then_inc(stored, 16)
                    sp.wait_ge(stored, 32)

        @block.gpsimd
        def _(pool):
            nc.gpsimd.memset(ones[:], 1.0).then_inc(ones_ready, 1)
            nc.gpsimd.memset(nhalf, -0.5).then_inc(ones_ready, 1)

            def clear(n, units=0):
                if n:
                    pool.wait_ge(sum_ready, n)
                    pool.wait_ge(unit_summed, units)
                nc.gpsimd.memset(ssq, 0.0).then_inc(sq_added, 1)

            def add(n, e, T):
                pool.wait_ge(sq_ready, DT * n + e + 1)
                pool.wait_ge(sq_added, (1 + POOLED) * n + e + 1)
                nc.gpsimd.tensor_tensor(ssq[:, 0:T], ssq[:, 0:T], tmp[:, e % 2, 0:T], ALU.add).then_inc(sq_added, 1)

            clear(0)
            for e in range(POOLED):
                add(0, e, TOK)
            for ph in phases:
                kind = ph["kind"]
                if kind in ("norm", "final"):
                    T = ph.get("T", LAT)
                    pool.wait_ge(var_ready, ph["n"] + 1)
                    if ph["n"] == 0:
                        pool.wait_ge(ones_ready, 2)
                    nc.gpsimd.tensor_tensor(rstd[:, 0:T // P], var[:, 0:T // P], nhalf.to_broadcast([P, T // P]), ALU.pow).then_inc(rstd_ready, 1)
                if kind == "norm":
                    T = ph["T"]
                    for k in range(DT):
                        pool.wait_ge(affine, ph["xh"] + T // LAT * (k + 1))
                        pool.wait_ge(x_hi_done, ph["xh"] + T // LAT * (k + 1))
                        nc.gpsimd.tensor_tensor(xl[:, k, 0:T], tmp[:, 2 + k % 2, 0:T], xh[:, k, 0:T].bitcast(F32),
                                                ALU.subtract).then_inc(x_ready, 1)
                if ph.get("units"):
                    u0 = ph["unit"]

                    def fetch(u, e, L):
                        if not (isinstance(u, int) and u == START_UNITS):
                            pool.wait_ge(unit_step, UNIT_STEPS * (u - 1 - others) + UNIT_STEPS // 2 * (e + 1))
                        j = u - L * MODT // 2
                        src = unit_v[L][:, e * DT // 2:(e + 1) * DT // 2]
                        src = src[:, :, j, :] if isinstance(j, int) else src[:, :, bass.ds(j, 1), :].rearrange("p k m c -> p k (m c)")
                        pool.dma_start(modw_slot[:, e], src).then_inc(mod_landed[e], 16)

                    if kind == "up" and ph["L"] == 0 and ph["f"] == 2:
                        pool.wait_ge(probs_turned, V)
                    for e in range(2):
                        fetch(u0, e, u0 // (MODT // 2))
                    for L in range(DEPTH):
                        a = max(u0 + 1, L * MODT // 2)
                        b = min(u0 + ph["units"], (L + 1) * MODT // 2)
                        if a < b:
                            with pool.Fori(a, b) as u:
                                for e in range(2):
                                    fetch(u, e, L)
                if kind == "down":
                    n, T = ph["n"], ph["T"]
                    clear(n, ph["unit"])
                    for e in range(POOLED):
                        add(n, e, T)
                elif kind == "diff_attn":
                    for h in range(DH):
                        pool.wait_ge(hvar_ready, h + 1)
                        cut = slice(TT * h, TT * (h + 1))
                        nc.gpsimd.tensor_tensor(hrstd[:, cut], hvar[:, cut], nhalf.to_broadcast([P, TT]), ALU.pow).then_inc(hrstd_ready, 1)
                        pool.wait_ge(o_hi, h + 1)
                        nc.gpsimd.tensor_tensor(xl[:, h, :], tmp[:, 2 + h % 2, :], xh[:, h, :].bitcast(F32),
                                                ALU.subtract).then_inc(x_ready, 1)
                elif kind == "ret_attn":
                    pool.wait_ge(rvar, 1)
                    nc.gpsimd.tensor_tensor(hrstd[:, 0:2 * RH], hvar[:, 0:2 * RH], nhalf.to_broadcast([P, 2 * RH]),
                                            ALU.pow).then_inc(rrstd, 1)

        @block.scalar
        def _(act):
            def split(pair, s, first=False, rows=DT):
                act.wait_ge(raw_landed[s], 16 * (pair + 1))
                if not first:
                    act.wait_ge(chunk_done, 2 * pair + s - 1)
                nc.scalar.copy(wh[:, s, 0:rows], raw[:, s, 0:rows]).then_inc(hi_ready, 1)

            def tile_done(set_use, s, t, n):
                if t == 0:
                    act.wait_ge(first_tile_done, 2 * set_use + s + 1)
                else:
                    act.wait_ge(chunk_done, n + 1)

            def square(n, e, slot, d, T):
                nc.scalar.activation(tmp[:, slot, 0:T], row(hT, d)[:, 0:T], ACT.Square).then_inc(sq_ready, 1)

            act.wait_ge(turned, 1)
            nc.scalar.activation(cond[:, :, 0], pt[:, 4, 0:DT], ACT.Silu).then_inc(cond_ready, 1)
            nc.scalar.activation(cond[:, :, 1], pt[:, 4, DT:2 * DT], ACT.Silu).then_inc(cond_ready, 1)
            nc.scalar.copy(gcols[:], pt[:, 4, 2 * DT:3 * DT + 1]).then_inc(cond_ready, 1)
            for d in range(DT):
                act.wait_ge(h_loaded, d + 1)
                if d >= 2:
                    act.wait_ge(sq_added, d)
                square(0, d, d % 2, d, TOK)
            for position, u in enumerate(start_rows):
                act.wait_ge(rows_made, position + 1)
                if position >= 2:
                    act.wait_ge(unit_summed, START_ORDER.index(start_rows[position - 2]) + 1)
                nc.scalar.copy(start_row(u), start_bank(u)[0:2, CW:2 * CW]).then_inc(rows_copied, 1)
            for s in range(2):
                split(0, s, first=True)

            for ph in phases:
                kind, q0, s0, T = ph["kind"], ph["q"], ph["s"], ph.get("T")
                if kind == "norm":
                    n, x0, m0 = ph["n"], ph["x"], ph["L"] * MODT + 3 * ph["sub"] * DT
                    act.wait_ge(cols_ready, 2 * n + 1)
                    act.wait_ge(unit_ready, units_of(ph["L"], 3 * ph["sub"] + 1))
                    for k in range(DT):
                        act.wait_ge(normed, DT * n + k + 1)
                        for b in range(T // LAT):
                            nc.scalar.activation(xh[:, k, b * LAT:(b + 1) * LAT], tmp[:, k % 2, b * LAT:(b + 1) * LAT],
                                                 ACT.Identity, bias=modT[:, m0 + k, b:b + 1],
                                                 scale=sc1[:, k, b:b + 1]).then_inc(x_hi_done, 1)
                elif kind == "up":
                    def pair(i):
                        for t in range(2):
                            tile_done(s0 + i, 0, t, 2 * (q0 + i))
                            nc.scalar.activation(tmp[:, t, 0:T], pt[:, t, 0:T], ACT.Silu).then_inc(evac[0], 1)
                        split(q0 + i + 1, 0)
                        for t in range(2):
                            act.wait_ge(evac[1], 2 * (s0 + i) + t + 1)
                            nc.scalar.copy(row(uh, 2 * i + t)[:, 0:T], tmp[:, 2 + t, 0:T]).then_inc(u_hi_done, 1)
                        split(q0 + i + 1, 1)

                    pair(0)
                    with act.Fori(1, UP_PAIRS) as i:
                        pair(i)
                elif kind == "down":
                    nc_, n = len(ph["rows"]), ph["n"]

                    def two_tiles(i):
                        for g in range(2):
                            for e in range(nc_):
                                c_ = g * nc_ + e
                                chunk = 2 * q0 + 2 * nc_ * i + c_
                                if e == nc_ - 1:
                                    for t in range(2):
                                        act.wait_ge(evac[g], 2 * (s0 + i) + t + 1)
                                        act.wait_ge(sq_added, (1 + POOLED) * n + 4 * i + 2 * g + t)
                                        square(n, None, t, 4 * i + 2 * g + t, T)
                                pair = q0 + nc_ * i + c_ // 2 + 1
                                if pair < pairs_total:
                                    split(pair, c_ % 2, rows=rows_after(ph, i, c_))

                    for i in range(2):
                        two_tiles(i)
                elif kind in ("diff_qk", "ret_q", "ret_k"):
                    dst, T = {"diff_qk": (qk, TOK), "ret_q": (qr, LAT), "ret_k": (kr, TOK)}[kind]
                    with act.Fori(0, (2 if kind != "diff_qk" else 4)) as i:
                        for s in range(2):
                            for t in range(2):
                                tile_done(s0 + i, s, t, 2 * (q0 + i) + s)
                                nc.scalar.copy(row(dst, 4 * i + 2 * s + t)[:, 0:T], pt[:, 2 * s + t, 0:T]).then_inc(evac[s], 1)
                            split(q0 + i + 1, s)
                elif kind in ("diff_v", "ret_v"):
                    dst, count = (vd, 2) if kind == "diff_v" else (vr, 4)
                    with act.Fori(0, count) as i:
                        for s in range(2):
                            for b in range(2):
                                tile_done(s0 + i, s, b, 2 * (q0 + i) + s)
                                nc.scalar.copy(dst[:, 2 * b:2 * b + 2, bass.ds((2 * i + s) * CW, CW)],
                                               pt[:, 2 * s + b, :].rearrange("p (a c) -> p a c", a=2)).then_inc(evac[s], 1)
                            split(q0 + i + 1, s)
                elif kind == "diff_attn":
                    act.wait_ge(lam_step, 2)
                    nc.scalar.activation(lam_e, lam2, ACT.Exp).then_inc(lam_exp, 1)

                    def exps(u, b):
                        nk = TOK if u % 2 == 0 else CTX
                        act.wait_ge(shifted, 2 * u + b + 1)
                        if u >= 2:
                            act.wait_ge(probs_turned, 2 * (u - 2) + b + 1)
                        for j in range(2):
                            nc.scalar.activation(ex(u, b)[:, j, 0:nk], pt[:, 2 * b + j, 0:nk], ACT.Exp, scale=DD ** -0.5,
                                                 bias=shift[:, 2 * b + j:2 * b + j + 1],
                                                 accum_out=masses(u, b)[:, j:j + 1]).then_inc(exped, 1)

                    def turn_out(u, b):
                        k0, nt = (0, TT) if u % 2 == 0 else (TT // 2, TT // 2)
                        act.wait_ge(probs_turned, 2 * u + b + 1)
                        if u >= 2:
                            act.wait_ge(pv_done, u - 1)
                        nc.scalar.copy(aTd[:, u % 2, k0:k0 + nt, b * P:(b + 1) * P],
                                       pt[:, 4 + b, k0 * P:(k0 + nt) * P].rearrange("p (k c) -> p k c", k=nt)).then_inc(probs_ready, 1)

                    def square_o(h):
                        act.wait_ge(o_copied, h + 1)
                        if h >= 2:
                            act.wait_ge(o_summed, h - 1)
                        nc.scalar.activation(tmp[:, h % 2, :], orawd[:, h, :], ACT.Square).then_inc(o_squared, 1)

                    def hi_o(h):
                        act.wait_ge(o_scaled, h + 1)
                        nc.scalar.copy(xh[:, h, :], tmp[:, 2 + h % 2, :]).then_inc(o_hi, 1)

                    for v in range(V_STEPS):
                        if v < V:
                            exps(v // 2, v % 2)
                        if 2 <= v < V + 2:
                            turn_out((v - 2) // 2, v % 2)
                        for at, step in ((AT_SQUARE, square_o), (AT_HI, hi_o)):
                            if at <= v < at + 4 * DH and (v - at) % 4 == 0:
                                step((v - at) // 4)
                elif kind == "ret_attn":
                    def square_r(h):
                        act.wait_ge(rcopied, h + 1)
                        if h:
                            act.wait_ge(rsummed, h)
                        nc.scalar.activation(tmp[:, 0:2, :].rearrange("p a c -> p (a c)"),
                                             orawr[:, 4 * h:4 * h + 4, :].rearrange("p a c -> p (a c)"),
                                             ACT.Square).then_inc(rsquared, 1)

                    act.wait_ge(g_step, 1)
                    y = hvar[:, 0:2 * RH]
                    nc.scalar.activation(y, lgam, ACT.Exp, scale=-float(np.log(2.0))).then_inc(g_act, 1)
                    act.wait_ge(g_step, 3)
                    nc.scalar.activation(lgam, one_less, ACT.Ln).then_inc(g_act, 1)
                    act.wait_ge(g_step, G_STEPS)
                    for h in range(RH):
                        if h >= 2:
                            act.wait_ge(rprobs, h - 1)
                        act.wait_ge(dec_sum, h + 1)
                        nc.scalar.activation(dec[:, h % 2, 0:2], dec[:, h % 2, 0:2], ACT.Exp).then_inc(dec_exp, 1)
                        for k in range(2):
                            nc.scalar.activation(dec[:, h % 2, 2 + k], gap, ACT.Exp, scale=lgam[:, h:h + 1],
                                                 bias=bias_f[:, 2 * h + k:2 * h + k + 1]).then_inc(dec_exp, 1)
                            nc.scalar.activation(tmp[:, 2 + h % 2, k * LAT:(k + 1) * LAT], gap, ACT.Exp,
                                                 scale=nlgam[:, RH + h:RH + h + 1],
                                                 bias=bias_b[:, 2 * h + k:2 * h + k + 1]).then_inc(dec_exp, 1)
                        if h:
                            square_r(h - 1)
                    square_r(RH - 1)
                elif kind == "ret_gate":
                    def gate_pair(i):
                        for s in range(2):
                            for t in range(2):
                                tile_done(s0 + i, s, t, 2 * (q0 + i) + s)
                                nc.scalar.activation(tmp[:, t, 0:LAT], pt[:, 2 * s + t, 0:LAT], ACT.Silu).then_inc(evac[s], 1)
                            for t in range(2):
                                act.wait_ge(gated, 4 * i + 2 * s + t + 1)
                                nc.scalar.copy(row(oh, 4 * i + 2 * s + t), tmp[:, 2 + t, 0:LAT]).then_inc(gate_hi, 1)
                            split(q0 + i + 1, s)

                    gate_pair(0)
                    with act.Fori(1, 4) as i:
                        gate_pair(i)

        @block.vector
        def _(dve):
            def rest(chunk, s, rows=DT):
                dve.wait_ge(hi_ready, chunk + 1)
                nc.vector.tensor_tensor(wl[:, s, 0:rows], raw[:, s, 0:rows], wh[:, s, 0:rows].bitcast(F32),
                                        ALU.subtract).then_inc(lo_ready, 1)

            def tile_done(set_use, s, t, n):
                if t == 0:
                    dve.wait_ge(first_tile_done, 2 * set_use + s + 1)
                else:
                    dve.wait_ge(chunk_done, n + 1)

            def unit(u, at, w, landed):
                for k in range(DT):
                    if k % (DT // 2) == 0:
                        dve.wait_ge(*landed(k // (DT // 2)))
                    for j in range(2):
                        if k:
                            dve.wait_ge(unit_step, UNIT_STEPS * u + 2 * k + j - 1)
                            nc.vector.scalar_tensor_tensor(at[:, j], w(k), cond[:, k, j:j + 1], at[:, j],
                                                           ALU.mult, ALU.add).then_inc(unit_step, 1)
                        else:
                            nc.vector.tensor_scalar(at[:, j], w(k), cond[:, k, j:j + 1], None, ALU.mult).then_inc(unit_step, 1)

            def unit_bias(u, position, at):
                dve.wait_ge(unit_summed, position + 1)
                two = slice(2 * u, 2 * u + 2) if isinstance(u, int) else bass.ds(2 * u, 2)
                nc.vector.tensor_tensor(modT[:, two, :], at.rearrange("p (t j) -> p t j", t=2),
                                        modb[:, two].rearrange("p (t j) -> p t j", j=1).broadcast_to([P, 2, 2]),
                                        ALU.add).then_inc(unit_ready, 1)

            def late_unit(u):
                unit(u - others, acc, lambda k: modw_slot[:, k // (DT // 2), k % (DT // 2), :],
                     lambda e: (mod_landed[e], 16 * (u - START_UNITS + 1)))

            def late_bias(u, odd):
                unit_bias(u, u, pt[:, 4 + odd, 0:4])

            def mean(dst, src, width):
                return nc.vector.tensor_scalar(dst, src, 1.0 / width, EPS, ALU.mult, ALU.add)

            def norm_mean(n, T):
                dve.wait_ge(sum_ready, n + 1)
                blocks = T // P
                if n:
                    mean(var[:, 0:blocks].rearrange("p (b a) -> p b a", a=1), pt[:, 4:4 + blocks, 0:1], D).then_inc(var_ready, 1)
                else:
                    mean(var[:, 0:blocks], pt[:, SUM, 0:blocks], D).then_inc(var_ready, 1)

            def gate_columns(ph):
                L, sub = ph["L"], ph["sub"]
                m0 = L * MODT + (3 * sub + 2) * DT
                dve.wait_ge(unit_ready, units_of(L, 3 * sub + 2))
                if ph["n"]:
                    dve.wait_ge(normed, DT * ph["n"])
                nc.vector.tensor_scalar(gate[:], modT[:, m0:m0 + DT, :], 1.0 if sub == 1 else 0.5, None,
                                        ALU.mult).then_inc(cols_ready, 1)

            dve.wait_ge(turned, 2)
            nc.vector.tensor_copy(modb[:, 0:MODT], pt[:, 5, 0:MODT]).then_inc(unturned, 1)
            dve.wait_ge(turned, 3)
            nc.vector.tensor_copy(modb[:, MODT:2 * MODT], pt[:, 6, 0:MODT]).then_inc(unturned, 1)
            for d in range(DT):
                dve.wait_ge(turned, 4 + d)
                nc.vector.tensor_copy(hT[:, d, :], pt[:, d % 4, :]).then_inc(h_loaded, 1)
            dve.wait_ge(rows_landed, 16 * 8)
            nc.vector.tensor_tensor(lamp, lamr[:, 0:4:2, :], lamr[:, 1:4:2, :], ALU.mult).then_inc(lam_step, 1)
            dve.wait_ge(lam_step, 1)
            nc.vector.tensor_reduce(lam2, lamp, AX.X, ALU.add).then_inc(lam_step, 1)
            nc.vector.tensor_copy(lgam, decr).then_inc(g_step, 1)
            dve.wait_ge(unturned, 2)
            dve.wait_ge(cond_ready, 3)
            for w, u in enumerate(START_DVE):
                if w >= 2:
                    dve.wait_ge(unit_summed, START_ORDER.index(START_DVE[w - 2]) + 1)
                if w == 1:
                    norm_mean(0, TOK)
                if w == len(START_DVE) - 1:
                    for position in range(START_EARLY):
                        unit_bias(START_ORDER[position], position, start_sum(START_ORDER[position]))
                unit(w, start_acc[w % 2], lambda k: stage[u][:, k, :], lambda e: (stage_landed[u], 16))
            rest(0, 0)
            for position in range(START_EARLY, START_UNITS):
                unit_bias(START_ORDER[position], position, start_sum(START_ORDER[position]))

            for ph in phases:
                kind, q0, s0, T = ph["kind"], ph["q"], ph["s"], ph.get("T")
                if kind in ("norm", "final"):
                    n, T = ph["n"], T or LAT
                    if kind == "norm":
                        L, first = ph["L"], 3 * ph["sub"]
                        m0 = L * MODT + (first + 1) * DT
                        dve.wait_ge(unit_ready, units_of(L, first + 1))
                        nc.vector.tensor_scalar(sc1[:], modT[:, m0:m0 + DT, :], 1.0, None, ALU.add).then_inc(cols_ready, 1)
                    if n:
                        norm_mean(n, T)
                    dve.wait_ge(bcast_ready, n + 1)
                    if kind == "final":
                        for d in range(DT):
                            nc.vector.scalar_tensor_tensor(ylast[:, d], hT[:, d, 0:LAT], gcols[:, d:d + 1],
                                                           pt[:, BC, 0:LAT], ALU.mult, ALU.mult).then_inc(y_done, 1)
                        for b in range(2):
                            for d in range(DT):
                                e = DT * b + d
                                dve.wait_ge(y_turned, e + 1)
                                nc.vector.tensor_copy(yrows[:, b, d * P:(d + 1) * P], pt[:, e % 4, 0:P]).then_inc(y_copied, 1)
                        continue
                    halves = T // LAT
                    m0 = L * MODT + first * DT
                    dve.wait_ge(cols_ready, 2 * n + 1)

                    for k in range(DT):
                        if k >= 2:
                            dve.wait_ge(x_hi_done, ph["xh"] + halves * (k - 1))
                        nc.vector.tensor_tensor(tmp[:, k % 2, 0:T], hT[:, k, 0:T], pt[:, BC, 0:T], ALU.mult).then_inc(normed, 1)
                        dve.wait_ge(normed, DT * n + k + 1)
                        if k >= 2:
                            dve.wait_ge(x_ready, ph["x"] + k - 1)
                        for b in range(halves):
                            cut = slice(b * LAT, (b + 1) * LAT)
                            nc.vector.tensor_scalar(tmp[:, 2 + k % 2, cut], tmp[:, k % 2, cut], sc1[:, k, b:b + 1],
                                                    modT[:, m0 + k, b:b + 1], ALU.mult, ALU.add).then_inc(affine, 1)
                    rest(2 * q0 + 1, 1)
                    if units_of(L, first + 2) <= ph["unit"]:
                        gate_columns(ph)
                elif kind == "up":
                    u0 = ph["unit"]

                    def pair(i, units, unit_first=False):
                        if units:
                            late_bias(u0 + 2 * i - 2, u0 % 2)
                            late_unit(u0 + 2 * i - 1)
                        rest(2 * (q0 + i + 1), 0)
                        if units:
                            late_bias(u0 + 2 * i - 1, (u0 + 1) % 2)
                            late_unit(u0 + 2 * i)
                        if unit_first:
                            late_unit(u0)
                        for t in range(2):
                            tile_done(s0 + i, 1, t, 2 * (q0 + i) + 1)
                            dve.wait_ge(evac[0], 2 * (s0 + i) + t + 1)
                            nc.vector.tensor_tensor(tmp[:, 2 + t, 0:T], tmp[:, t, 0:T], pt[:, 2 + t, 0:T],
                                                    ALU.mult).then_inc(evac[1], 1)
                        for t in range(2):
                            dve.wait_ge(u_hi_done, ph["u"] + 2 * i + t + 1)
                            nc.vector.tensor_tensor(row(ul, 2 * i + t)[:, 0:T], tmp[:, 2 + t, 0:T],
                                                    row(uh, 2 * i + t)[:, 0:T].bitcast(F32), ALU.subtract).then_inc(u_ready, 1)
                        rest(2 * (q0 + i + 1) + 1, 1)

                    pair(0, False, unit_first=ph["units"] > 0)
                    beside = 1 + ph["units"] // 2
                    if beside > 1:
                        with dve.Fori(1, beside) as i:
                            pair(i, True)
                        late_bias(u0 + ph["units"] - 1, u0 % 2)
                    if beside < UP_PAIRS:
                        with dve.Fori(beside, UP_PAIRS) as i:
                            pair(i, False)
                    sub = 0 if ph["f"] == 1 else 2
                    if units_of(ph["L"], 3 * sub + 2) > u0:
                        gate_columns(dict(L=ph["L"], sub=sub, n=ph["n"] - 1))
                elif kind == "down":
                    nc_ = len(ph["rows"])
                    dve.wait_ge(cols_ready, 2 * ph["n"])

                    def two_tiles(i):
                        for g in range(2):
                            for e in range(nc_):
                                c_ = g * nc_ + e
                                chunk = 2 * q0 + 2 * nc_ * i + c_
                                if e == nc_ - 1:
                                    for t in range(2):
                                        tile_done(s0 + i, g, t, chunk)
                                        d = 4 * i + 2 * g + t
                                        for b in range(T // LAT):
                                            cut = slice(b * LAT, (b + 1) * LAT)
                                            ins = nc.vector.scalar_tensor_tensor(
                                                row(hT, d)[:, cut], pt[:, 2 * g + t, cut], row(gate, d)[:, b:b + 1],
                                                row(hT, d)[:, cut], ALU.mult, ALU.add)
                                        ins.then_inc(evac[g], 1)
                                if chunk + 2 < 2 * pairs_total and c_ + 2 * nc_ * i < 4 * nc_ - 1:
                                    rest(chunk + 2, c_ % 2, rows=rows_after(ph, i, c_))

                    for i in range(2):
                        two_tiles(i)
                elif kind == "diff_qk":
                    for i in range(4):
                        rest(2 * (q0 + i + 1), 0)
                        if i < ph["units"]:
                            late_unit(ph["unit"] + i)
                        rest(2 * (q0 + i + 1) + 1, 1)
                        if i < ph["units"]:
                            late_bias(ph["unit"] + i, (ph["unit"] + i) % 2)
                elif kind in ("ret_q", "ret_k"):
                    with dve.Fori(0, 2) as i:
                        for s in range(2):
                            rest(2 * (q0 + i + 1) + s, s)
                elif kind in ("diff_v", "ret_v"):
                    diff = kind == "diff_v"
                    per, count, base = (4, 2, 0) if diff else (2, 4, 16)
                    cos_sin = (lambda t: (droped[:, 0], droped[:, 1])) if diff else (lambda t: (rroped[:, 0, t % 2], rroped[:, 1, t % 2]))

                    def rope(r, bank, tile, table):
                        cos, sin = table
                        dve.wait_ge(swapped, r + 1)
                        nc.vector.tensor_tensor(tmp[:, bank % 2, 0:LAT], pt[:, bank, 0:LAT], sin, ALU.mult).then_inc(rope_terms, 1)
                        nc.vector.tensor_tensor(tile, tile, cos, ALU.mult).then_inc(rope_terms, 1)
                        dve.wait_ge(rope_terms, 2 * r + 2)
                        nc.vector.tensor_tensor(tile, tile, tmp[:, bank % 2, 0:LAT], ALU.add).then_inc(roped, 1)

                    dve.wait_ge(rope_landed, 16 if diff else 32)
                    for s in range(2):
                        dve.wait_ge(evac[s], 2 * s0)
                    with dve.Fori(0, count) as i:
                        for s in range(2):
                            for e in range(per):
                                r = base + 2 * per * i + per * s + e
                                tile = row(qk, 8 * i + 4 * s + e) if diff else row((qr, kr)[s], 2 * i + e)
                                rope(r, 4 + (per * s + e) % 4, tile[:, 0:LAT], cos_sin(e))
                            rest(2 * (q0 + i + 1) + s, s)
                elif kind == "diff_attn":
                    dve.wait_ge(lam_exp, 1)
                    nc.vector.tensor_tensor(neglam, lam_e[:, 1:2], lam_e[:, 0:1], ALU.subtract).then_inc(lam_step, 1)
                    dve.wait_ge(lam_step, 3)
                    nc.vector.tensor_scalar(neglam, neglam, -LAM_INIT, None, ALU.add).then_inc(lam_step, 1)
                    nc.vector.tensor_scalar(subg, gcols[:, DT:DT + 1], 1.0 - LAM_INIT, None, ALU.mult).then_inc(lam_step, 1)
                    dve.wait_ge(lam_step, 5)

                    def row_max(u, b):
                        nk = TOK if u % 2 == 0 else CTX
                        dve.wait_ge(scored, 2 * u + b + 1)
                        nc.vector.tensor_reduce(top[:, 2 * b:2 * b + 2], pt[:, 2 * b:2 * b + 2, 0:nk], AX.X, ALU.max).then_inc(topped, 1)
                        dve.wait_ge(topped, 2 * u + b + 1)
                        nc.vector.tensor_scalar(shift[:, 2 * b:2 * b + 2], top[:, 2 * b:2 * b + 2], -(DD ** -0.5), None,
                                                ALU.mult).then_inc(shifted, 1)

                    def mix(u, b):
                        nk = TOK if u % 2 == 0 else CTX
                        v = 2 * u + b
                        dve.wait_ge(exped, 2 * v + 2)
                        nc.vector.reciprocal(share[:, 2 * b:2 * b + 2], masses(u, b)).then_inc(share_step, 1)
                        dve.wait_ge(share_step, 3 * v + 1)
                        nc.vector.tensor_tensor(share[:, 2 * b + 1:2 * b + 2], share[:, 2 * b + 1:2 * b + 2], neglam,
                                                ALU.mult).then_inc(share_step, 1)
                        e = ex(u, b)
                        nc.vector.tensor_scalar(e[:, 0, 0:nk], e[:, 0, 0:nk], share[:, 2 * b:2 * b + 1], None,
                                                ALU.mult).then_inc(share_step, 1)
                        dve.wait_ge(share_step, 3 * v + 3)
                        nc.vector.scalar_tensor_tensor(e[:, 0, 0:nk], e[:, 1, 0:nk], share[:, 2 * b + 1:2 * b + 2],
                                                       e[:, 0, 0:nk], ALU.mult, ALU.add).then_inc(mixed, 1)

                    def copy_o(h):
                        dve.wait_ge(pv_done, 2 * h + 2)
                        nc.vector.tensor_copy(orawd[:, h, :], pt[:, 6, :]).then_inc(o_copied, 1)

                    row_max(0, 0)
                    row_max(0, 1)
                    def mean_o(h):
                        dve.wait_ge(o_summed, h + 1)
                        mean(hvar[:, TT * h:TT * (h + 1)], pt[:, SUM, 0:TT], P).then_inc(hvar_ready, 1)

                    def scale_o(h):
                        dve.wait_ge(hbcast_ready, h + 1)
                        if h >= 2:
                            dve.wait_ge(x_ready, ph["x"] + h - 1)
                        nc.vector.scalar_tensor_tensor(tmp[:, 2 + h % 2, :], orawd[:, h, :], subg, pt[:, SUM, :],
                                                       ALU.mult, ALU.mult).then_inc(o_scaled, 1)

                    for v in range(V_STEPS):
                        if v < V:
                            mix(v // 2, v % 2)
                        for at, step in ((AT_VALUES, copy_o), (AT_SUM, mean_o), (AT_SPREAD, scale_o)):
                            if at <= v + 1 < at + 4 * DH and (v + 1 - at) % 4 == 0:
                                step((v + 1 - at) // 4)
                        if v + 2 < V:
                            row_max(v // 2 + 1, v % 2)
                elif kind == "ret_attn":
                    y = hvar[:, 0:2 * RH]
                    step = [1]

                    def link(ins, wait=True):
                        step[0] += 1
                        ins.then_inc(g_step, 1)
                        if wait:
                            dve.wait_ge(g_step, step[0])

                    dve.wait_ge(g_act, 1)
                    link(nc.vector.tensor_scalar(one_less, y, -1.0, 1.0, ALU.mult, ALU.add))
                    link(nc.vector.tensor_scalar(left, one_less, -1.0, 1.0, ALU.mult, ALU.add))
                    link(nc.vector.tensor_tensor(left, left, y, ALU.subtract), wait=False)
                    link(nc.vector.reciprocal(corr, one_less))
                    link(nc.vector.tensor_tensor(corr, corr, left, ALU.mult))
                    dve.wait_ge(g_act, 2)
                    link(nc.vector.tensor_tensor(lgam, lgam, corr, ALU.add))
                    link(nc.vector.tensor_scalar(nlgam, lgam, -1.0, None, ALU.mult), wait=False)
                    for k in range(2):
                        link(nc.vector.tensor_scalar(bias_f[:, k:2 * RH:2], lgam[:, 0:RH], float(CTX - k * P), None, ALU.mult), wait=False)
                        link(nc.vector.tensor_scalar(bias_b[:, k:2 * RH:2], lgam[:, RH:2 * RH], float(LAT + k * P), None, ALU.mult), wait=False)
                    for k in range(2):
                        link(nc.vector.tensor_scalar(later[:, k], gap, -float(k * P), 0.0, ALU.add, ALU.max), wait=False)
                        link(nc.vector.tensor_scalar(earlier[:, k], gap, -float(k * P), 0.0, ALU.add, ALU.min), wait=False)
                        link(nc.vector.tensor_scalar(twice[:, k], gap, float(k * P), 1.0, ALU.is_equal, ALU.add), wait=False)
                    assert step[0] == G_STEPS
                    dve.wait_ge(g_step, G_STEPS)

                    def decays(h):
                        if h >= 2:
                            dve.wait_ge(rprobs, h - 1)
                        nc.vector.tensor_scalar(dec[:, h % 2, 0:2], earlier, nlgam[:, RH + h:RH + h + 1], None,
                                                ALU.mult).then_inc(expo_ready, 1)
                        dve.wait_ge(expo_ready, h + 1)
                        nc.vector.scalar_tensor_tensor(dec[:, h % 2, 0:2], later, lgam[:, h:h + 1], dec[:, h % 2, 0:2],
                                                       ALU.mult, ALU.add).then_inc(dec_sum, 1)

                    def copy_r(h):
                        dve.wait_ge(rpv, h + 1)
                        nc.vector.tensor_copy(orawr[:, 4 * h:4 * h + 4, :].rearrange("p k t -> p (k t)"),
                                              pt[:, 4:6, :].rearrange("p k t -> p (k t)")).then_inc(rcopied, 1)

                    decays(0)
                    for h in range(RH):
                        if h + 1 < RH:
                            decays(h + 1)
                        dve.wait_ge(dec_exp, 5 * h + 1)
                        nc.vector.tensor_tensor(dec[:, h % 2, 0:2], dec[:, h % 2, 0:2], twice, ALU.mult).then_inc(dec_done, 1)
                        dve.wait_ge(dec_exp, 5 * h + 5)
                        nc.vector.tensor_tensor(dec[:, h % 2, 2:4], dec[:, h % 2, 2:4],
                                                tmp[:, 2 + h % 2, :].rearrange("p (k t) -> p k t", k=2), ALU.add).then_inc(dec_done, 1)
                        dve.wait_ge(dec_done, 2 * h + 2)
                        dve.wait_ge(rscored, h + 1)
                        if h >= 2:
                            dve.wait_ge(rpv, h - 1)
                        nc.vector.scalar_tensor_tensor(aTr[:, h % 2].rearrange("p k t -> p (k t)"),
                                                       pt[:, 2 * (h % 2):2 * (h % 2) + 2, :].rearrange("p k t -> p (k t)"),
                                                       RK ** -0.5, dec[:, h % 2].rearrange("p k t -> p (k t)"),
                                                       ALU.mult, ALU.mult).then_inc(rprobs, 1)
                        if h:
                            copy_r(h - 1)
                    copy_r(RH - 1)
                    dve.wait_ge(rsummed, RH)
                    mean(hvar[:, 0:2 * RH], pt[:, SUM, 0:2 * RH], RV).then_inc(rvar, 1)
                    dve.wait_ge(rrstd, 1)

                    def head_diag(h):
                        if h >= 2:
                            dve.wait_ge(rbcast, h - 1)
                        for b in range(2):
                            nc.vector.tensor_scalar(tmp[:, h % 2, b * P:(b + 1) * P], ident,
                                                    hrstd[:, 2 * h + b:2 * h + b + 1], None, ALU.mult).then_inc(rdiag, 1)

                    head_diag(0)
                    for h in range(RH):
                        if h + 1 < RH:
                            head_diag(h + 1)
                        dve.wait_ge(rbcast, h + 1)
                        nc.vector.tensor_tensor(orawr[:, 4 * h:4 * h + 4, :], orawr[:, 4 * h:4 * h + 4, :],
                                                pt[:, 6 + h % 2:7 + h % 2, 0:LAT].broadcast_to([P, 4, LAT]),
                                                ALU.mult).then_inc(rscaled, 1)
                elif kind == "ret_gate":
                    dve.wait_ge(rscaled, RH)

                    def gate_pair(i):
                        for s in range(2):
                            for t in range(2):
                                dve.wait_ge(evac[s], 2 * (s0 + i) + t + 1)
                                dve.wait_ge(x_ready, ph["x"] + 4 * i + 2 * s + t - 1)
                                nc.vector.tensor_tensor(tmp[:, 2 + t, 0:LAT], tmp[:, t, 0:LAT],
                                                        row(orawr, 4 * i + 2 * s + t), ALU.mult).then_inc(gated, 1)
                            for t in range(2):
                                tile = 4 * i + 2 * s + t
                                dve.wait_ge(gate_hi, tile + 1)
                                nc.vector.tensor_tensor(row(ol, tile), tmp[:, 2 + t, 0:LAT], row(oh, tile).bitcast(F32),
                                                        ALU.subtract).then_inc(x_ready, 1)
                            rest(2 * (q0 + i + 1) + s, s)

                    with dve.Fori(0, 4) as i:
                        gate_pair(i)

        @block.tensor
        def _(pe):
            def products(s, out_set, nk, hi, lo, T, start, stop, between=None, by_row=None):
                def one(t, k, parts):
                    a, b = start and k == 0, stop and k == nk - 1
                    cut = slice(t * P, (t + 1) * P)
                    bank = pt[:, 2 * out_set + t, 0:T]
                    if "hi" in parts:
                        nc.tensor.matmul(bank, wh[:, s, k, cut], hi(k), start=a, stop=False)
                        nc.tensor.matmul(bank, wl[:, s, k, cut], hi(k), start=False, stop=False)
                    if "lo" in parts:
                        return nc.tensor.matmul(bank, wh[:, s, k, cut], lo(k), start=False, stop=b)

                if by_row:
                    for k in range(nk):
                        by_row[0](k)
                        one(0, k, ("hi",))
                        one(1, k, ("hi",))
                        by_row[1](k)
                        a = one(0, k, ("lo",))
                        b = one(1, k, ("lo",))
                    if stop:
                        a.then_inc(first_tile_done, 1)
                else:
                    for k in range(nk):
                        a = one(0, k, ("hi", "lo"))
                    if stop:
                        a.then_inc(first_tile_done, 1)
                    if between:
                        between()
                    for k in range(nk):
                        b = one(1, k, ("hi", "lo"))
                b.then_inc(chunk_done, 1)

            def claim(s, set_use):
                if not (isinstance(set_use, int) and set_use == 0):
                    pe.wait_ge(evac[s], 2 * set_use)

            def unit_rows(u):
                pe.wait_ge(stage_landed[u], 16)
                for k in range(DT):
                    ins = nc.tensor.matmul(start_bank(u)[0:2, CW:2 * CW], cond[:, k, :], stage[u][:, k, :],
                                           start=(k == 0), stop=(k == DT - 1))
                ins.then_inc(rows_made, 1)

            def unit_columns(u):
                pe.wait_ge(rows_copied, start_rows.index(u) + 1)
                for t in range(2):
                    ins = turn(start_sum(u)[:, 2 * t:2 * t + 2], start_row(u)[:, t * P:(t + 1) * P])
                ins.then_inc(unit_summed, 1)

            def sum_unit(w, at, out_):
                pe.wait_ge(unit_step, UNIT_STEPS * (w + 1))
                for t in range(2):
                    for j in range(2):
                        ins = nc.tensor.matmul(out_[:, 2 * t + j:2 * t + j + 1], at[:, j, t * P:(t + 1) * P], ones[:, 0:1],
                                               start=True, stop=True)
                ins.then_inc(unit_summed, 1)

            def sum_late(u, odd):
                pe.wait_ge(unit_ready, u - 1)
                sum_unit(u - others, acc, pt[:, 4 + odd, 0:4])

            def x_tiles(T):
                return (lambda k: xh[:, k, 0:T]), (lambda k: xl[:, k, 0:T])

            def linear_pair(ph, i, T, first, x0, units=()):
                hi, lo = x_tiles(T)
                for s in range(2):
                    pe.wait_ge(lo_ready, 2 * (ph["q"] + i) + s + 1)
                    claim(s, ph["s"] + i)
                    if first and s == 0:
                        xh0 = ph["xh"] - DT * (T // LAT)
                        products(s, s, DT, hi, lo, T, True, True, by_row=(
                            lambda k: pe.wait_ge(x_hi_done, xh0 + T // LAT * (k + 1)),
                            lambda k: pe.wait_ge(x_ready, x0 + k + 1)))
                    else:
                        products(s, s, DT, hi, lo, T, True, True, (lambda: sum_late(*units[s])) if s < len(units) else None)

            def sum_bank(n, b):
                return pt[:, 4 + b, 0:1] if n else pt[:, SUM, b:b + 1]

            def norm_sums(n, T, units=0):
                if units:
                    pe.wait_ge(unit_ready, units)
                pe.wait_ge(sq_added, (1 + POOLED) * (n + 1))
                squares = [ssq] + [tmp[:, e % 2, :] for e in range(POOLED, DT)]
                steps = [(e, b) for e in range(len(squares)) for b in range(T // P)]
                if n == 0:
                    pe.wait_ge(sq_ready, DT)
                    steps.sort(key=lambda step: step[1])
                for e, b in steps:
                    if n and e and b == 0:
                        pe.wait_ge(sq_ready, DT * n + POOLED + e)
                    ins = nc.tensor.matmul(sum_bank(n, b), squares[e][:, b * P:(b + 1) * P], ones[:, 0:1],
                                           start=(e == 0), stop=(e == len(squares) - 1))
                ins.then_inc(sum_ready, 1)

            def norm_spread(n, T):
                pe.wait_ge(rstd_ready, n + 1)
                for b in range(T // P):
                    ins = nc.tensor.matmul(pt[:, BC, b * P:(b + 1) * P], rstd[:, b:b + 1].broadcast_to([P, P]), ident,
                                           start=True, stop=True)
                ins.then_inc(bcast_ready, 1)

            def turn(dst, src):
                n = src.shape[0]
                return nc.tensor.transpose(dst, src, ident[0:n, 0:n])

            pe.wait_ge(keep_landed, 16)
            pe.wait_ge(rows_landed, 16 * 8)
            turn(pt[:, 4, 0:3 * DT + 1], crows[0:3 * DT + 1, :]).then_inc(turned, 1)
            for L in range(DEPTH):
                turn(pt[:, 5 + L, 0:MODT], brows[0:MODT, L, :]).then_inc(turned, 1)
            pe.wait_ge(xrows_landed, 16 * TT)
            for d in range(DT):
                if d >= 4:
                    pe.wait_ge(h_loaded, d - 3)
                for n in range(TT):
                    ins = turn(pt[:, d % 4, n * P:(n + 1) * P], xrows[:, n, d * P:(d + 1) * P])
                ins.then_inc(turned, 1)
            pe.wait_ge(cond_ready, 3)
            pe.wait_ge(unturned, 2)
            pe.wait_ge(ones_ready, 1)
            pe.wait_ge(h_loaded, DT)
            for step, u in START_PE:
                if step == "norm sums":
                    norm_sums(0, TOK)
                elif step == "norm spread":
                    norm_spread(0, TOK)
                elif step == "rows":
                    if u >= 6:
                        pe.wait_ge(unit_ready, START_ORDER.index(u - 6) + 1)
                    unit_rows(u)
                elif step == "columns":
                    unit_columns(u)
                else:
                    if u >= 6:
                        pe.wait_ge(unit_ready, START_ORDER.index(u - 6) + 1)
                    sum_unit(START_DVE.index(u), start_acc[START_DVE.index(u) % 2], start_sum(u))

            for ph in phases:
                kind, q0, s0, T = ph["kind"], ph["q"], ph["s"], ph.get("T")
                if kind in ("norm", "final"):
                    n, T = ph["n"], T or LAT
                    if n:
                        norm_sums(n, T, ph["unit"])
                        norm_spread(n, T)
                    if kind == "final":
                        for b in range(2):
                            for d in range(DT):
                                e = DT * b + d
                                pe.wait_ge(y_done, d + 1)
                                if e >= 4:
                                    pe.wait_ge(y_copied, e - 3)
                                turn(pt[:, e % 4, 0:P], ylast[:, d, b * P:(b + 1) * P]).then_inc(y_turned, 1)
                elif kind == "up":
                    x0 = ph["x"] - DT
                    u0 = ph["unit"]
                    linear_pair(ph, 0, T, True, x0)
                    beside = 1 + ph["units"] // 2
                    if beside > 1:
                        with pe.Fori(1, beside) as i:
                            linear_pair(ph, i, T, False, x0, [(u0 + 2 * i - 2, u0 % 2), (u0 + 2 * i - 1, (u0 + 1) % 2)])
                        sum_late(u0 + ph["units"] - 1, u0 % 2)
                    if beside < UP_PAIRS:
                        with pe.Fori(beside, UP_PAIRS) as i:
                            linear_pair(ph, i, T, False, x0)
                elif kind in ("diff_qk", "ret_q", "ret_k", "ret_gate"):
                    count, T = {"diff_qk": (4, TOK), "ret_q": (2, LAT), "ret_k": (2, TOK), "ret_gate": (4, LAT)}[kind]
                    fresh = kind in ("diff_qk", "ret_q")
                    if fresh:
                        linear_pair(ph, 0, T, True, ph["x"] - DT)
                    if kind == "diff_qk":
                        for i in range(1, count):
                            u = ph["unit"] + i - 1
                            linear_pair(ph, i, T, False, None, [(u, u % 2)])
                        pe.wait_ge(unit_ready, ph["unit"] + ph["units"])
                    else:
                        with pe.Fori(1 if fresh else 0, count) as i:
                            linear_pair(ph, i, T, False, None)
                elif kind in ("diff_v", "ret_v"):
                    diff = kind == "diff_v"
                    per, count, base = (4, 2, 0) if diff else (2, 4, 16)

                    def natural_pair(i, first):
                        for s in range(2):
                            pe.wait_ge(lo_ready, 2 * (q0 + i) + s + 1)
                            claim(s, s0 + i)
                            for e in range(per):
                                r = base + 2 * per * i + per * s + e
                                tile = row(qk, 8 * i + 4 * s + e) if diff else row((qr, kr)[s], 2 * i + e)
                                if not (first and per * s + e < 4):
                                    pe.wait_ge(roped, r - 3)
                                nc.tensor.matmul(pt[:, 4 + (per * s + e) % 4, 0:LAT], swap_d if diff else swap_r,
                                                 tile[:, 0:LAT], start=True, stop=True).then_inc(swapped, 1)
                            for n in range(TT):
                                at = pt[:, 2 * s + n // 2, (n % 2) * CW:(n % 2 + 1) * CW]
                                cut = slice(n * P, (n + 1) * P)
                                for k in range(DT):
                                    nc.tensor.matmul(at, xh[:, k, cut], wh[:, s, k, :], start=(k == 0), stop=False)
                                    nc.tensor.matmul(at, xh[:, k, cut], wl[:, s, k, :], start=False, stop=False)
                                    ins = nc.tensor.matmul(at, xl[:, k, cut], wh[:, s, k, :], start=False, stop=(k == DT - 1))
                                if n == 1:
                                    ins.then_inc(first_tile_done, 1)
                            ins.then_inc(chunk_done, 1)

                    natural_pair(0, True)
                    with pe.Fori(1, count) as i:
                        natural_pair(i, False)
                elif kind == "diff_attn":
                    def score(u, b):
                        h, g = u // 2, u % 2
                        nk, k0 = (TOK, 0) if g == 0 else (CTX, LAT)
                        if u:
                            pe.wait_ge(exped, 4 * (u - 1) + 2 * b + 2)
                        for j in range(2):
                            half = slice(j * DD, (j + 1) * DD)
                            ins = nc.tensor.matmul(pt[:, 2 * b + j, 0:nk],
                                                   qk[half, h, g * LAT + b * P:g * LAT + (b + 1) * P],
                                                   qk[half, DH + h, k0:k0 + nk], start=True, stop=True)
                        ins.then_inc(scored, 1)

                    def turn_probs(u, b):
                        k0 = 0 if u % 2 == 0 else TT // 2
                        pe.wait_ge(mixed, 2 * u + b + 1)
                        if u:
                            pe.wait_ge(probs_ready, 2 * (u - 1) + b + 1)
                        for k in range(k0, TT):
                            ins = turn(pt[:, 4 + b, k * P:(k + 1) * P], ex(u, b)[:, 0, (k - k0) * P:(k - k0 + 1) * P])
                        ins.then_inc(probs_turned, 1)

                    def values(u):
                        h, g = u // 2, u % 2
                        k0 = 0 if g == 0 else TT // 2
                        pe.wait_ge(probs_ready, 2 * u + 2)
                        if g == 0 and h:
                            pe.wait_ge(o_copied, h)
                        for k in range(k0, TT):
                            ins = nc.tensor.matmul(pt[:, 6, g * LAT:(g + 1) * LAT], vd[:, k, h * P:(h + 1) * P],
                                                   aTd[:, u % 2, k, :], start=(k == k0), stop=(k == TT - 1))
                        ins.then_inc(pv_done, 1)

                    def sum_head(h):
                        pe.wait_ge(o_squared, h + 1)
                        if h:
                            pe.wait_ge(o_scaled, h)
                        for b in range(TT):
                            ins = nc.tensor.matmul(pt[:, SUM, b:b + 1], tmp[:, h % 2, b * P:(b + 1) * P],
                                                   ones[:, 0:1], start=True, stop=True)
                        ins.then_inc(o_summed, 1)

                    for s in range(2):
                        pe.wait_ge(evac[s], 2 * s0)
                    pe.wait_ge(roped, 16)
                    def spread_head(h):
                        pe.wait_ge(hrstd_ready, h + 1)
                        for b in range(TT):
                            column = hrstd[:, TT * h + b:TT * h + b + 1]
                            ins = nc.tensor.matmul(pt[:, SUM, b * P:(b + 1) * P], column.broadcast_to([P, P]), ident,
                                                   start=True, stop=True)
                        ins.then_inc(hbcast_ready, 1)

                    for v in range(V_STEPS):
                        if v < V:
                            score(v // 2, v % 2)
                        if 4 <= v < V + 4 and v % 2 == 0:
                            values(v // 2 - 2)
                        if 2 <= v < V + 2:
                            turn_probs(v // 2 - 1, v % 2)
                        for at, step in ((AT_SUM, sum_head), (AT_SPREAD, spread_head)):
                            if at <= v < at + 4 * DH and (v - at) % 4 == 0:
                                step((v - at) // 4)
                elif kind == "ret_attn":
                    def score_r(h):
                        b0 = 2 * (h % 2)
                        if h >= 2:
                            pe.wait_ge(rprobs, h - 1)
                        for k in range(TT):
                            for e in range(2):
                                ins = nc.tensor.matmul(pt[:, b0 + k // 2, (k % 2) * LAT:(k % 2 + 1) * LAT],
                                                       kr[:, 2 * h + e, k * P:(k + 1) * P], qr[:, 2 * h + e, :],
                                                       start=(e == 0), stop=(e == 1))
                        ins.then_inc(rscored, 1)

                    def values_r(h):
                        pe.wait_ge(rprobs, h + 1)
                        if h:
                            pe.wait_ge(rcopied, h)
                        for e in range(4):
                            for k in range(TT):
                                ins = nc.tensor.matmul(pt[:, 4 + e // 2, (e % 2) * LAT:(e % 2 + 1) * LAT],
                                                       vr[:, k, h * RV + e * P:h * RV + (e + 1) * P], aTr[:, h % 2, k, :],
                                                       start=(k == 0), stop=(k == TT - 1))
                        ins.then_inc(rpv, 1)

                    def sum_r(h):
                        pe.wait_ge(rsquared, h + 1)
                        for b in range(2):
                            for e in range(4):
                                at = e * LAT + b * P
                                ins = nc.tensor.matmul(pt[:, SUM, 2 * h + b:2 * h + b + 1],
                                                       tmp[:, at // TOK, at % TOK:at % TOK + P], ones[:, 0:1],
                                                       start=(e == 0), stop=(e == 3))
                        ins.then_inc(rsummed, 1)

                    for s in range(2):
                        pe.wait_ge(evac[s], 2 * s0)
                    pe.wait_ge(roped, 32)
                    score_r(0)
                    for h in range(RH):
                        if h + 1 < RH:
                            score_r(h + 1)
                        values_r(h)
                        if h:
                            sum_r(h - 1)
                    sum_r(RH - 1)
                    for h in range(RH):
                        pe.wait_ge(rdiag, 2 * (h + 1))
                        if h >= 2:
                            pe.wait_ge(rscaled, h - 1)
                        nc.tensor.matmul(pt[:, 6 + h % 2, 0:LAT], ones[:], tmp[:, h % 2, 0:LAT], start=True, stop=True).then_inc(rbcast, 1)
                elif kind == "down":
                    nc_, x0, u0 = len(ph["rows"]), ph["x"], ph["u"]
                    if ph["f"]:
                        hi, lo = (lambda k: uh[:, k, 0:T]), (lambda k: ul[:, k, 0:T])
                    elif ph["L"] == 0:
                        hi, lo = x_tiles(T)
                    else:
                        hi, lo = (lambda k: oh[:, k, :]), (lambda k: ol[:, k, :])
                    ready, upto = (u_ready, u0 - FT) if ph["f"] else (x_ready, x0 - sum(ph["rows"]))
                    with pe.Fori(0, 2) as i:
                        for g in range(2):
                            claim(g, s0 + i)
                            k0 = 0
                            for e, rows_ in enumerate(ph["rows"]):
                                c_ = g * nc_ + e
                                pe.wait_ge(lo_ready, 2 * q0 + 2 * nc_ * i + c_ + 1)
                                last = e == nc_ - 1
                                h_, l_ = (lambda k, k0=k0: hi(k0 + k)), (lambda k, k0=k0: lo(k0 + k))
                                if c_ == 0 and not ph["f"]:
                                    products(c_ % 2, g, rows_, h_, l_, T, e == 0, last,
                                             by_row=(lambda k: pe.wait_ge(ready, upto + k + 1), lambda k: None))
                                else:
                                    if g == 0:
                                        pe.wait_ge(ready, upto + k0 + rows_)
                                    products(c_ % 2, g, rows_, h_, l_, T, e == 0, last)
                                k0 += rows_


_INPUTS = ["x", "c", "ctx", "c_ctx", "mod_w", "mod_b", "ffn1_w13", "ffn1_w2", "ffn2_w13", "ffn2_w2",
           "diff_w_in", "diff_w_out", "diff_lambda", "diff_subln_g", "ret_w_in", "ret_w_out", "ret_decay_exp",
           "final_norm_g"]


def kernel(**inputs):
    import concourse.bacc as bacc
    from concourse.bass_utils import run_bass_kernel_spmd

    nc = bacc.Bacc("TRN2", target_bir_lowering=False, num_devices=1)
    arrays, args = {}, []
    for name in _INPUTS:
        a = np.ascontiguousarray(inputs[name])
        arrays[f"in_{name}"] = a
        args.append(nc.dram_tensor(f"in_{name}", a.shape, mybir.dt.from_np(a.dtype), kind="ExternalInput").ap())
    a = shape_constants()
    arrays["shape_constants"] = a
    args.append(nc.dram_tensor("shape_constants", a.shape, F32, kind="ExternalInput").ap())
    out = nc.dram_tensor("latent_out", (1, LAT, D), F32, kind="ExternalOutput").ap()
    trunk(nc, *args, out)
    r = run_bass_kernel_spmd(nc, [arrays], core_ids=[0])
    return r.results[0]["latent_out"]
```
